# Optimizing a Trainium2 kernel written in Bass

```python
import math
import jax, jax.numpy as jnp
from jax import lax
import numpy as np

D_MODEL = 1024
BATCH = 1
SEQ = 512
DEPTH = 1

CHUNK = 64
Q_BLOCK = 128
N_MEM = 256
MIX_WIDTH = D_MODEL
FOX_WIDTH = MIX_WIDTH // 2
HGRN_WIDTH = MIX_WIDTH - FOX_WIDTH
FOX_HEAD_DIM = 64
FOX_HEADS = FOX_WIDTH // FOX_HEAD_DIM
HGRN_KEY_DIM = 128
HGRN_HEADS = HGRN_WIDTH // HGRN_KEY_DIM
HGRN_VAL_DIM = HGRN_WIDTH // HGRN_HEADS
X_HEADS = 4
X_HEAD_DIM = D_MODEL // X_HEADS
D_FF = 4 * D_MODEL
EPS = 1e-6
SPLITS = (FOX_WIDTH, FOX_WIDTH, FOX_WIDTH, FOX_HEADS, HGRN_WIDTH, HGRN_WIDTH, HGRN_WIDTH, HGRN_WIDTH)
IN_COLS = sum(SPLITS)


def rmsnorm(x, g):
    xf = x.astype(jnp.float32)
    y = xf * lax.rsqrt(jnp.mean(xf * xf, axis=-1, keepdims=True) + EPS)
    return (y * g.astype(jnp.float32)).astype(x.dtype)

def fox_attention(q, k, v, log_f):
    b_, h_, s_, d_ = q.shape
    nb = s_ // Q_BLOCK
    scale = 1.0 / math.sqrt(d_)
    F = jnp.cumsum(log_f, axis=-1)
    qb = q.reshape(b_, h_, nb, Q_BLOCK, d_).transpose(2, 0, 1, 3, 4)
    Fb = F.reshape(b_, h_, nb, Q_BLOCK).transpose(2, 0, 1, 3)
    pos = jnp.arange(s_, dtype=jnp.int32).reshape(nb, Q_BLOCK)
    key_pos = jnp.arange(s_, dtype=jnp.int32)

    def block(args):
        qi, Fi, pi = args
        s = jnp.einsum('bhqd,bhkd->bhqk', qi, k).astype(jnp.float32) * scale
        s = s + Fi[..., None] - F[:, :, None, :]
        mask = pi[:, None] >= key_pos[None, :]
        s = jnp.where(mask, s, -jnp.inf)
        p = jax.nn.softmax(s, axis=-1)
        return jnp.einsum('bhqk,bhkd->bhqd', p.astype(v.dtype), v)

    out = lax.map(block, (qb, Fb, pos))
    return out.transpose(1, 2, 0, 3, 4).reshape(b_, h_, s_, d_)

def hgrn2_chunkwise(q, f_logit, i, lb):
    b_, s_, _ = q.shape
    n_c = s_ // CHUNK

    def heads(t, d):
        return t.astype(jnp.float32).reshape(b_, n_c, CHUNK, HGRN_HEADS, d).transpose(1, 0, 3, 2, 4)

    lbh = lb.astype(jnp.float32).reshape(HGRN_HEADS, 1, HGRN_KEY_DIM)
    f = lbh + (1.0 - lbh) * jax.nn.sigmoid(heads(f_logit, HGRN_KEY_DIM))
    kk = 1.0 - f
    g = jnp.log(f)
    qq = jax.nn.silu(heads(q, HGRN_KEY_DIM))
    ii = heads(i, HGRN_VAL_DIM)
    causal = jnp.tril(jnp.ones((CHUNK, CHUNK), dtype=bool))

    def step(state, inp):
        qc, kc, ic, gc = inp
        bcum = jnp.cumsum(gc, axis=2)
        diff = bcum[:, :, :, None, :] - bcum[:, :, None, :, :]
        decay = jnp.exp(jnp.where(causal[:, :, None], diff, -jnp.inf))
        attn = jnp.einsum('bhtd,bhsd,bhtsd->bhts', qc, kc, decay)
        intra = jnp.einsum('bhts,bhsv->bhtv', attn, ic)
        inter = jnp.einsum('bhtd,bhdv->bhtv', qc * jnp.exp(bcum), state)
        b_last = bcum[:, :, -1]
        k_dec = kc * jnp.exp(b_last[:, :, None, :] - bcum)
        new_state = jnp.exp(b_last)[..., None] * state + jnp.einsum('bhsd,bhsv->bhdv', k_dec, ic)
        return new_state, intra + inter

    s0 = jnp.zeros((b_, HGRN_HEADS, HGRN_KEY_DIM, HGRN_VAL_DIM), jnp.float32)
    _, outs = lax.scan(step, s0, (qq, kk, ii, g))
    return outs.transpose(1, 0, 3, 2, 4).reshape(b_, s_, HGRN_HEADS, HGRN_VAL_DIM)

def memory_cross_attention(h, mem_n, w_q, w_kv, w_o):
    b_, s_, _ = h.shape
    m_ = mem_n.shape[1]
    q = (h @ w_q).reshape(b_, s_, X_HEADS, X_HEAD_DIM)
    kv = mem_n @ w_kv
    k, v = jnp.split(kv, 2, axis=-1)
    k = k.reshape(b_, m_, X_HEADS, X_HEAD_DIM)
    v = v.reshape(b_, m_, X_HEADS, X_HEAD_DIM)
    s = jnp.einsum('bshd,bmhd->bhsm', q, k).astype(jnp.float32) / math.sqrt(X_HEAD_DIM)
    p = jax.nn.softmax(s, axis=-1)
    o = jnp.einsum('bhsm,bmhd->bshd', p.astype(v.dtype), v).reshape(b_, s_, D_MODEL)
    return o @ w_o

def first_inputs(seed: int = 0) -> dict:
    key = jax.random.key(seed)
    ks = jax.random.split(key, 20)
    nrm = lambda k, shape, s: jax.random.normal(k, shape, jnp.float32) * s
    gain = lambda k, shape: 1.0 + 0.02 * jax.random.normal(k, shape, jnp.float32)
    return {
        "x": nrm(ks[0], (BATCH, SEQ, D_MODEL), 1.0),
        "mem": nrm(ks[1], (BATCH, N_MEM, D_MODEL), 1.0),
        "norm_mix_g": gain(ks[2], (DEPTH, D_MODEL)),
        "w_in": nrm(ks[3], (DEPTH, D_MODEL, IN_COLS), D_MODEL ** -0.5),
        "fox_f_bias": 1.0 + 0.1 * jax.random.normal(ks[4], (DEPTH, FOX_HEADS), jnp.float32),
        "hgrn_lb_logits": nrm(ks[5], (DEPTH + 1, HGRN_WIDTH), 0.1),
        "hgrn_norm_g": gain(ks[6], (DEPTH, HGRN_VAL_DIM)),
        "w_out": nrm(ks[7], (DEPTH, MIX_WIDTH, D_MODEL), MIX_WIDTH ** -0.5),
        "norm_x_g": gain(ks[8], (DEPTH, D_MODEL)),
        "norm_mem_g": gain(ks[9], (DEPTH, D_MODEL)),
        "w_xq": nrm(ks[10], (DEPTH, D_MODEL, D_MODEL), D_MODEL ** -0.5),
        "w_xkv": nrm(ks[11], (DEPTH, D_MODEL, 2 * D_MODEL), D_MODEL ** -0.5),
        "w_xo": nrm(ks[12], (DEPTH, D_MODEL, D_MODEL), D_MODEL ** -0.5),
        "norm_ff_g": gain(ks[13], (DEPTH, D_MODEL)),
        "w1": nrm(ks[14], (DEPTH, D_MODEL, D_FF), D_MODEL ** -0.5),
        "w2": nrm(ks[15], (DEPTH, D_FF, D_MODEL), D_FF ** -0.5),
        "final_norm_g": gain(ks[16], (D_MODEL,)),
    }

def first_block(x, mem, norm_mix_g, w_in, fox_f_bias, hgrn_lb_logits, hgrn_norm_g, w_out,
              norm_x_g, norm_mem_g, w_xq, w_xkv, w_xo, norm_ff_g, w1, w2, final_norm_g):
    b_, s_, _ = x.shape
    lbs = jnp.cumsum(jax.nn.softmax(hgrn_lb_logits.astype(jnp.float32), axis=0), axis=0)
    split_idx = list(np.cumsum(SPLITS)[:-1])
    h = x
    for l in range(DEPTH):
        hn = rmsnorm(h, norm_mix_g[l])
        proj = hn @ w_in[l]
        fq, fk, fv, ff, gq, gf, gi, gg = jnp.split(proj, split_idx, axis=-1)
        to_heads = lambda t: t.reshape(b_, s_, FOX_HEADS, FOX_HEAD_DIM).transpose(0, 2, 1, 3)
        log_f = jax.nn.log_sigmoid((ff + fox_f_bias[l]).astype(jnp.float32)).transpose(0, 2, 1)
        fox_out = fox_attention(to_heads(fq), to_heads(fk), to_heads(fv), log_f)
        fox_out = fox_out.transpose(0, 2, 1, 3).reshape(b_, s_, FOX_WIDTH)
        rec = hgrn2_chunkwise(gq, gf, gi, lbs[l])
        rec = rmsnorm(rec, hgrn_norm_g[l]) * jax.nn.silu(
            gg.astype(jnp.float32).reshape(b_, s_, HGRN_HEADS, HGRN_VAL_DIM))
        rec = rec.reshape(b_, s_, HGRN_WIDTH).astype(h.dtype)
        h = h + jnp.concatenate([fox_out, rec], axis=-1) @ w_out[l]
        mem_n = rmsnorm(mem, norm_mem_g[l])
        h = h + memory_cross_attention(rmsnorm(h, norm_x_g[l]), mem_n, w_xq[l], w_xkv[l], w_xo[l])
        u = rmsnorm(h, norm_ff_g[l]) @ w1[l]
        h = h + jnp.square(jax.nn.relu(u)) @ w2[l]
    return rmsnorm(h, final_norm_g)


DEPTH_2 = 2

GRID_W = 64

POOL_WINDOWS = (2, 4, 8, 16)
N_POOL_GROUPS = 4
POOL_GROUP_DIM = D_MODEL // 8
POOL_DIM = N_POOL_GROUPS * POOL_GROUP_DIM

ATT_HEADS = 8
ATT_KV_HEADS = 2
ATT_HEAD_DIM = D_MODEL // 16
ATT_Q_DIM = ATT_HEADS * ATT_HEAD_DIM
ATT_KV_DIM = ATT_KV_HEADS * ATT_HEAD_DIM
ROPE_THETA = 10000.0

EVEN_IN_DIM = POOL_DIM + ATT_Q_DIM + 2 * ATT_KV_DIM
EVEN_MIX_DIM = POOL_DIM + ATT_Q_DIM

MLSTM_HEADS = 8
MLSTM_QK_DIM = D_MODEL // 16
MLSTM_V_DIM = D_MODEL // 8
MLSTM_QK_WIDTH = MLSTM_HEADS * MLSTM_QK_DIM
MLSTM_V_WIDTH = MLSTM_HEADS * MLSTM_V_DIM
N_GATES = 4 * MLSTM_HEADS
ODD_IN_DIM = 2 * MLSTM_QK_WIDTH + 2 * MLSTM_V_WIDTH + N_GATES
CONV_K = 5
CHUNK_2 = 128

FFN_HIDDEN = -(-8 * D_MODEL // (3 * 256)) * 256


def rms_norm(x):
    x32 = x.astype(jnp.float32)
    y = x32 * lax.rsqrt(jnp.mean(x32 * x32, axis=-1, keepdims=True) + EPS)
    return y.astype(x.dtype)

def modulate(h, shift, scale):
    return h * (1.0 + scale[:, None, :]) + shift[:, None, :]

def grid_rope(seq_len):
    rows = seq_len // GRID_W
    row = jnp.repeat(jnp.arange(rows), GRID_W).astype(jnp.float32)
    col = jnp.tile(jnp.arange(GRID_W), rows).astype(jnp.float32)
    n_freq = ATT_HEAD_DIM // 4
    inv_freq = ROPE_THETA ** (-jnp.arange(n_freq, dtype=jnp.float32) / n_freq)
    ang = jnp.concatenate([row[:, None] * inv_freq, col[:, None] * inv_freq], axis=-1)
    return jnp.cos(ang), jnp.sin(ang)

def apply_rope(x, cos, sin):
    x32 = x.astype(jnp.float32)
    x1, x2 = x32[..., 0::2], x32[..., 1::2]
    c, s = cos[None, :, None, :], sin[None, :, None, :]
    out = jnp.stack([x1 * c - x2 * s, x1 * s + x2 * c], axis=-1).reshape(x.shape)
    return out.astype(x.dtype)

def multiscale_pool(u):
    B, S, _ = u.shape
    u32 = u.astype(jnp.float32)
    csum = jnp.concatenate([jnp.zeros((B, 1, POOL_DIM), jnp.float32), jnp.cumsum(u32, axis=1)], axis=1)
    t = jnp.arange(S)
    means = []
    for g, w in enumerate(POOL_WINDOWS):
        lo = jnp.clip(t - w // 2, 0, S)
        hi = jnp.clip(t + w - w // 2, 0, S)
        cg = csum[..., g * POOL_GROUP_DIM:(g + 1) * POOL_GROUP_DIM]
        total = jnp.take(cg, hi, axis=1) - jnp.take(cg, lo, axis=1)
        count = (hi - lo).astype(jnp.float32)
        means.append(total / count[None, :, None])
    return (jnp.concatenate(means, axis=-1) - u32).astype(u.dtype)

def grid_attention(q, k, v, cos, sin, q_gain, k_gain):
    q = apply_rope(rms_norm(q) * q_gain, cos, sin)
    k = apply_rope(rms_norm(k) * k_gain, cos, sin)
    B, S, H, Dh = q.shape
    G = H // ATT_KV_HEADS
    nb = S // Q_BLOCK
    qb = q.reshape(B, nb, Q_BLOCK, ATT_KV_HEADS, G, Dh).transpose(1, 0, 3, 4, 2, 5)
    kt = k.transpose(0, 2, 1, 3)
    vt = v.transpose(0, 2, 1, 3)
    scale = Dh ** -0.5

    def block(q_blk):
        s = jnp.einsum('bkgqd,bksd->bkgqs', q_blk, kt).astype(jnp.float32) * scale
        p = jax.nn.softmax(s, axis=-1).astype(vt.dtype)
        return jnp.einsum('bkgqs,bksd->bkgqd', p, vt)

    o = lax.map(block, qb)
    return o.transpose(1, 0, 4, 2, 3, 5).reshape(B, S, H * Dh)

def pool_attention_mixer(h, w_in, w_pool, b_pool, pool_scale, q_gain, k_gain, w_out, cos, sin):
    B, S, _ = h.shape
    z = h @ w_in
    u = z[..., :POOL_DIM]
    q = z[..., POOL_DIM:POOL_DIM + ATT_Q_DIM]
    k = z[..., POOL_DIM + ATT_Q_DIM:POOL_DIM + ATT_Q_DIM + ATT_KV_DIM]
    v = z[..., POOL_DIM + ATT_Q_DIM + ATT_KV_DIM:]
    pooled = multiscale_pool(u).reshape(B, S, N_POOL_GROUPS, POOL_GROUP_DIM)
    a = (jnp.einsum('bsgc,gcd->bsgd', pooled, w_pool) + b_pool).reshape(B, S, POOL_DIM) * pool_scale
    att = grid_attention(q.reshape(B, S, ATT_HEADS, ATT_HEAD_DIM),
                         k.reshape(B, S, ATT_KV_HEADS, ATT_HEAD_DIM),
                         v.reshape(B, S, ATT_KV_HEADS, ATT_HEAD_DIM),
                         cos, sin, q_gain, k_gain)
    return jnp.concatenate([a, att], axis=-1) @ w_out

def centred_depthwise_conv(u, w, b):
    y = lax.conv_general_dilated(u, w[:, None, :].astype(u.dtype), window_strides=(1,),
                                 padding=[(CONV_K // 2, CONV_K // 2)],
                                 dimension_numbers=('NWC', 'WIO', 'NWC'),
                                 feature_group_count=u.shape[-1])
    return y + b

def mlstm_chunkwise(q, k, v, log_i, log_f):
    q, k, v = (a.astype(jnp.float32) for a in (q, k, v))
    B, H, S, Dk = q.shape
    Dv = v.shape[-1]
    nc = S // CHUNK_2

    def to_chunks(a):
        return jnp.moveaxis(a.reshape(B, H, nc, CHUNK_2, *a.shape[3:]), 2, 0)

    qc, kc, vc, ic, fc = (to_chunks(a) for a in (q, k, v, log_i, log_f))
    lower = jnp.tril(jnp.ones((CHUNK_2, CHUNK_2), bool))

    def step(carry, inp):
        C, n, m = carry
        qj, kj, vj, ij, fj = inp
        b = jnp.cumsum(fj, axis=-1)
        a = b + m[..., None]
        D = jnp.where(lower, b[..., :, None] - b[..., None, :] + ij[..., None, :], -jnp.inf)
        m_t = jnp.maximum(a, jnp.max(D, axis=-1))
        w_inter = jnp.exp(a - m_t)
        s = jnp.einsum('bhtd,bhsd->bhts', qj, kj) * jnp.exp(D - m_t[..., None])
        num = jnp.einsum('bhts,bhsv->bhtv', s, vj) + w_inter[..., None] * jnp.einsum('bhvd,bhtd->bhtv', C, qj)
        den = jnp.sum(s, axis=-1) + w_inter * jnp.einsum('bhd,bhtd->bht', n, qj)
        h = num / jnp.maximum(jnp.abs(den), jnp.exp(-m_t))[..., None]
        bL = b[..., -1]
        g = bL[..., None] - b + ij
        m_new = jnp.maximum(bL + m, jnp.max(g, axis=-1))
        decay = jnp.exp(bL + m - m_new)
        wk = jnp.exp(g - m_new[..., None])
        C = decay[..., None, None] * C + jnp.einsum('bhsv,bhsd->bhvd', vj * wk[..., None], kj)
        n = decay[..., None] * n + jnp.einsum('bhs,bhsd->bhd', wk, kj)
        return (C, n, m_new), h

    init = (jnp.zeros((B, H, Dv, Dk), jnp.float32), jnp.zeros((B, H, Dk), jnp.float32),
            jnp.zeros((B, H), jnp.float32))
    _, hc = lax.scan(step, init, (qc, kc, vc, ic, fc))
    return jnp.moveaxis(hc, 0, 2).reshape(B, H, S, Dv)

def mlstm_mixer(h, w_in, conv_w, conv_b, gate_b, head_gain, w_out):
    B, S, _ = h.shape
    z = h @ w_in
    qk_raw = z[..., :2 * MLSTM_QK_WIDTH]
    v = z[..., 2 * MLSTM_QK_WIDTH:2 * MLSTM_QK_WIDTH + MLSTM_V_WIDTH]
    o = z[..., 2 * MLSTM_QK_WIDTH + MLSTM_V_WIDTH:2 * MLSTM_QK_WIDTH + 2 * MLSTM_V_WIDTH]
    gates = z[..., 2 * MLSTM_QK_WIDTH + 2 * MLSTM_V_WIDTH:]
    qk = jax.nn.silu(centred_depthwise_conv(qk_raw, conv_w, conv_b))
    q = qk[..., :MLSTM_QK_WIDTH].reshape(B, S, MLSTM_HEADS, MLSTM_QK_DIM).transpose(0, 2, 1, 3)
    k = (qk[..., MLSTM_QK_WIDTH:] * MLSTM_QK_DIM ** -0.5).reshape(B, S, MLSTM_HEADS, MLSTM_QK_DIM).transpose(0, 2, 1, 3)
    v = v.reshape(B, S, MLSTM_HEADS, MLSTM_V_DIM).transpose(0, 2, 1, 3)
    g = (gates.astype(jnp.float32) + gate_b.astype(jnp.float32)).reshape(B, S, 2, 2, MLSTM_HEADS)
    g = jnp.transpose(g, (2, 3, 0, 4, 1))
    h_fwd = mlstm_chunkwise(q, k, v, g[0, 0], jax.nn.log_sigmoid(g[0, 1]))
    flip = lambda a: jnp.flip(a, axis=2)
    h_bwd = flip(mlstm_chunkwise(flip(q), flip(k), flip(v), flip(g[1, 0]), flip(jax.nn.log_sigmoid(g[1, 1]))))
    hs = (h_fwd + h_bwd).transpose(0, 2, 1, 3).astype(h.dtype)
    hs = rms_norm(hs) * head_gain
    out = jax.nn.sigmoid(o).reshape(B, S, MLSTM_HEADS, MLSTM_V_DIM) * hs
    return out.reshape(B, S, MLSTM_V_WIDTH) @ w_out

def swiglu(h, w1, w3, w2):
    return (jax.nn.silu(h @ w1) * (h @ w3)) @ w2

def second_inputs(seed: int = 0) -> dict:
    key = jax.random.key(seed)
    ks = jax.random.split(key, 24)
    n_ev = (DEPTH_2 + 1) // 2
    n_od = DEPTH_2 // 2
    f32 = jnp.float32

    def nrm(k, shape, scale):
        return jax.random.normal(k, shape, f32) * scale

    i_bias = nrm(ks[14], (n_od, 2, MLSTM_HEADS), 0.1)
    f_bias = jnp.linspace(3.0, 6.0, MLSTM_HEADS, dtype=f32)[None, None, :] + nrm(ks[15], (n_od, 2, MLSTM_HEADS), 0.1)
    return {
        'x': nrm(ks[0], (BATCH, SEQ, D_MODEL), 1.0),
        'c': nrm(ks[1], (BATCH, D_MODEL), 1.0),
        'ada_w': nrm(ks[2], (DEPTH_2, D_MODEL, 6 * D_MODEL), D_MODEL ** -0.5),
        'ada_b': nrm(ks[3], (DEPTH_2, 6 * D_MODEL), 0.02),
        'ev_w_in': nrm(ks[4], (n_ev, D_MODEL, EVEN_IN_DIM), D_MODEL ** -0.5),
        'ev_w_pool': nrm(ks[5], (n_ev, N_POOL_GROUPS, POOL_GROUP_DIM, POOL_GROUP_DIM), POOL_GROUP_DIM ** -0.5),
        'ev_b_pool': nrm(ks[6], (n_ev, N_POOL_GROUPS, POOL_GROUP_DIM), 0.02),
        'ev_pool_scale': 1.0 + nrm(ks[7], (n_ev, POOL_DIM), 0.1),
        'ev_q_gain': 1.0 + nrm(ks[8], (n_ev, ATT_HEAD_DIM), 0.1),
        'ev_k_gain': 1.0 + nrm(ks[9], (n_ev, ATT_HEAD_DIM), 0.1),
        'ev_w_out': nrm(ks[10], (n_ev, EVEN_MIX_DIM, D_MODEL), EVEN_MIX_DIM ** -0.5),
        'od_w_in': nrm(ks[11], (n_od, D_MODEL, ODD_IN_DIM), D_MODEL ** -0.5),
        'od_conv_w': nrm(ks[12], (n_od, CONV_K, 2 * MLSTM_QK_WIDTH), CONV_K ** -0.5),
        'od_conv_b': nrm(ks[13], (n_od, 2 * MLSTM_QK_WIDTH), 0.02),
        'od_gate_b': jnp.stack([i_bias, f_bias], axis=2).reshape(n_od, N_GATES),
        'od_head_gain': 1.0 + nrm(ks[16], (n_od, MLSTM_HEADS, MLSTM_V_DIM), 0.1),
        'od_w_out': nrm(ks[17], (n_od, MLSTM_V_WIDTH, D_MODEL), MLSTM_V_WIDTH ** -0.5),
        'ffn_w1': nrm(ks[18], (DEPTH_2, D_MODEL, FFN_HIDDEN), D_MODEL ** -0.5),
        'ffn_w3': nrm(ks[19], (DEPTH_2, D_MODEL, FFN_HIDDEN), D_MODEL ** -0.5),
        'ffn_w2': nrm(ks[20], (DEPTH_2, FFN_HIDDEN, D_MODEL), FFN_HIDDEN ** -0.5),
    }

def second_block(x, c, ada_w, ada_b, ev_w_in, ev_w_pool, ev_b_pool, ev_pool_scale, ev_q_gain, ev_k_gain,
              ev_w_out, od_w_in, od_conv_w, od_conv_b, od_gate_b, od_head_gain, od_w_out,
              ffn_w1, ffn_w3, ffn_w2):
    cos, sin = grid_rope(x.shape[1])
    cond = jax.nn.silu(c)
    for layer in range(DEPTH_2):
        mod = cond @ ada_w[layer] + ada_b[layer]
        sh1, sc1, g1, sh2, sc2, g2 = jnp.split(mod, 6, axis=-1)
        h = modulate(rms_norm(x), sh1, sc1)
        j = layer // 2
        if layer % 2 == 0:
            y = pool_attention_mixer(h, ev_w_in[j], ev_w_pool[j], ev_b_pool[j], ev_pool_scale[j],
                                     ev_q_gain[j], ev_k_gain[j], ev_w_out[j], cos, sin)
        else:
            y = mlstm_mixer(h, od_w_in[j], od_conv_w[j], od_conv_b[j], od_gate_b[j],
                            od_head_gain[j], od_w_out[j])
        x = x + g1[:, None, :] * y
        h = modulate(rms_norm(x), sh2, sc2)
        x = x + g2[:, None, :] * swiglu(h, ffn_w1[layer], ffn_w3[layer], ffn_w2[layer])
    return x


def setup_inputs(seed=0):
    out = dict(first_inputs(seed))
    for name, value in second_inputs(seed + 1).items():
        if name != "x":
            out[name + "_2"] = value
    return out


def reference(
    x, mem, norm_mix_g, w_in, fox_f_bias, hgrn_lb_logits, hgrn_norm_g, w_out, norm_x_g,
    norm_mem_g, w_xq, w_xkv, w_xo, norm_ff_g, w1, w2, final_norm_g, c_2, ada_w_2, ada_b_2,
    ev_w_in_2, ev_w_pool_2, ev_b_pool_2, ev_pool_scale_2, ev_q_gain_2, ev_k_gain_2, ev_w_out_2,
    od_w_in_2, od_conv_w_2, od_conv_b_2, od_gate_b_2, od_head_gain_2, od_w_out_2, ffn_w1_2,
    ffn_w3_2, ffn_w2_2,
):
    x = first_block(
        x, mem, norm_mix_g, w_in, fox_f_bias, hgrn_lb_logits, hgrn_norm_g, w_out, norm_x_g,
        norm_mem_g, w_xq, w_xkv, w_xo, norm_ff_g, w1, w2, final_norm_g,
    )
    return second_block(
        x, c_2, ada_w_2, ada_b_2, ev_w_in_2, ev_w_pool_2, ev_b_pool_2, ev_pool_scale_2,
        ev_q_gain_2, ev_k_gain_2, ev_w_out_2, od_w_in_2, od_conv_w_2, od_conv_b_2, od_gate_b_2,
        od_head_gain_2, od_w_out_2, ffn_w1_2, ffn_w3_2, ffn_w2_2,
    )


_drawn_inputs = setup_inputs


def setup_inputs(seed=0):
    import zlib

    import numpy as np

    out = dict(_drawn_inputs(seed))
    spreads = {}
    factors = {'norm_mix_g': 3.332,
     'hgrn_lb_logits': 8.0,
     'hgrn_norm_g': 6.187,
     'norm_x_g': 8.0,
     'norm_mem_g': 8.0,
     'norm_ff_g': 2.985,
     'ev_b_pool_2': 6.106,
     'ev_q_gain_2': 8.0,
     'ev_k_gain_2': 8.0,
     'od_conv_b_2': 25.502}
    for name, (base, spread) in spreads.items():
        noise = np.random.default_rng([zlib.crc32(name.encode()), seed]).standard_normal(out[name].shape)
        drawn = base * np.exp(spread * noise) if base else spread * noise
        out[name] = __import__('jax').numpy.asarray(drawn.astype(out[name].dtype))
    for name, factor in factors.items():
        out[name] = (out[name] * factor).astype(out[name].dtype)
    return out
```

```python
from contextlib import ExitStack

import numpy as np

import concourse.bass as bass
from concourse import mybir

F32 = mybir.dt.float32
F32R = mybir.dt.float32r
BF16 = mybir.dt.bfloat16
U32 = mybir.dt.uint32
ALU = mybir.AluOpType
ACT = mybir.ActivationFunctionType
AX = mybir.AxisListType.X

P = 128
D = 1024
S = 512
KC = D // P
TB = S // P
M_MEM = 256
EPS = 1e-6
UC = 256
FF1 = 4096
FF2 = 2816
FOX_H, FOX_D = 8, 64
HG_H = 4
HG_LEVELS = (1, 2, 4, 8, 16, 32, 64)
X_H = 4
GA_H = 8
ML_H, ML_V = 8, 128
WINDOWS = (2, 4, 8, 16)
CONV_K = 5
NEG = -1.0e30

C_IDENT, C_ONES, C_HALF, C_ROT, C_DUP0, C_DUP1, C_GSEL, C_CAUSAL = range(8)
N_CONST = 8

V_MIX, V_X, V_MEM, V_FF, V_FINAL, V_LB, V_HG, V_C, V_BPOOL, V_SPOOL, V_CW, V_CB, V_QG, V_KG = (
    0, 8, 16, 24, 32, 40, 48, 49, 57, 61, 65, 105, 113, 114)
V_ROWS = 115


def plan():
    units = []

    def add(w, k0, kc, c0, cols, blocks=2):
        units.append((w, k0, kc, c0, cols, blocks))

    at = {}

    def stage(name):
        at[name] = (len(units), sum(u[5] for u in units))

    stage("in")
    for c0 in (0, 256, 512, 768, 1024, 1280):
        add("w_in", 0, KC, c0, UC)
    add("w_in", 0, KC, 1536, P, 1)
    for c0 in range(1544, 3592, UC):
        add("w_in", 0, KC, c0, UC)
    stage("out")
    for c0 in range(0, D, UC):
        add("w_out", 0, KC, c0, UC)
    stage("xkv")
    for c0 in range(0, 2 * D, UC):
        add("w_xkv", 0, KC, c0, UC)
    stage("xq")
    for c0 in range(0, D, UC):
        add("w_xq", 0, KC, c0, UC)
    stage("xo")
    for c0 in range(0, D, UC):
        add("w_xo", 0, KC, c0, UC)
    stage("ff1")
    for g in range(FF1 // D):
        for c0 in range(g * D, (g + 1) * D, UC):
            add("w1", 0, KC, c0, UC)
        for c0 in range(0, D, UC):
            add("w2", g * KC, KC, c0, UC)
    stage("ev_in")
    for c0 in range(0, 1280, UC):
        add("ev_w_in_2", 0, KC, c0, UC)
    stage("ev_out")
    for c0 in range(0, D, UC):
        add("ev_w_out_2", 0, KC, c0, UC)
    for layer in range(2):
        if layer == 1:
            stage("od_in")
            for c0 in range(0, 3072, UC):
                add("od_w_in_2", 0, KC, c0, UC)
            add("od_w_in_2", 0, KC, 3104 - P, P, 1)
            stage("od_out")
            for c0 in range(0, D, UC):
                add("od_w_out_2", 0, KC, c0, UC)
        stage(f"ff2_{layer}")
        for g0 in range(0, FF2, D):
            for c0 in range(g0, min(g0 + D, FF2), UC):
                add(f"ffn_w1_2.{layer}", 0, KC, c0, UC)
                add(f"ffn_w3_2.{layer}", 0, KC, c0, UC)
            for c0 in range(0, D, UC):
                add(f"ffn_w2_2.{layer}", g0 // P, min(g0 + D, FF2) // P - g0 // P, c0, UC)
    stage("end")
    return units, at


UNITS, AT = plan()
N_UNITS = len(UNITS)
BLOCK0 = [sum(u[5] for u in UNITS[:n]) for n in range(N_UNITS + 1)]
BY_ACT = [u[0].startswith("ffn_w1") for u in UNITS for _ in range(u[5])]
TAKEN = [sum(not x for x in BY_ACT[:b]) for b in range(len(BY_ACT) + 1)]
SILUS = [sum(x for x in BY_ACT[:b]) for b in range(len(BY_ACT) + 1)]

Q0 = {}
_q = 0
for _name, _count in (("mix_norm", 8), ("mix", 8), ("mem", 8), ("x_norm", 8), ("x_att", 8), ("ff1_norm", 8),
                      ("ff1_u", 32), ("ev_norm", 8), ("ev_mix", 8), ("ff2_0_norm", 8), ("ff2_0_u", 22),
                      ("od_norm", 8), ("od_mix", 8), ("ff2_1_norm", 8), ("ff2_1_u", 22)):
    Q0[_name] = _q
    _q += _count

ATT = {
    "fox": dict(heads=FOX_H, step0=0, pv0=0, pvh=1, q0=Q0["mix"], col0=0),
    "cross": dict(heads=X_H, step0=32, pv0=8, pvh=2, q0=Q0["x_att"], col0=0),
    "grid": dict(heads=GA_H, step0=48, pv0=16, pvh=1, q0=Q0["ev_mix"], col0=4),
}
NORMS = {n: i for i, n in enumerate(("mix", "x", "ff1", "final", "ev", "ff2_0", "od", "ff2_1"))}


GA_SCALE = 64 ** -0.5
LB_SHIFTED = 3
POOL_STEPS = sum(g + 2 for g in range(len(WINDOWS)))


def ranges(name):
    starts = sorted(v[0] for v in AT.values())
    n = AT[name][0]
    return n, starts[starts.index(n) + 1]


def add(i, count):
    return count if i is None else i + count


def outputs(kind, t):
    h = t // TB
    if t % TB != TB - 1 or not 0 <= h < ATT[kind]["heads"]:
        return []
    return [2 * h, 2 * h + 1] if kind == "cross" else [h // 2] if h % 2 else []


def bass_block_pair(nc, a, out):
    BASE = 16512
    top = [0]

    def place(name, shape, dt, offset=None):
        size = int(np.prod(shape[1:])) * (2 if dt == BF16 else 4)
        if offset is None:
            offset = top[0]
            top[0] += -(-size // 32) * 32
        return nc.alloc_sbuf_tensor_at(name, shape, dt, offset=BASE + offset), offset

    raw = [place(f"raw{i}", [P, KC, UC], F32)[0] for i in range(2)]
    wH = [place(f"wH{i}", [P, KC, UC], F32R)[0] for i in range(2)]
    wL = [place(f"wL{i}", [P, KC, UC], F32R)[0] for i in range(2)]
    xT = place("xT", [P, KC, S], F32)[0]
    hnH, HN = place("hnH", [P, KC, S], F32R)
    hnL = place("hnL", [P, KC, S], F32R)[0]
    uH = place("uH", [P, KC, S], F32R)[0]
    uL = place("uL", [P, KC, S], F32R)[0]
    cst = place("cst", [P, N_CONST, P], F32)[0]
    identb = place("identb", [P, P], BF16)[0]
    causalb = place("causalb", [P, P], BF16)[0]
    cols = place("cols", [P, P], F32)[0]
    adab = place("adab", [P, 96], F32)[0]
    mod = place("mod", [P, 96], F32)[0]
    modp = place("modp", [P, 96], F32)[0]
    small = place("small", [P, 160], F32)[0]
    T, TOFF = [], []
    for i in range(2):
        t, o = place(f"T{i}", [P, S], F32)
        T.append(t)
        TOFF.append(o)
    R, ROFF = [], []
    for i in range(2):
        t, o = place(f"R{i}", [P, S], F32)
        R.append(t)
        ROFF.append(o)
    sq, SQOFF = [], []
    for i in range(2):
        t, o = place(f"sq{i}", [P, S], F32)
        sq.append(t)
        SQOFF.append(o)
    ssum, SSOFF = place("ssum", [P, S], F32)
    rs, RSOFF = place("rs", [P, S], F32)
    AR = top[0]
    assert BASE + AR + 57600 <= 229344, AR

    ident = cst[:, C_IDENT, :]
    ones = cst[:, C_ONES, :]

    eps = small[:, 0:1]
    nmax = small[:, 4:8]
    rsum = small[:, 8:12]
    rinv = small[:, 12:16]
    lb = small[:, 16:20]
    omlb = small[:, 20:24]
    lbt = small[:, 24:40]
    condc = small[:, 40:48]
    fbias = small[:, 48:49]
    gbias = small[:, 49:50]
    mstat = small[:, 56:64]
    mden = small[:, 64:72]
    hstat = small[:, 72:104]
    hrs = small[:, 104:136]
    nmraw = small[:, 136:140]

    xtok = place("xtok", [P, TB, D], F32, AR)[0]
    vrow = place("vrow", [P, P], F32, AR + 16384)[0]
    brow = place("brow", [P, P], F32, AR + 16896)[0]
    fq = place("fq", [P, 4, S], F32, AR)[0]
    fk = place("fk", [P, 4, S], F32, AR + 8192)[0]
    fv = place("fv", [P, TB, 512], F32, AR + 16384)[0]
    gq = place("gq", [P, HG_H, S], F32, AR + 24576)[0]
    gk = place("gk", [P, HG_H, S], F32, AR + 32768)[0]
    gi = place("gi", [P, TB, 512], F32, AR + 40960)[0]
    gg = place("gg", [P, HG_H, S], F32, AR + 49152)[0]
    pr = [place(f"pr{i}", [P, S], F32, HN + 2048 * i)[0] for i in range(3)]
    pT = [place(f"pT{i}", [P, TB, S], F32, HN + 6144 + 8192 * i)[0] for i in range(2)]
    fbc = [place(f"fbc{i}", [P, S], F32, HN + 22528 + 2048 * i)[0] for i in range(2)]
    fz = place("fz", [FOX_H, S], F32, TOFF[0])[0]
    frow = [place(f"frow{i}", [FOX_H, S], F32, HN + 26624 + 2048 * i)[0] for i in range(3)]
    gb = place("gb", [P, HG_H, S], F32, AR)[0]
    lvl = place("lvl", [P, 8, P], F32, AR + 8192)[0]
    ho = place("ho", [P, HG_H, S], F32, AR + 12288)[0]
    hrsb = [place(f"hrsb{i}", [P, S], F32, AR + 20480 + 2048 * i)[0] for i in range(2)]
    dd = [place(f"dd{i}", [P, S], F32, HN + 2048 * i)[0] for i in range(2)]
    qt = [place(f"qt{i}", [P, S], F32, HN + 4096 + 2048 * i)[0] for i in range(2)]
    kt = [place(f"kt{i}", [P, S], F32, HN + 8192 + 2048 * i)[0] for i in range(2)]
    at_ = [place(f"at{i}", [P, TB, P], F32, HN + 12288 + 2048 * i)[0] for i in range(2)]
    qb = place("qb", [P, S], F32, HN + 16384)[0]
    kd = place("kd", [P, S], F32, HN + 18432)[0]
    eb = place("eb", [P, S], F32, HN + 20480)[0]
    ed = place("ed", [P, S], F32, HN + 22528)[0]
    kdT = place("kdT", [P, 3, P], F32, HN + 24576)[0]
    st = place("st", [P, 3, P], F32, HN + 26112)[0]
    rmask = place("rmask", [P, S], F32, HN + 27648)[0]
    memH = place("memH", [P, KC, M_MEM], F32R, AR)[0]
    memL = place("memL", [P, KC, M_MEM], F32R, AR + 8192)[0]
    mtok = place("mtok", [P, 2, D], F32, AR + 49152)[0]
    xk = place("xk", [P, KC, M_MEM], F32, AR + 16384)[0]
    xv = place("xv", [P, 2, D], F32, AR + 24576)[0]
    xq = place("xq", [P, KC, S], F32, AR + 32768)[0]
    mdump = place("mdump", [P, D], F32, HN)[0]
    mT = [place(f"mT{i}", [P, M_MEM], F32, ROFF[i])[0] for i in range(2)]
    adaw = [place(f"adaw{i}", [P, KC, UC], F32, AR + 8192 * i)[0] for i in range(2)]
    adacc = [place(f"adacc{i}", [P, UC], F32, AR + 16384 + 1024 * i)[0] for i in range(2)]
    pu = place("pu", [P, 4, S + 24], F32, AR)[0]
    evq = place("evq", [P, 5, S], F32, AR + 8704)[0]
    evv = place("evv", [P, TB, P], F32, AR + 18944)[0]
    kdup = place("kdup", [P, 2, S], F32, AR + 20992)[0]
    cosb = place("cosb", [P, S], F32, AR + 25088)[0]
    sinb = place("sinb", [P, S], F32, AR + 27136)[0]
    icnt = place("icnt", [P, 4, S], F32, AR + 29184)[0]
    gs = place("gs", [P, 5, S], F32, HN)[0]
    wpool = place("wpool", [P, 4, P], F32, AR + 37376)[0]
    pw = [place(f"pw{i}", [P, S + 24], F32, AR + 39424 + 2176 * i)[0] for i in range(2)]
    pd = place("pd", [P, 4, S], F32, AR + 43776)[0]
    cz = place("cz", [P, KC, S + 4], F32, AR)[0]
    hs = place("hs", [P, TB, D], F32, AR)[0]
    vx = place("vx", [P, TB, ML_H, ML_V + 1], F32, AR + 16512)[0]
    mo = place("mo", [P, TB, D], F32, AR + 33024)[0]
    hgain = place("hgain", [P, D], F32, AR + 49408)[0]
    wt = [place(f"wt{i}", [P, S], F32, AR + 53504 + 2048 * i)[0] for i in range(2)]
    cy = place("cy", [P, KC, S], F32, HN)[0]
    ma = [place(f"ma{i}", [P, TB, S], F32, HN + 16384 + 8192 * i)[0] for i in range(2)]
    hsq = place("hsq", [P, TB, D], F32, HN)[0]
    grow = place("grow", [P, S], F32, TOFF[0])[0]
    irow = place("irow", [64, S], F32, TOFF[1])[0]
    lrow = place("lrow", [64, S], F32, ROFF[0])[0]
    Frow = place("Frow", [64, S], F32, ROFF[1])[0]
    Mrow = place("Mrow", [64, S], F32, SQOFF[0])[0]
    erow = place("erow", [64, S], F32, SQOFF[1])[0]
    ccol = place("ccol", [P, TB, 64], F32, SSOFF)[0]
    ecol = place("ecol", [P, TB, 64], F32, RSOFF)[0]
    otok = place("otok", [P, TB, D], F32, AR)[0]

    with ExitStack() as ctx:
        ps = [ctx.enter_context(nc.psum_tensor(f"ps{i}", [P, S], F32)) for i in range(8)]

        def sem(name):
            return ctx.enter_context(nc.semaphore(name))

        raw_in = [sem(f"raw_in{i}") for i in range(2)]
        w_hi, w_lo = sem("w_hi"), sem("w_lo")
        blk_done = sem("blk_done")
        blk_taken = sem("blk_taken")
        op_t, op_hi, op_lo = sem("op_t"), sem("op_hi"), sem("op_lo")
        sq_done, sq_added, sum_done, rs_done, ln_done = (
            sem("sq_done"), sem("sq_added"), sem("sum_done"), sem("rs_done"), sem("ln_done"))
        cst_in, x_in, vec_in, vec_tr, vec_cols = sem("cst_in"), sem("x_in"), sem("vec_in"), sem("vec_tr"), sem("vec_cols")
        x_tr, x_cols = sem("x_tr"), sem("x_cols")
        setup, setup_d = sem("setup"), sem("setup_d")
        dstep = sem("dstep")
        astep = sem("astep")
        gstep = sem("gstep")
        sc_done, mx_done, ex_done, pn_done, tp_done, pt_done, pv_done = (
            sem("sc_done"), sem("mx_done"), sem("ex_done"), sem("pn_done"), sem("tp_done"), sem("pt_done"), sem("pv_done"))
        f_z, f_e, f_l, f_rows, f_bc, f_bcs = sem("f_z"), sem("f_e"), sem("f_l"), sem("f_rows"), sem("f_bc"), sem("f_bcs")
        lvl_in = sem("lvl_in")
        h_act, h_fk, h_ln, h_b = sem("h_act"), sem("h_fk"), sem("h_ln"), sem("h_b")
        h_d, h_e, h_q, h_k, h_pl, h_at = sem("h_d"), sem("h_e"), sem("h_q"), sem("h_k"), sem("h_pl"), sem("h_at")
        h_eb, h_qb, h_kd, h_kt, h_kts, h_sp, h_st, h_o, h_os = (
            sem("h_eb"), sem("h_qb"), sem("h_kd"), sem("h_kt"), sem("h_kts"), sem("h_sp"), sem("h_st"), sem("h_o"), sem("h_os"))
        h_sq, h_sum, h_rs, h_t = sem("h_sq"), sem("h_sum"), sem("h_rs"), sem("h_t")
        mem_in, m_sq, m_rs, m_n, m_tr, m_t = sem("mem_in"), sem("m_sq"), sem("m_rs"), sem("m_n"), sem("m_tr"), sem("m_t")
        ada_in = [sem(f"ada_in{i}") for i in range(2)]
        ada_step = sem("ada_step")
        ada_acc, ada_mm, mod_done = sem("ada_acc"), sem("ada_mm"), sem("mod_done")
        relu_done, silu_done = sem("relu_done"), sem("silu_done")
        x_fin = sem("x_fin")
        ev_in, g_sq, g_sum, g_rs, g_n, g_rot, g_roped, g_dup, g_kd = (
            sem("ev_c_in"), sem("g_sq"), sem("g_sum"), sem("g_rs"), sem("g_n"), sem("g_rot"), sem("g_roped"), sem("g_dup"), sem("g_kd"))
        p_done, p_mm = sem("p_done"), sem("p_mm")
        gain_in, c_pad, c_y, c_silu, o_sig = sem("gain_in"), sem("c_pad"), sem("c_y"), sem("c_silu"), sem("o_sig")
        r_g, r_sel, r_i, r_abs, r_ln, r_rows, r_em, r_tr, r_cols = (
            sem("r_g"), sem("r_sel"), sem("r_i"), sem("r_abs"), sem("r_ln"), sem("r_rows"), sem("r_em"), sem("r_tr"), sem("r_cols"))
        l_bc, l_qk, l_w, l_a, l_wm, l_o, l_h = sem("l_bc"), sem("l_qk"), sem("l_w"), sem("l_a"), sem("l_wm"), sem("l_o"), sem("l_h")
        n_sq, n_sum, n_rs, n_h, n_tr = sem("n_sq"), sem("n_sum"), sem("n_rs"), sem("n_h"), sem("n_tr")
        o_tr, o_cp, o_out = sem("o_tr"), sem("o_cp"), sem("o_out")

        block = ctx.enter_context(nc.Block())

        def weight_view(name):
            if "." in name:
                name, layer = name.split(".")
                w = a[name][int(layer)]
            else:
                w = a[name][0]
            return w.rearrange("(k p) n -> p k n", p=P)

        @block.sync
        def _(sp):
            def load(n, value=None, src=None):
                w, k0, kc, c0, c, _ = UNITS[n]
                if n >= 2:
                    sp.wait_ge(w_lo, (n if value is None else value) - 1)
                if src is None:
                    src = weight_view(w)[:, k0:k0 + kc, c0:c0 + c]
                sp.dma_start(raw[n % 2][:, 0:kc, 0:c], src).then_inc(raw_in[n % 2], 16)

            def loads(first, last):
                for n in range(first, last):
                    load(n)

            sp.dma_start(cst[:], a["const"].rearrange("c p m -> p c m")).then_inc(cst_in, 16)
            rows = [("norm_mix_g", V_MIX, 8), ("norm_x_g", V_X, 8), ("norm_mem_g", V_MEM, 8), ("norm_ff_g", V_FF, 8),
                    ("final_norm_g", V_FINAL, 8), ("hgrn_lb_logits", V_LB, 8), ("hgrn_norm_g", V_HG, 1), ("c_2", V_C, 8),
                    ("ev_b_pool_2", V_BPOOL, 4), ("ev_pool_scale_2", V_SPOOL, 4), ("od_conv_w_2", V_CW, 40),
                    ("od_conv_b_2", V_CB, 8)]
            for tb in range(TB):
                sp.dma_start(xtok[:, tb, :], a["x"][0, tb * P:(tb + 1) * P, :]).then_inc(x_in, 16)
            for name, r0, count in rows:
                src = a[name]
                nd = len(src.shape)
                flat = {1: "a -> a", 2: "a b -> (a b)", 3: "a b c -> (a b c)"}[nd]
                src = src if nd == 1 else src.rearrange(flat)
                sp.dma_start(vrow[r0:r0 + count, :], src.rearrange("(r m) -> r m", m=P)).then_inc(vec_in, 16)
            for name, r0 in (("ev_q_gain_2", V_QG), ("ev_k_gain_2", V_KG)):
                for half in range(2):
                    sp.dma_start(vrow[r0:r0 + 1, half * 64:half * 64 + 64], a[name][0:1, :]).then_inc(vec_in, 16)
            sp.dma_start(brow[0:96, :], a["ada_b_2"].rearrange("l (r m) -> (l r) m", m=P)).then_inc(vec_in, 16)
            sp.dma_start(fbias[0:8, :], a["fox_f_bias"].rearrange("a b -> b a")).then_inc(vec_in, 16)
            sp.dma_start(gbias[96:128, :], a["od_gate_b_2"].rearrange("a b -> b a")).then_inc(vec_in, 16)
            loads(0, AT["out"][0] + 1)
            sp.wait_ge(op_lo, Q0["mix"] + 4)
            sp.dma_start(lvl[:], a["levels"].rearrange("l s t -> s l t")).then_inc(lvl_in, 16)
            sp.wait_ge(op_lo, Q0["mix"] + 8)
            for mb in range(2):
                sp.dma_start(mtok[:, mb, :], a["mem"][0, mb * P:(mb + 1) * P, :]).then_inc(mem_in, 16)
            loads(AT["out"][0] + 1, AT["ff1"][0])

            n0 = AT["ff1"][0]
            w1v, w2v = weight_view("w1"), weight_view("w2")
            sp.wait_ge(op_lo, Q0["x_att"] + 8)
            for layer in range(2):
                adav = a["ada_w_2"][layer].rearrange("(k p) n -> p k n", p=P)
                with sp.Fori(0, 2) as half:
                    i = half + 2 * layer
                    m = 0
                    for u in range(8):
                        if u < 4:
                            load(n0 + u, i * 8 + (n0 + u), w1v[:, :, bass.ds(i * D + u * UC, UC)])
                        else:
                            load(n0 + u, i * 8 + (n0 + u), w2v[:, bass.ds(i * KC, KC), (u - 4) * UC:(u - 3) * UC])
                        for _ in range(2 - u % 2):
                            sp.wait_ge(ada_acc, i * 12 + (m + 1))
                            sp.dma_start(adaw[m % 2][:], adav[:, :, bass.ds(half * 3072 + m * UC, UC)]).then_inc(ada_in[m % 2], 16)
                            m += 1
            loads(AT["ev_in"][0], AT["ev_out"][0])
            sp.wait_ge(mod_done, 6)
            sp.dma_start(cosb[:], a["rope"][0]).then_inc(ev_in, 16)
            sp.dma_start(sinb[:], a["rope"][1]).then_inc(ev_in, 16)
            sp.dma_start(wpool[:], a["ev_w_pool_2"][0].rearrange("g c d -> c g d")).then_inc(ev_in, 16)
            sp.dma_start(icnt[:], a["icount"].rearrange("(o g) t -> o g t", o=1).to_broadcast([P, 4, S])).then_inc(ev_in, 16)
            loads(AT["ev_out"][0], AT["ff2_0"][0])

            def gated_ffn(layer):
                n0 = AT[f"ff2_{layer}"][0]
                w1v, w3v, w2v = (weight_view(f"ffn_w{j}_2.{layer}") for j in (1, 3, 2))
                with sp.Fori(0, 2) as i:
                    for u in range(12):
                        if u < 8:
                            src = (w1v, w3v)[u % 2][:, :, bass.ds(i * D + (u // 2) * UC, UC)]
                        else:
                            src = w2v[:, bass.ds(i * KC, KC), (u - 8) * UC:(u - 7) * UC]
                        load(n0 + u, i * 12 + (n0 + u), src)
                loads(n0 + 24, n0 + 34)

            gated_ffn(0)
            loads(AT["od_in"][0], AT["od_in"][0] + 2)
            sp.wait_ge(op_lo, Q0["od_norm"] + 8)
            sp.dma_start(hgain[:], a["od_head_gain_2"].rearrange("o h v -> o (h v)").to_broadcast([P, D])).then_inc(gain_in, 16)
            loads(AT["od_in"][0] + 2, AT["ff2_1"][0])
            gated_ffn(1)
            for tb in range(TB):
                sp.wait_ge(o_cp, 2 * tb + 2)
                sp.dma_start(out[0, tb * P:(tb + 1) * P, :], otok[:, tb, :]).then_inc(o_out, 16)
            sp.wait_ge(o_out, 16 * TB)

        @block.gpsimd
        def _(pool):
            def low(n, value=None):
                _, _, kc, _, c, _ = UNITS[n]
                pool.wait_ge(w_hi, (n if value is None else value) + 1)
                nc.gpsimd.tensor_tensor(wL[n % 2][:, 0:kc, 0:c], raw[n % 2][:, 0:kc, 0:c],
                                        wH[n % 2][:, 0:kc, 0:c].bitcast(F32), ALU.subtract).then_inc(w_lo, 1)

            def lows(first, last):
                for n in range(first, last):
                    low(n)

            lows(0, AT["out"][0] + 1)
            v = 0
            for h in range(HG_H):
                for l in range(len(HG_LEVELS)):
                    pool.wait_ge(h_e, v + 1)
                    if v >= 2:
                        pool.wait_ge(h_pl, 8 * ((v - 2) // 7) + (v - 2) % 7 + 1)
                    nc.gpsimd.tensor_tensor(kt[v % 2][:], gk[:, h, :], dd[v % 2][:], ALU.mult).then_inc(h_k, 1)
                    v += 1
                pool.wait_ge(h_eb, 2 * h + 2)
                if h:
                    pool.wait_ge(h_kt, h)
                nc.gpsimd.tensor_tensor(kd[:], gk[:, h, :], ed[:], ALU.mult).then_inc(h_kd, 1)
            lows(AT["out"][0] + 1, AT["ff1"][0])
            n0 = AT["ff1"][0]
            with pool.Fori(0, 4) as i:
                for u in range(8):
                    low(n0 + u, i * 8 + (n0 + u))
            lows(AT["ev_in"][0], AT["ev_out"][0] + 1)
            pool.wait_ge(ev_in, 64)
            pool.wait_ge(blk_taken, TAKEN[BLOCK0[AT["ev_in"][0]] + 4])
            g = 0
            for grp, w in enumerate(WINDOWS):
                src, half = pu[:, grp, :], 1
                for lev in range(grp + 1):
                    n_out = S + 16 - 2 * half + 1
                    if g:
                        pool.wait_ge(gstep, g)
                    dst = pw[lev % 2]
                    nc.gpsimd.tensor_tensor(dst[:, 0:n_out], src[:, 0:n_out], src[:, half:half + n_out], ALU.add).then_inc(gstep, 1)
                    g += 1
                    src, half = dst[:], 2 * half
                off = 8 - w // 2
                pool.wait_ge(gstep, g)
                nc.gpsimd.tensor_tensor(pd[:, grp, :], src[:, off:off + S], icnt[:, grp, :], ALU.mult).then_inc(gstep, 1)
                g += 1
                pool.wait_ge(gstep, g)
                nc.gpsimd.tensor_tensor(pd[:, grp, :], pd[:, grp, :], pu[:, grp, 8:8 + S], ALU.subtract).then_inc(p_done, 1)

            def gated_ffn(layer):
                n0 = AT[f"ff2_{layer}"][0]
                with pool.Fori(0, 2) as i:
                    for u in range(12):
                        low(n0 + u, i * 12 + (n0 + u))
                lows(n0 + 24, n0 + 34)

            lows(AT["ev_out"][0] + 1, AT["ff2_0"][0])
            gated_ffn(0)
            lows(AT["od_in"][0], AT["od_out"][0] + 1)
            pool.wait_ge(gain_in, 16)
            pool.wait_ge(o_sig, 1)
            for tb in range(TB):
                nc.gpsimd.tensor_tensor(mo[:, tb, :], mo[:, tb, :], hgain[:], ALU.mult).then_inc(gstep, 1)
            for h in range(ML_H):
                for d in range(2):
                    for j in range(TB):
                        r = 8 * h + 4 * d + j
                        pool.wait_ge(l_w, r + 1)
                        diag = wt[r % 2][:, j * P:(j + 1) * P]
                        sign = 1 if d == 0 else -1
                        nc.gpsimd.affine_select(out=diag, in_=diag, compare_op=ALU.is_ge, fill=0.0, base=0,
                                                pattern=[[sign, P]], channel_multiplier=-sign).then_inc(l_wm, 1)
            lows(AT["od_out"][0] + 1, AT["ff2_1"][0])
            gated_ffn(1)

        @block.scalar
        def _(act):
            acts = [0]

            def chain(ins):
                acts[0] += 1
                ins.then_inc(astep, 1)
                act.wait_ge(astep, acts[0])

            def high(n, i=None, du=0, db=0):
                if n >= N_UNITS:
                    return
                _, _, kc, _, c, _ = UNITS[n]
                act.wait_ge(raw_in[n % 2], add(None if i is None else i * (8 * du), 16 * (n // 2 + 1)))
                if n >= 2:
                    act.wait_ge(blk_done, add(None if i is None else i * db, BLOCK0[n - 1]))
                nc.scalar.activation(wH[n % 2][:, 0:kc, 0:c], raw[n % 2][:, 0:kc, 0:c], ACT.Copy).then_inc(w_hi, 1)

            def norm_sums(name, ready):
                i = NORMS[name]
                for j in range(KC):
                    act.wait_ge(*ready(j))
                    if 8 * i + j >= 2:
                        act.wait_ge(sq_added, 8 * i + j - 1)
                    nc.scalar.activation(sq[j % 2][:], xT[:, j, :], ACT.Square).then_inc(sq_done, 1)
                act.wait_ge(sum_done, i + 1)
                if i:
                    act.wait_ge(ln_done, i)
                chain(nc.scalar.activation(rs[:], ps[4][:], ACT.Ln, bias=eps, scale=1.0 / D))
                nc.scalar.activation(rs[:], rs[:], ACT.Exp, scale=-0.5).then_inc(rs_done, 1)

            def high_op(q, dstH, src, wait, bias=None):
                act.wait_ge(*wait)
                if bias is None:
                    nc.scalar.activation(dstH, src, ACT.Copy).then_inc(op_hi, 1)
                else:
                    nc.scalar.activation(dstH, src, ACT.Identity, bias=bias).then_inc(op_hi, 1)

            tq = [0]

            def norm_highs(q0, shift=None):
                for j in range(KC):
                    tq[0] += 1
                    high_op(q0 + j, hnH[:, j, :], T[(q0 + j) % 2][:], (op_t, tq[0]), None if shift is None else shift(j))

            def attention(kind):
                c = ATT[kind]
                ns = c["heads"] * TB
                width = {"fox": None, "cross": M_MEM, "grid": S}[kind]
                for s in range(ns + 6):
                    g = c["step0"] + s
                    if kind == "fox":
                        h = 0 if s == 0 else (s + 2) // 4 if s % 4 == 2 else FOX_H
                        if h < FOX_H:
                            act.wait_ge(f_bc, h + 1)
                            if h >= 2:
                                act.wait_ge(mx_done, 4 * (h - 1))
                            nc.scalar.activation(fbc[h % 2][:], ps[2 + h % 2][:], ACT.Copy).then_inc(f_bcs, 1)
                    if s < ns:
                        i = s % TB
                        w = (i + 1) * P if kind == "fox" else width
                        act.wait_ge(mx_done, g + 1)
                        if kind == "fox":
                            src = pr[g % 3][:, 0:w]
                        else:
                            src = ps[4 + g % 2][:, 0:w]
                            act.wait_ge(tp_done, g - 2)
                        nc.scalar.activation(pr[g % 3][:, 0:w], src, ACT.Exp, bias=nmax[:, g % 3:g % 3 + 1],
                                             accum_out=rsum[:, g % 3:g % 3 + 1]).then_inc(ex_done, 1)
                    if kind == "fox" and s == 8:
                        act.wait_ge(blk_taken, TAKEN[BLOCK0[AT["out"][0]]])
                        nc.scalar.activation(gq[:], gq[:], ACT.Silu).then_inc(h_act, 1)
                        nc.scalar.activation(gg[:], gg[:], ACT.Silu).then_inc(h_act, 1)
                        nc.scalar.activation(gk[:], gk[:], ACT.Sigmoid).then_inc(h_act, 1)
                    t = s - 2
                    if 0 <= t < ns:
                        h, i = t // TB, t % TB
                        nj = (i + 1) if kind == "fox" else width // P
                        act.wait_ge(tp_done, c["step0"] + t + 1)
                        if i == 0 and h >= 2:
                            act.wait_ge(pv_done, c["pv0"] + c["pvh"] * (h - 1))
                        nc.scalar.activation(pT[h % 2][:, 0:nj, i * P:(i + 1) * P],
                                             ps[6 + (c["step0"] + t) % 2][:, 0:nj * P].rearrange("p (j t) -> p j t", j=nj),
                                             ACT.Copy).then_inc(pt_done, 1)
                    if s >= 7 and (s - 7) % TB == 0 or s == ns + 5:
                        pass
                    for o in outputs(kind, s - 4):
                        act.wait_ge(pv_done, c["pv0"] + (o + 1 if kind == "cross" else 2 * o + 2))
                        nc.scalar.activation(uH[:, c["col0"] + o, :], ps[o % 2][:], ACT.Copy).then_inc(op_hi, 1)

            act.wait_ge(vec_cols, 2)
            nc.scalar.activation(condc, cols[:, V_C:V_C + 8], ACT.Silu).then_inc(setup, 1)
            act.wait_ge(dstep, LB_SHIFTED)
            nc.scalar.activation(lbt[:, 8:16], lbt[:, 0:8], ACT.Exp).then_inc(setup, 1)
            high(0)

            norm_sums("mix", lambda j: (x_cols, j + 1))
            norm_highs(Q0["mix_norm"])
            for n in range(*ranges("in")):
                high(n + 1)
            b = BLOCK0[AT["in"][0]] + 12
            act.wait_ge(f_z, 1)
            chain(nc.scalar.activation(frow[1][:], frow[0][:], ACT.Abs))
            chain(nc.scalar.activation(frow[1][:], frow[1][:], ACT.Exp, scale=-1.0))
            nc.scalar.activation(frow[1][:], frow[1][:], ACT.Ln, bias=ones[0:FOX_H, 0:1]).then_inc(f_l, 1)
            attention("fox")
            for h in range(HG_H):
                act.wait_ge(h_fk, h + 1)
                nc.scalar.activation(ho[:, h, :], ho[:, h, :], ACT.Ln).then_inc(h_ln, 1)
            v = 0
            for h in range(HG_H):
                for l in range(len(HG_LEVELS)):
                    act.wait_ge(h_d, v + 1)
                    chain(nc.scalar.activation(dd[v % 2][:], dd[v % 2][:], ACT.Abs))
                    nc.scalar.activation(dd[v % 2][:], dd[v % 2][:], ACT.Exp, scale=-1.0).then_inc(h_e, 1)
                    v += 1
                if h:
                    act.wait_ge(h_qb, h)
                    act.wait_ge(h_st, 3 * h)
                act.wait_ge(h_b, h + 1)
                nc.scalar.activation(eb[:], gb[:, h, :], ACT.Exp).then_inc(h_eb, 1)
                act.wait_ge(h_t, h + 1)
                nc.scalar.activation(ed[:], ed[:], ACT.Exp).then_inc(h_eb, 1)
                act.wait_ge(h_kt, h + 1)
                if h:
                    act.wait_ge(h_sp, h)
                nc.scalar.activation(kdT[:], ps[6][:, 0:384].rearrange("p (c d) -> p c d", c=3), ACT.Copy).then_inc(h_kts, 1)
            hr = [dd[0], dd[1], kt[0], kt[1]]
            act.wait_ge(h_pl, 8 * HG_H)
            act.wait_ge(h_q, 7 * HG_H)
            for h in range(HG_H):
                act.wait_ge(h_os, h + 1)
                nc.scalar.activation(hr[h][:], ho[:, h, :], ACT.Square).then_inc(h_sq, 1)
            for h in range(HG_H):
                act.wait_ge(h_sum, h + 1)
                chain(nc.scalar.activation(hr[h][:], ps[4 + h][:], ACT.Ln, bias=eps, scale=1.0 / P))
            for h in range(HG_H):
                nc.scalar.activation(hr[h][:], hr[h][:], ACT.Exp, scale=-0.5).then_inc(h_rs, 1)
            for h in range(HG_H):
                tq[0] += 1
                high_op(Q0["mix"] + 4 + h, uH[:, 4 + h, :], T[h % 2][:], (op_t, tq[0]))
            for n in range(*ranges("out")):
                high(n + 1)
            act.wait_ge(mem_in, 32)
            act.wait_ge(blk_done, BLOCK0[AT["xkv"][0]])
            for mb in range(2):
                chain(nc.scalar.activation(mdump[:], mtok[:, mb, :], ACT.Square, accum_out=mstat[:, mb:mb + 1]))
            chain(nc.scalar.activation(mstat[:, 2:4], mstat[:, 0:2], ACT.Ln, bias=eps, scale=1.0 / D))
            nc.scalar.activation(mstat[:, 4:6], mstat[:, 2:4], ACT.Exp, scale=-0.5).then_inc(m_rs, 1)
            for j in range(KC):
                high_op(Q0["mem"] + j, memH[:, j, :], mT[j % 2][:], (m_t, j + 1))
            b = BLOCK0[AT["out"][0]]
            norm_sums("x", lambda j: (blk_taken, TAKEN[b + j + 1]))
            for n in range(*ranges("xkv")):
                high(n + 1)
            norm_highs(Q0["x_norm"])
            for n in range(*ranges("xq")):
                high(n + 1)
            attention("cross")
            for n in range(*ranges("xo")):
                high(n + 1)
            b = BLOCK0[AT["xo"][0]]
            norm_sums("ff1", lambda j: (blk_taken, TAKEN[b + j + 1]))
            norm_highs(Q0["ff1_norm"])
            n0, b0, q0 = AT["ff1"][0], AT["ff1"][1], Q0["ff1_u"]
            t0 = TAKEN[b0]
            with act.Fori(0, 4) as i:
                for u in range(8):
                    high(n0 + u + 1, i, 8, 16)
                    if u < 4:
                        for c in range(2):
                            act.wait_ge(blk_done, i * 16 + (b0 + 2 * u + c + 1))
                            act.wait_ge(blk_taken, i * 16 + (t0 + 2 * u + c - 1))
                            nc.scalar.activation(R[c][:], ps[(b0 + 2 * u + c) % 4][:], ACT.Relu).then_inc(relu_done, 1)
                        for c in range(2):
                            act.wait_ge(blk_taken, i * 16 + (t0 + 2 * u + c + 1))
                            nc.scalar.activation(uH[:, 2 * u + c, :], T[(q0 + c) % 2][:], ACT.Copy).then_inc(op_hi, 1)
            norm_sums("final", lambda j: (blk_taken, TAKEN[AT["ff1"][1] + 64 - 8 + j + 1]))
            norm_sums("ev", lambda j: (x_fin, j + 1))
            norm_highs(Q0["ev_norm"], lambda j: mod[:, j:j + 1])
            for n in range(*ranges("ev_in")):
                high(n + 1)
            b = TAKEN[BLOCK0[AT["ev_in"][0]]]
            act.wait_ge(blk_done, BLOCK0[AT["ev_out"][0]])
            for j in range(5):
                act.wait_ge(blk_taken, b + 4 + j + 1)
                nc.scalar.activation(gs[:, j, :], evq[:, j, :], ACT.Square).then_inc(g_sq, 1)
            for j in range(5):
                act.wait_ge(g_sum, j + 1)
                chain(nc.scalar.activation(gs[:, j, :], ps[j][:], ACT.Ln, bias=eps, scale=1.0 / 64))
            for j in range(5):
                nc.scalar.activation(gs[:, j, :], gs[:, j, :], ACT.Exp, scale=-0.5).then_inc(g_rs, 1)
            for j in range(2):
                act.wait_ge(g_dup, j + 1)
                nc.scalar.activation(kdup[:, j, :], ps[6 + j][:], ACT.Copy).then_inc(g_kd, 1)
            attention("grid")
            for j in range(4):
                tq[0] += 1
                high_op(Q0["ev_mix"] + 4 + j, uH[:, j, :], T[j % 2][:], (op_t, tq[0]))
            for n in range(*ranges("ev_out")):
                high(n + 1)

            def gated_ffn(layer):
                name = f"ff2_{layer}"
                n0, b0 = AT[name]
                q0 = Q0[name + "_u"]
                t0, s0 = TAKEN[b0], SILUS[b0]

                def pair(p, i=None):
                    last = 0 if i is not None else 1
                    n, b = n0 + 24 * last + 2 * p, b0 + 48 * last + 4 * p
                    taken = None if i is None else i * 16
                    high(n + 1, i, 12, 24)
                    for c in range(2):
                        act.wait_ge(blk_done, add(None if i is None else i * 24, b + c + 1))
                        act.wait_ge(blk_taken, add(taken, TAKEN[b] - 1 + c))
                        nc.scalar.activation(R[c][:], ps[(b + c) % 4][:], ACT.Silu).then_inc(silu_done, 1)
                    high(n + 2, i, 12, 24)
                    for c in range(2):
                        act.wait_ge(blk_taken, add(taken, TAKEN[b + 2 + c + 1]))
                        nc.scalar.activation(uH[:, 2 * p + c, :], T[(q0 + c) % 2][:], ACT.Copy).then_inc(op_hi, 1)

                with act.Fori(0, 2) as i:
                    for p in range(4):
                        pair(p, i)
                    for u in range(8, 12):
                        high(n0 + u + 1, i, 12, 24)
                for p in range(3):
                    pair(p)
                for n in range(n0 + 30, n0 + 34):
                    high(n + 1)

            def gated_norm(name, b, part, layer):
                norm_sums(name, lambda j: (blk_taken, TAKEN[b + j + 1]))
                norm_highs(Q0[name + "_norm"], lambda j: mod[:, layer * 48 + part * 8 + j:layer * 48 + part * 8 + j + 1])

            gated_norm("ff2_0", BLOCK0[AT["ev_out"][0]], 3, 0)
            gated_ffn(0)
            gated_norm("od", BLOCK0[AT["od_in"][0]] - 8, 0, 1)
            for n in range(*ranges("od_in")):
                high(n + 1)
            act.wait_ge(blk_taken, TAKEN[BLOCK0[AT["od_out"][0]]])
            nc.scalar.activation(mo[:], mo[:], ACT.Sigmoid).then_inc(o_sig, 1)
            act.wait_ge(r_sel, 1)
            chain(nc.scalar.activation(Frow[:], ps[5][0:64, :], ACT.Abs))
            chain(nc.scalar.activation(Frow[:], Frow[:], ACT.Exp, scale=-1.0))
            nc.scalar.activation(Frow[:], Frow[:], ACT.Ln, bias=ones[0:64, 0:1]).then_inc(r_ln, 1)
            for j in range(KC):
                act.wait_ge(c_y, j + 1)
                nc.scalar.activation(cy[:, j, :], cy[:, j, :], ACT.Silu).then_inc(c_silu, 1)
            act.wait_ge(r_rows, 1)
            nc.scalar.activation(erow[:], erow[:], ACT.Exp, scale=-1.0).then_inc(r_em, 1)
            act.wait_ge(r_tr, 2)
            nc.scalar.activation(ccol[:], ps[6][:, 0:256].rearrange("p (a b) -> p a b", a=TB), ACT.Copy).then_inc(r_cols, 1)
            nc.scalar.activation(ecol[:], ps[7][:, 0:256].rearrange("p (a b) -> p a b", a=TB), ACT.Copy).then_inc(r_cols, 1)
            act.wait_ge(r_cols, 2)
            for h in range(ML_H):
                for d in range(2):
                    for j in range(TB):
                        r = 8 * h + 4 * d + j
                        lo, hi = (j * P, S) if d == 0 else (0, (j + 1) * P)
                        act.wait_ge(l_bc, 2 * h + d + 1)
                        if r >= 2:
                            act.wait_ge(l_a, r - 1)
                        row = h + 32 * d
                        nc.scalar.activation(wt[r % 2][:, lo:hi], ps[4 + d][:, lo:hi], ACT.Exp,
                                             bias=ccol[:, j, row:row + 1]).then_inc(l_w, 1)
            act.wait_ge(l_h, 16)
            nc.scalar.activation(hsq[:], hs[:], ACT.Square).then_inc(n_sq, 1)
            act.wait_ge(n_sum, 1)
            chain(nc.scalar.activation(hrs, hstat, ACT.Ln, bias=eps, scale=1.0 / ML_V))
            nc.scalar.activation(hrs, hrs, ACT.Exp, scale=-0.5).then_inc(n_rs, 1)
            for j in range(KC):
                high_op(Q0["od_mix"] + j, uH[:, j, :], ps[4 + j % 4][:], (n_tr, j + 1))
            for n in range(*ranges("od_out")):
                high(n + 1)
            gated_norm("ff2_1", BLOCK0[AT["od_out"][0]], 3, 1)
            gated_ffn(1)

        @block.vector
        def _(dve):
            steps = [0]

            def chain(ins):
                steps[0] += 1
                ins.then_inc(dstep, 1)
                dve.wait_ge(dstep, steps[0])

            def norm_adds(name):
                i = NORMS[name]
                if i:
                    dve.wait_ge(sum_done, i)
                for j in range(KC):
                    dve.wait_ge(sq_done, 8 * i + j + 1)
                    if j == 0:
                        nc.vector.tensor_copy(ssum[:], sq[0][:]).then_inc(sq_added, 1)
                    else:
                        dve.wait_ge(sq_added, 8 * i + j)
                        nc.vector.tensor_tensor(ssum[:], ssum[:], sq[j % 2][:], ALU.add).then_inc(sq_added, 1)

            def low_op(q, dstL, src, dstH, bias=None):
                dve.wait_ge(op_hi, q + 1)
                if bias is None:
                    nc.vector.tensor_tensor(dstL, src, dstH.bitcast(F32), ALU.subtract).then_inc(op_lo, 1)
                else:
                    nc.vector.scalar_tensor_tensor(out=dstL, in0=src, scalar=bias, in1=dstH.bitcast(F32),
                                                   op0=ALU.add, op1=ALU.subtract).then_inc(op_lo, 1)

            def normed(name, gain, q0, shift=None):
                dve.wait_ge(rs_done, NORMS[name] + 1)

                def low(j):
                    low_op(q0 + j, hnL[:, j, :], T[(q0 + j) % 2][:], hnH[:, j, :], None if shift is None else shift(j))

                for j in range(KC):
                    if q0 + j >= 2:
                        dve.wait_ge(op_lo, q0 + j - 1)
                    ins = nc.vector.scalar_tensor_tensor(out=T[(q0 + j) % 2][:], in0=xT[:, j, :], scalar=gain(j), in1=rs[:],
                                                         op0=ALU.mult, op1=ALU.mult)
                    ins.then_inc(op_t, 1)
                    if j:
                        low(j - 1)
                low(KC - 1)
                nc.vector.tensor_copy(small[:, 144:145], rs[:, 0:1]).then_inc(ln_done, 1)

            def col(c0):
                return lambda j: cols[:, c0 + j:c0 + j + 1]

            def take(b, out_ap, in_ap, scale=None):
                dve.wait_ge(blk_done, b + 1)
                if scale is None:
                    nc.vector.tensor_copy(out_ap, in_ap).then_inc(blk_taken, 1)
                else:
                    nc.vector.tensor_scalar(out_ap, in_ap, scale, None, ALU.mult).then_inc(blk_taken, 1)

            def residual(b, j, gate=None, value=None):
                dve.wait_ge(blk_done, (b if value is None else value) + 1)
                if gate is None:
                    nc.vector.tensor_tensor(xT[:, j, :], ps[b % 4][:], xT[:, j, :], ALU.add).then_inc(blk_taken, 1)
                else:
                    nc.vector.scalar_tensor_tensor(out=xT[:, j, :], in0=ps[b % 4][:], scalar=gate(j), in1=xT[:, j, :],
                                                   op0=ALU.mult, op1=ALU.add).then_inc(blk_taken, 1)

            def attention(kind):
                c = ATT[kind]
                ns = c["heads"] * TB
                width = {"fox": None, "cross": M_MEM, "grid": S}[kind]
                for s in range(ns + 7):
                    g = c["step0"] + s
                    if s < ns:
                        h, i = s // TB, s % TB
                        m = g % 3
                        dve.wait_ge(sc_done, g + 1)
                        if kind == "fox":
                            w = (i + 1) * P
                            if g >= 3:
                                dve.wait_ge(tp_done, g - 2)
                            dve.wait_ge(f_bcs, h + 1)
                            chain(nc.vector.tensor_tensor_reduce(pr[m][:, 0:w], ps[4 + g % 2][:, 0:w], fbc[h % 2][:, 0:w], 1.0, -3.0e38,
                                                                 ALU.subtract, ALU.max, nmraw[:, m:m + 1]))
                        else:
                            chain(nc.vector.tensor_reduce(nmraw[:, m:m + 1], ps[4 + g % 2][:, 0:width], AX, ALU.max))
                        nc.vector.tensor_scalar(nmax[:, m:m + 1], nmraw[:, m:m + 1], -1.0, None, ALU.mult).then_inc(mx_done, 1)
                    if 1 <= s <= ns:
                        m = (g - 1) % 3
                        w = ((s - 1) % TB + 1) * P if kind == "fox" else width
                        dve.wait_ge(ex_done, g)
                        chain(nc.vector.reciprocal(rinv[:, m:m + 1], rsum[:, m:m + 1]))
                        nc.vector.tensor_scalar(pr[m][:, 0:w], pr[m][:, 0:w], rinv[:, m:m + 1], None, ALU.mult).then_inc(pn_done, 1)
                    for o in outputs(kind, s - 5):
                        low_op(c["q0"] + o, uL[:, c["col0"] + o, :], ps[o % 2][:], uH[:, c["col0"] + o, :])

            nc.vector.memset(eps, EPS).then_inc(setup_d, 1)
            dve.wait_ge(cst_in, 16)
            nc.vector.tensor_copy(identb[:], ident).then_inc(setup_d, 1)
            nc.vector.tensor_copy(causalb[:], cst[:, C_CAUSAL, :]).then_inc(setup_d, 1)
            dve.wait_ge(vec_tr, 2)
            nc.vector.tensor_copy(cols[:, 0:V_ROWS], ps[5][:, 0:V_ROWS]).then_inc(vec_cols, 1)
            nc.vector.tensor_copy(adab[:], ps[5][:, 128:224]).then_inc(vec_cols, 1)
            dve.wait_ge(vec_cols, 2)
            dve.sem_inc(ada_acc, 2)
            dve.sem_inc(mod_done, 1)
            l0, l1 = cols[:, V_LB:V_LB + 4], cols[:, V_LB + 4:V_LB + 8]
            chain(nc.vector.tensor_tensor(lbt[:, 8:12], l0, l1, ALU.max))
            chain(nc.vector.tensor_tensor(lbt[:, 0:4], l0, lbt[:, 8:12], ALU.subtract))
            chain(nc.vector.tensor_tensor(lbt[:, 4:8], l1, lbt[:, 8:12], ALU.subtract))
            assert steps[0] == LB_SHIFTED
            dve.wait_ge(setup, 2)
            chain(nc.vector.tensor_tensor(lbt[:, 0:4], lbt[:, 8:12], lbt[:, 12:16], ALU.add))
            chain(nc.vector.reciprocal(lbt[:, 4:8], lbt[:, 0:4]))
            chain(nc.vector.tensor_tensor(lb, lbt[:, 8:12], lbt[:, 4:8], ALU.mult))
            chain(nc.vector.tensor_scalar(omlb, lb, -1.0, 1.0, ALU.mult, ALU.add))
            chain(nc.vector.tensor_scalar(small[:, 148:149], cols[:, V_QG:V_QG + 1], GA_SCALE, None, ALU.mult))
            for j in range(KC):
                dve.wait_ge(x_tr, j + 1)
                nc.vector.tensor_copy(xT[:, j, :], ps[6 + j % 2][:]).then_inc(x_cols, 1)
            norm_adds("mix")
            normed("mix", col(V_MIX), Q0["mix_norm"])

            n, b = AT["in"]
            for j in range(4):
                take(b + j, fq[:, j, :], ps[(b + j) % 4][:], FOX_D ** -0.5)
            for j in range(4):
                take(b + 4 + j, fk[:, j, :], ps[(b + 4 + j) % 4][:])

            def take_tokens(b, dst, c0, width=UC):
                for half in range(2):
                    take(b + half, dst[:, 2 * half:2 * half + 2, c0:c0 + width],
                         ps[(b + half) % 4][:, 0:2 * width].rearrange("p (a c) -> p a c", a=2))

            for u in range(2):
                take_tokens(b + 8 + 2 * u, fv, u * UC)
            fb = b + 12
            dve.wait_ge(blk_done, fb + 1)
            nc.vector.tensor_scalar(fz[:], ps[fb % 4][0:FOX_H, :], fbias[0:FOX_H, :], None, ALU.add).then_inc(blk_taken, 1)
            for j in range(4):
                take(fb + 1 + j, gq[:, j, :], ps[(fb + 1 + j) % 4][:])
            for j in range(4):
                take(fb + 5 + j, gk[:, j, :], ps[(fb + 5 + j) % 4][:])
            for u in range(2):
                take_tokens(fb + 9 + 2 * u, gi, u * UC)
            for j in range(4):
                take(fb + 13 + j, gg[:, j, :], ps[(fb + 13 + j) % 4][:])
            dve.wait_ge(blk_taken, TAKEN[fb + 1])
            nc.vector.tensor_copy(frow[0][:], fz[:]).then_inc(f_z, 1)
            dve.wait_ge(f_z, 1)
            dve.wait_ge(f_l, 1)
            chain(nc.vector.tensor_scalar(frow[2][:], frow[0][:], 0.0, None, ALU.min))
            chain(nc.vector.tensor_tensor(frow[2][:], frow[2][:], frow[1][:], ALU.subtract))
            nc.vector.tensor_tensor_scan(frow[0][:], ones[0:FOX_H, 0:1].to_broadcast([FOX_H, S]), frow[2][:], 0.0,
                                         ALU.mult, ALU.add).then_inc(f_rows, 1)
            attention("fox")
            nc.vector.memset(rmask[:], 1.0).then_inc(dstep, 1)
            steps[0] += 1
            dve.wait_ge(dstep, steps[0])
            chain(nc.vector.memset(rmask[:].rearrange("p (c t) -> p c t", c=TB)[:, :, 0:1], 0.0))
            for i in range(2):
                chain(nc.vector.memset(at_[i][:], 0.0))
            dve.wait_ge(h_act, 3)
            for h in range(HG_H):
                chain(nc.vector.tensor_scalar(ho[:, h, :], gk[:, h, :], omlb[:, h:h + 1], lb[:, h:h + 1], ALU.mult, ALU.add))
                nc.vector.tensor_scalar(gk[:, h, :], ho[:, h, :], -1.0, 1.0, ALU.mult, ALU.add).then_inc(h_fk, 1)
            for h in range(HG_H):
                dve.wait_ge(h_ln, h + 1)
                nc.vector.tensor_tensor_scan(gb[:, h, :], rmask[:], ho[:, h, :], 0.0, ALU.mult, ALU.add).then_inc(h_b, 1)
            levels = [(h, l) for h in range(HG_H) for l in range(len(HG_LEVELS))]

            def level_exponent(v):
                h, l = levels[v]
                L = HG_LEVELS[l]
                if v >= 2:
                    dve.wait_ge(h_q, v - 1)
                    dve.wait_ge(h_k, v - 1)
                dve.wait_ge(h_b, h + 1)
                x = gb[:, h, :].rearrange("p (n t) -> p n t", t=2 * L)
                nc.vector.tensor_tensor(dd[v % 2][:].rearrange("p (n t) -> p n t", t=2 * L), x,
                                        x[:, :, L - 1:L].to_broadcast([P, S // (2 * L), 2 * L]), ALU.subtract).then_inc(h_d, 1)

            def level_q(v):
                h, l = levels[v]
                dve.wait_ge(h_e, v + 1)
                if v >= 2:
                    dve.wait_ge(h_pl, 8 * levels[v - 2][0] + levels[v - 2][1] + 1)
                nc.vector.tensor_tensor(qt[v % 2][:], gq[:, h, :], dd[v % 2][:], ALU.mult).then_inc(h_q, 1)

            def level_scores(e):
                h, l = e // 8, e % 8
                dve.wait_ge(h_pl, e + 1)
                if e:
                    dve.wait_ge(h_at, e)
                if l == 0 and h >= 2:
                    dve.wait_ge(h_o, h - 1)
                nc.vector.copy_predicated(at_[h % 2][:],
                                          lvl[:, l, :].bitcast(U32).rearrange("p (a c) -> p a c", a=1).to_broadcast([P, TB, P]),
                                          ps[4 + e % 2][:].rearrange("p (c t) -> p c t", c=TB)).then_inc(h_at, 1)

            dve.wait_ge(lvl_in, 16)
            level_exponent(0)
            v = 0
            for h in range(HG_H):
                for l in range(len(HG_LEVELS)):
                    if v + 1 < len(levels):
                        level_exponent(v + 1)
                    level_q(v)
                    if l:
                        level_scores(8 * h + l - 1)
                    v += 1
                if h:
                    dve.wait_ge(h_kd, h)
                x = gb[:, h, :].rearrange("p (c t) -> p c t", c=TB)
                nc.vector.tensor_tensor(ed[:].rearrange("p (c t) -> p c t", c=TB), x[:, :, P - 1:P].to_broadcast([P, TB, P]), x,
                                        ALU.subtract).then_inc(h_t, 1)
                level_scores(8 * h + 6)
                level_scores(8 * h + 7)
                if h:
                    dve.wait_ge(h_o, h)
                dve.wait_ge(h_eb, 2 * h + 1)
                nc.vector.tensor_tensor(qb[:], gq[:, h, :], eb[:], ALU.mult).then_inc(h_qb, 1)
                dve.wait_ge(h_sp, h + 1)
                for c in range(3):
                    part = ps[7][:, c * P:(c + 1) * P]
                    if c == 0:
                        nc.vector.tensor_copy(st[:, 0, :], part).then_inc(h_st, 1)
                    else:
                        dve.wait_ge(h_st, 3 * h + c)
                        nc.vector.scalar_tensor_tensor(out=st[:, c, :], in0=st[:, c - 1, :], scalar=eb[:, c * P + P - 1:c * P + P],
                                                       in1=part, op0=ALU.mult, op1=ALU.add).then_inc(h_st, 1)
                dve.wait_ge(h_o, h + 1)
                nc.vector.tensor_copy(ho[:, h, :], ps[h % 2][:]).then_inc(h_os, 1)
            hr = [dd[0], dd[1], kt[0], kt[1]]
            for h in range(HG_H):
                dve.wait_ge(h_rs, h + 1)
                chain(nc.vector.scalar_tensor_tensor(out=ho[:, h, :], in0=ho[:, h, :], scalar=cols[:, V_HG:V_HG + 1], in1=hr[h][:],
                                                     op0=ALU.mult, op1=ALU.mult))
                nc.vector.tensor_tensor(T[h % 2][:], ho[:, h, :], gg[:, h, :], ALU.mult).then_inc(op_t, 1)
                low_op(Q0["mix"] + 4 + h, uL[:, 4 + h, :], T[h % 2][:], uH[:, 4 + h, :])
            n, b = AT["out"]
            for j in range(KC):
                residual(b + j, j)
            dve.wait_ge(m_rs, 1)
            for mb in range(2):
                nc.vector.tensor_scalar(mtok[:, mb, :], mtok[:, mb, :], mstat[:, 4 + mb:5 + mb], None, ALU.mult).then_inc(m_n, 1)
            for j in range(KC):
                dve.wait_ge(m_tr, j + 1)
                if j >= 2:
                    dve.wait_ge(op_lo, Q0["mem"] + j - 1)
                nc.vector.tensor_scalar(mT[j % 2][:], ps[6 + j % 2][:, 0:M_MEM], cols[:, V_MEM + j:V_MEM + j + 1], None,
                                        ALU.mult).then_inc(m_t, 1)
                low_op(Q0["mem"] + j, memL[:, j, :], mT[j % 2][:], memH[:, j, :])
            norm_adds("x")
            n, b = AT["xkv"]
            for j in range(KC):
                take(b + j, xk[:, j, :], ps[(b + j) % 4][:, 0:M_MEM])
            for u in range(4):
                for mb in range(2):
                    bb = b + 8 + 2 * u + mb
                    take(bb, xv[:, mb, u * UC:(u + 1) * UC], ps[bb % 4][:, 0:UC])
            normed("x", col(V_X), Q0["x_norm"])
            n, b = AT["xq"]
            for j in range(KC):
                take(b + j, xq[:, j, :], ps[(b + j) % 4][:], 1.0 / 16)
            attention("cross")
            n, b = AT["xo"]
            for j in range(KC):
                residual(b + j, j)
            norm_adds("ff1")
            normed("ff1", col(V_FF), Q0["ff1_norm"])
            n0, b0 = AT["ff1"]
            q0 = Q0["ff1_u"]
            dve.wait_ge(setup, 1)
            for layer in range(2):
                with dve.Fori(0, 2) as half:
                    i = half + 2 * layer
                    m = 0
                    for u in range(8):
                        for c in range(2):
                            b = b0 + 2 * u + c
                            if u < 4:
                                q = q0 + 2 * u + c
                                dve.wait_ge(relu_done, i * 8 + (2 * u + c + 1))
                                dve.wait_ge(op_lo, i * 8 + (q - 1))
                                nc.vector.scalar_tensor_tensor(out=T[q % 2][:], in0=ps[b % 4][:], scalar=0.0, in1=R[c][:],
                                                               op0=ALU.max, op1=ALU.mult).then_inc(blk_taken, 1)
                            else:
                                residual(b, 2 * (u - 4) + c, None, i * 16 + b)
                        if u < 4:
                            for c in range(2):
                                q = q0 + 2 * u + c
                                dve.wait_ge(op_hi, i * 8 + (q + 1))
                                nc.vector.tensor_tensor(uL[:, 2 * u + c, :], T[q % 2][:], uH[:, 2 * u + c, :].bitcast(F32),
                                                        ALU.subtract).then_inc(op_lo, 1)
                        for _ in range(2 - u % 2):
                            acc = adacc[m % 2][:]
                            dve.wait_ge(ada_in[m % 2], i * 96 + 16 * (m // 2 + 1))
                            dve.wait_ge(ada_mm, i * 12 + (m + 1))
                            for k in range(KC):
                                if k == 0:
                                    ins = nc.vector.tensor_scalar(acc, adaw[m % 2][:, 0, :], condc[:, 0:1], None, ALU.mult)
                                else:
                                    dve.wait_ge(ada_step, i * 84 + (7 * m + k))
                                    ins = nc.vector.scalar_tensor_tensor(out=acc, in0=adaw[m % 2][:, k, :], scalar=condc[:, k:k + 1],
                                                                         in1=acc, op0=ALU.mult, op1=ALU.add)
                                ins.then_inc(ada_acc if k == KC - 1 else ada_step, 1)
                            m += 1
                    dve.wait_ge(ada_mm, i * 12 + 14)
                    nc.vector.tensor_tensor(mod[:, bass.ds(i * 24, 24)], ps[5][:, 0:24], adab[:, bass.ds(i * 24, 24)],
                                            ALU.add).then_inc(mod_done, 1)
            dve.wait_ge(mod_done, 5)
            nc.vector.tensor_scalar(modp[:], mod[:], 1.0, None, ALU.add).then_inc(mod_done, 1)
            dve.wait_ge(mod_done, 6)

            def mcol(t, layer, part):
                return lambda j: t[:, layer * 48 + part * 8 + j:layer * 48 + part * 8 + j + 1]

            norm_adds("final")
            dve.wait_ge(rs_done, NORMS["final"] + 1)
            for j in range(KC):
                nc.vector.scalar_tensor_tensor(out=xT[:, j, :], in0=xT[:, j, :], scalar=cols[:, V_FINAL + j:V_FINAL + j + 1],
                                               in1=rs[:], op0=ALU.mult, op1=ALU.mult).then_inc(x_fin, 1)
            nc.vector.tensor_copy(small[:, 144:145], rs[:, 0:1]).then_inc(ln_done, 1)
            norm_adds("ev")
            normed("ev", mcol(modp, 0, 1), Q0["ev_norm"], mcol(mod, 0, 0))
            chain(nc.vector.memset(pu[:, :, 0:8], 0.0))
            chain(nc.vector.memset(pu[:, :, 8 + S:S + 24], 0.0))
            n, b = AT["ev_in"]
            for j in range(4):
                take(b + j, pu[:, j, 8:8 + S], ps[(b + j) % 4][:])
            for j in range(5):
                take(b + 4 + j, evq[:, j, :], ps[(b + 4 + j) % 4][:])
            take(b + 9, evv[:], ps[(b + 9) % 4][:].rearrange("p (a c) -> p a c", a=TB))
            dve.wait_ge(ev_in, 64)
            for j in range(5):
                dve.wait_ge(g_rs, j + 1)
                gain = small[:, 148:149] if j < 4 else cols[:, V_KG:V_KG + 1]
                nc.vector.scalar_tensor_tensor(out=evq[:, j, :], in0=evq[:, j, :], scalar=gain, in1=gs[:, j, :],
                                               op0=ALU.mult, op1=ALU.mult).then_inc(g_n, 1)
            for j in range(5):
                dve.wait_ge(g_rot, j + 1)
                chain(nc.vector.tensor_tensor(T[j % 2][:], ps[4 + j % 2][:], sinb[:], ALU.mult))
                chain(nc.vector.tensor_tensor(evq[:, j, :], evq[:, j, :], cosb[:], ALU.mult))
                nc.vector.tensor_tensor(evq[:, j, :], evq[:, j, :], T[j % 2][:], ALU.add).then_inc(g_roped, 1)
            attention("grid")
            for j in range(4):
                dve.wait_ge(p_mm, j + 1)
                nc.vector.tensor_scalar(T[j % 2][:], ps[2 + j % 2][:], cols[:, V_BPOOL + j:V_BPOOL + j + 1],
                                        cols[:, V_SPOOL + j:V_SPOOL + j + 1], ALU.add, ALU.mult).then_inc(op_t, 1)
                low_op(Q0["ev_mix"] + 4 + j, uL[:, j, :], T[j % 2][:], uH[:, j, :])
            n, b = AT["ev_out"]
            for j in range(KC):
                residual(b + j, j, mcol(mod, 0, 2))

            def gated_ffn(layer):
                name = f"ff2_{layer}"
                n0, b0 = AT[name]
                q0 = Q0[name + "_u"]

                def pair(p, i=None):
                    last = 0 if i is not None else 1
                    blocks, chunks = (None, None) if i is None else (i * 24, i * 8)
                    for c in range(2):
                        b, q = b0 + 48 * last + 4 * p + 2 + c, q0 + 16 * last + 2 * p + c
                        dve.wait_ge(silu_done, add(chunks, SILUS[b - 2] + 1))
                        dve.wait_ge(blk_done, add(blocks, b + 1))
                        dve.wait_ge(op_lo, add(chunks, q - 1))
                        nc.vector.tensor_tensor(T[(q0 + c) % 2][:], ps[b % 4][:], R[c][:], ALU.mult).then_inc(blk_taken, 1)
                    for c in range(2):
                        q = q0 + 16 * last + 2 * p + c
                        dve.wait_ge(op_hi, add(chunks, q + 1))
                        nc.vector.tensor_tensor(uL[:, 2 * p + c, :], T[(q0 + c) % 2][:], uH[:, 2 * p + c, :].bitcast(F32),
                                                ALU.subtract).then_inc(op_lo, 1)

                with dve.Fori(0, 2) as i:
                    for p in range(4):
                        pair(p, i)
                    for j in range(KC):
                        residual(b0 + 16 + j, j, mcol(mod, layer, 5), i * 24 + (b0 + 16 + j))
                for p in range(3):
                    pair(p)
                for j in range(KC):
                    residual(b0 + 60 + j, j, mcol(mod, layer, 5))

            def gated_norm(name, part, layer):
                norm_adds(name)
                normed(name, mcol(modp, layer, part + 1), Q0[name + "_norm"], mcol(mod, layer, part))

            gated_norm("ff2_0", 3, 0)
            gated_ffn(0)
            gated_norm("od", 0, 1)
            chain(nc.vector.memset(cz[:, :, 0:2], 0.0))
            chain(nc.vector.memset(cz[:, :, 2 + S:4 + S], 0.0))
            chain(nc.vector.memset(vx[:, :, :, ML_V:ML_V + 1], 1.0))
            n, b = AT["od_in"]
            for j in range(KC):
                take(b + j, cz[:, j, 2:2 + S], ps[(b + j) % 4][:])
            for u in range(4):
                for half in range(2):
                    bb = b + 8 + 2 * u + half
                    dve.wait_ge(blk_done, bb + 1)
                    for tb in range(2):
                        src = ps[bb % 4][:, tb * UC:(tb + 1) * UC].rearrange("p (h v) -> p h v", h=2)
                        ins = nc.vector.tensor_copy(vx[:, 2 * half + tb, 2 * u:2 * u + 2, 0:ML_V], src)
                    ins.then_inc(blk_taken, 1)
            for u in range(4):
                take_tokens(b + 16 + 2 * u, mo, u * UC)
            gb_ = b + 24
            dve.wait_ge(blk_done, gb_ + 1)
            dve.wait_ge(op_lo, Q0["od_norm"] + 8)
            nc.vector.tensor_scalar(grow[96:128, :], ps[gb_ % 4][96:128, :], gbias[96:128, :], None, ALU.add).then_inc(blk_taken, 1)
            dve.wait_ge(r_sel, 1)
            chain(nc.vector.tensor_copy(irow[:], ps[4][0:64, :]))
            dve.wait_ge(r_ln, 1)
            chain(nc.vector.tensor_scalar(lrow[:], ps[5][0:64, :], 0.0, None, ALU.min))
            chain(nc.vector.tensor_tensor(lrow[:], lrow[:], Frow[:], ALU.subtract))
            chain(nc.vector.memset(Mrow[:], 0.0))
            one8 = [ones[32 * d:32 * d + 8, 0:1].to_broadcast([8, S]) for d in range(2)]
            chain(nc.vector.tensor_tensor_scan(Frow[0:8, :], one8[0], lrow[0:8, :], 0.0, ALU.mult, ALU.add))
            chain(nc.vector.tensor_tensor_scan(Frow[32:40, ::-1], one8[1], lrow[32:40, ::-1], 0.0, ALU.mult, ALU.add))
            chain(nc.vector.tensor_tensor(irow[:], irow[:], Frow[:], ALU.subtract))
            chain(nc.vector.tensor_tensor_scan(Mrow[0:8, :], irow[0:8, :], irow[0:8, :], 0.0, ALU.max, ALU.max))
            chain(nc.vector.tensor_tensor_scan(Mrow[32:40, ::-1], irow[32:40, ::-1], irow[32:40, ::-1], 0.0, ALU.max, ALU.max))
            nc.vector.tensor_tensor(erow[:], Frow[:], Mrow[:], ALU.add).then_inc(r_rows, 1)
            dve.wait_ge(r_rows, 1)
            nc.vector.tensor_scalar(Mrow[:], Mrow[:], -1.0, None, ALU.mult).then_inc(r_rows, 1)
            for j in range(KC):
                for k in range(CONV_K):
                    tap = cols[:, V_CW + 8 * k + j:V_CW + 8 * k + j + 1]
                    src = cz[:, j, k:k + S]
                    if k == 0:
                        chain(nc.vector.tensor_scalar(cy[:, j, :], src, tap, cols[:, V_CB + j:V_CB + j + 1], ALU.mult, ALU.add))
                    else:
                        ins = nc.vector.scalar_tensor_tensor(out=cy[:, j, :], in0=src, scalar=tap, in1=cy[:, j, :],
                                                             op0=ALU.mult, op1=ALU.add)
                        if k < CONV_K - 1:
                            chain(ins)
                        else:
                            ins.then_inc(c_y, 1)
            dve.wait_ge(c_y, KC)

            def decayed(r):
                h, d, j = r // 8, r // 4 % 2, r % 4
                lo, hi = (j * P, S) if d == 0 else (0, (j + 1) * P)
                dve.wait_ge(l_wm, r + 1)
                dve.wait_ge(l_qk, 4 * h + j + 1)
                if h:
                    dve.wait_ge(l_o, 2 * h - 2 + d + 1)
                nc.vector.scalar_tensor_tensor(out=ma[d][:, j, lo:hi], in0=ps[j][:, lo:hi], scalar=FOX_D ** -0.5,
                                               in1=wt[r % 2][:, lo:hi], op0=ALU.mult, op1=ALU.mult).then_inc(l_a, 1)

            def heads_out(h, d):
                dve.wait_ge(l_o, 2 * h + d + 1)
                row = h + 32 * d
                for p in range(2):
                    den = ps[6 + p][:, 0:258].rearrange("p (a c) -> p a c", a=2)[:, :, ML_V]
                    chain(nc.vector.scalar_tensor_tensor(out=mden[:, 2 * p:2 * p + 2], in0=den, scalar=-1.0,
                                                         in1=ecol[:, 2 * p:2 * p + 2, row], op0=ALU.mult, op1=ALU.max))
                    chain(nc.vector.tensor_tensor(mden[:, 2 * p:2 * p + 2], den, mden[:, 2 * p:2 * p + 2], ALU.max))
                chain(nc.vector.reciprocal(mden[:, 4:8], mden[:, 0:4]))
                for i in range(TB):
                    num = ps[6 + i // 2][:, (i % 2) * 129:(i % 2) * 129 + ML_V]
                    dst = hs[:, i, h * P:(h + 1) * P]
                    if d == 0:
                        ins = nc.vector.tensor_scalar(dst, num, mden[:, 4 + i:5 + i], None, ALU.mult)
                    else:
                        ins = nc.vector.scalar_tensor_tensor(out=dst, in0=num, scalar=mden[:, 4 + i:5 + i], in1=dst,
                                                             op0=ALU.mult, op1=ALU.add)
                ins.then_inc(l_h, 1)
                dve.wait_ge(l_h, 2 * h + d + 1)

            for h in range(ML_H):
                for d in range(2):
                    for j in range(TB):
                        decayed(8 * h + 4 * d + j)
                    if d == 0 and h:
                        heads_out(h - 1, 1)
                    if d == 1:
                        heads_out(h, 0)
            heads_out(ML_H - 1, 1)
            dve.wait_ge(n_sq, 1)
            nc.vector.tensor_reduce(hstat, hsq[:].rearrange("p t (h v) -> p (t h) v", v=ML_V), AX, ALU.add).then_inc(n_sum, 1)
            dve.wait_ge(n_rs, 1)
            dve.wait_ge(gstep, POOL_STEPS + TB)
            for tb in range(TB):
                x = hs[:, tb, :].rearrange("p (h v) -> p h v", v=ML_V)
                chain(nc.vector.tensor_tensor(x, x, hrs[:, 8 * tb:8 * tb + 8].rearrange("p (h o) -> p h o", o=1)
                                              .to_broadcast([P, ML_H, ML_V]), ALU.mult))
                nc.vector.tensor_tensor(hs[:, tb, :], hs[:, tb, :], mo[:, tb, :], ALU.mult).then_inc(n_h, 1)
            for j in range(KC):
                low_op(Q0["od_mix"] + j, uL[:, j, :], ps[4 + j % 4][:], uH[:, j, :])
            n, b = AT["od_out"]
            for j in range(KC):
                residual(b + j, j, mcol(mod, 1, 2))
            gated_norm("ff2_1", 3, 1)
            gated_ffn(1)
            for o in range(2 * TB):
                tb, half = o // 2, o % 2
                dve.wait_ge(o_tr, o + 1)
                nc.vector.tensor_copy(otok[:, tb, half * 512:(half + 1) * 512], ps[4 + o % 4][:]).then_inc(o_cp, 1)

        @block.tensor
        def _(pe):
            def bank_free(b, taken=None, silus=None):
                if b < 4:
                    return
                if BY_ACT[b - 4]:
                    pe.wait_ge(silu_done, add(silus, SILUS[b - 3]))
                else:
                    pe.wait_ge(blk_taken, add(taken, TAKEN[b - 3]))

            def parts(out_ap, wa, xa, first, last):
                (wh, wl), (xh, xl) = wa, xa
                nc.tensor.matmul(out_ap, wh, xh, start=first, stop=False)
                nc.tensor.matmul(out_ap, wh, xl, start=False, stop=False)
                return nc.tensor.matmul(out_ap, wl, xh, start=False, stop=last)

            def unit_ready(n, units=None):
                pe.wait_ge(w_hi, add(units, n + 1))
                pe.wait_ge(w_lo, add(units, n + 1))

            def feature_unit(n, xh, xl, tokens=S, need=None, i=None, du=0, dt=0, ds=0):
                units, taken, silus = (None,) * 3 if i is None else (i * du, i * dt, i * ds)
                unit_ready(n, units)
                kc = UNITS[n][2]
                for c in range(UNITS[n][5]):
                    b = BLOCK0[n] + c
                    bank_free(b, taken, silus)
                    cs = slice(c * P, (c + 1) * P)
                    for k in range(kc):
                        if need is not None and c == 0:
                            pe.wait_ge(op_lo, need(k))
                        ins = parts(ps[b % 4][:, 0:tokens], (wH[n % 2][:, k, cs], wL[n % 2][:, k, cs]),
                                    (xh[:, k, :], xl[:, k, :]), k == 0, k == kc - 1)
                    ins.then_inc(blk_done, 1)

            def token_block(n, b, tbs, xh, xl, c0=0, width=UC):
                bank_free(b)
                for pos, tb in enumerate(tbs):
                    for k in range(KC):
                        ts = slice(tb * P, (tb + 1) * P)
                        ins = parts(ps[b % 4][:, pos * width:(pos + 1) * width], (xh[:, k, ts], xl[:, k, ts]),
                                    (wH[n % 2][:, k, c0:c0 + width], wL[n % 2][:, k, c0:c0 + width]), k == 0, k == KC - 1)
                ins.then_inc(blk_done, 1)

            def token_unit(n, xh, xl, blocks=((0, 1), (2, 3))):
                unit_ready(n)
                for c, tbs in enumerate(blocks):
                    token_block(n, BLOCK0[n] + c, tbs, xh, xl)

            def norm_sum(name):
                i = NORMS[name]
                pe.wait_ge(sq_added, 8 * i + 8)
                nc.tensor.matmul(ps[4][:], ones, ssum[:], start=True, stop=True).then_inc(sum_done, 1)

            def chunks_of(q0):
                return lambda k: q0 + k + 1

            def all_chunks_of(q0):
                return lambda k: q0 + KC

            def attention(kind):
                c = ATT[kind]
                ns = c["heads"] * TB
                pe.wait_ge(blk_taken, TAKEN[BLOCK0[AT[{"fox": "out", "cross": "xo", "grid": "ev_out"}[kind]][0]]])

                def gates_everywhere(h):
                    if h >= 2:
                        pe.wait_ge(f_bcs, h - 1)
                    nc.tensor.matmul(ps[2 + h % 2][:], ident[0:FOX_H, h:h + 1].to_broadcast([FOX_H, P]), frow[0][:],
                                     start=True, stop=True).then_inc(f_bc, 1)

                def scores(g, h, i):
                    hp, blk, ts = (h % 2) * 64, h // 2, slice(i * P, (i + 1) * P)
                    dst = ps[4 + g % 2]
                    if g >= 2:
                        pe.wait_ge(mx_done if kind == "fox" else ex_done, g - 1)
                    if kind == "fox":
                        nc.tensor.matmul(dst[:, 0:(i + 1) * P], fq[hp:hp + 64, blk, ts], fk[hp:hp + 64, blk, 0:(i + 1) * P],
                                         start=True, stop=False)
                        ins = nc.tensor.matmul(dst[:, ts], identb[:], causalb[:], start=False, stop=True)
                    elif kind == "cross":
                        nc.tensor.matmul(dst[:, 0:M_MEM], xq[:, 2 * h, ts], xk[:, 2 * h, :], start=True, stop=False)
                        ins = nc.tensor.matmul(dst[:, 0:M_MEM], xq[:, 2 * h + 1, ts], xk[:, 2 * h + 1, :], start=False, stop=True)
                    else:
                        ins = nc.tensor.matmul(dst[:], evq[hp:hp + 64, blk, ts], kdup[hp:hp + 64, h // 4, :], start=True, stop=True)
                    ins.then_inc(sc_done, 1)

                def values(h):
                    hp = (h % 2) * 64
                    pe.wait_ge(pt_done, c["step0"] + TB * h + TB)
                    if kind == "cross":
                        for cc in range(2):
                            if h:
                                pe.wait_ge(op_lo, c["q0"] + 2 * (h - 1) + cc + 1)
                            for m in range(2):
                                ins = nc.tensor.matmul(ps[cc][:], xv[:, m, h * UC + cc * P:h * UC + (cc + 1) * P],
                                                       pT[h % 2][:, m, :], start=(m == 0), stop=(m == 1))
                            ins.then_inc(pv_done, 1)
                        return
                    if h % 2 == 0 and h >= 4:
                        pe.wait_ge(op_lo, c["q0"] + h // 2 - 1)
                    for j in range(TB):
                        t0 = j * P if kind == "fox" else 0
                        v = fv[:, j, h * 64:(h + 1) * 64] if kind == "fox" else evv[:, j, (h // 4) * 64:(h // 4) * 64 + 64]
                        ins = nc.tensor.matmul(ps[h // 2 % 2][hp:hp + 64, t0:S], v, pT[h % 2][:, j, t0:S],
                                               start=(j == 0), stop=(j == TB - 1))
                    ins.then_inc(pv_done, 1)

                if kind == "fox":
                    pe.wait_ge(f_rows, 1)
                    gates_everywhere(0)
                if kind == "grid":
                    pe.wait_ge(g_kd, 2)
                for s in range(ns + 3):
                    if kind == "fox" and s % 4 == 1 and s // 4 + 1 < FOX_H:
                        gates_everywhere(s // 4 + 1)
                    if s < ns:
                        scores(c["step0"] + s, s // TB, s % TB)
                    t = s - 2
                    if 0 <= t < ns:
                        g, i = c["step0"] + t, t % TB
                        nj = {"fox": i + 1, "cross": 2, "grid": TB}[kind]
                        pe.wait_ge(pn_done, g + 1)
                        if g >= 2:
                            pe.wait_ge(pt_done, g - 1)
                        for j in range(nj):
                            ins = nc.tensor.transpose(ps[6 + g % 2][:, j * P:(j + 1) * P], pr[g % 3][:, j * P:(j + 1) * P], ident)
                        ins.then_inc(tp_done, 1)
                    if s >= 3 and (s - 3) % TB == TB - 1:
                        values((s - 3) // TB)

            pe.wait_ge(cst_in, 16)
            pe.wait_ge(vec_in, 16 * 19)
            nc.tensor.transpose(ps[5][:, 0:V_ROWS], vrow[0:V_ROWS, :], ident[0:V_ROWS, 0:V_ROWS]).then_inc(vec_tr, 1)
            nc.tensor.transpose(ps[5][:, 128:224], brow[0:96, :], ident[0:96, 0:96]).then_inc(vec_tr, 1)
            pe.sem_inc(ada_mm, 2)
            pe.wait_ge(x_in, 16 * TB)
            for j in range(KC):
                if j >= 2:
                    pe.wait_ge(x_cols, j - 1)
                for tb in range(TB):
                    ins = nc.tensor.transpose(ps[6 + j % 2][:, tb * P:(tb + 1) * P], xtok[:, tb, j * P:(j + 1) * P], ident)
                ins.then_inc(x_tr, 1)
            norm_sum("mix")

            n = AT["in"][0]
            for u in range(4):
                feature_unit(n + u, hnH, hnL, need=chunks_of(Q0["mix_norm"]) if u == 0 else None)
            for u in range(4, 6):
                token_unit(n + u, hnH, hnL)
            for u in range(6, 11):
                feature_unit(n + u, hnH, hnL)
            for u in range(11, 13):
                token_unit(n + u, hnH, hnL)
            for u in range(13, 15):
                feature_unit(n + u, hnH, hnL)
            attention("fox")
            v = 0
            for h in range(HG_H):
                for l in range(8):
                    e = 8 * h + l
                    if l < 7:
                        pe.wait_ge(h_q, v + 1)
                        pe.wait_ge(h_k, v + 1)
                    if e >= 2:
                        pe.wait_ge(h_at, e - 1)
                    for c in range(TB):
                        cs = slice(c * P, (c + 1) * P)
                        k_, q_ = (kt[v % 2][:, cs], qt[v % 2][:, cs]) if l < 7 else (gk[:, h, cs], gq[:, h, cs])
                        ins = nc.tensor.matmul(ps[4 + e % 2][:, cs], k_, q_, start=True, stop=True)
                    ins.then_inc(h_pl, 1)
                    v += l < 7
                pe.wait_ge(h_kd, h + 1)
                if h:
                    pe.wait_ge(h_kts, h)
                for c in range(3):
                    ins = nc.tensor.transpose(ps[6][:, c * P:(c + 1) * P], kd[:, c * P:(c + 1) * P], ident)
                ins.then_inc(h_kt, 1)
                pe.wait_ge(h_kts, h + 1)
                if h:
                    pe.wait_ge(h_st, 3 * h)
                hv = slice(h * P, (h + 1) * P)
                for c in range(3):
                    ins = nc.tensor.matmul(ps[7][:, c * P:(c + 1) * P], kdT[:, c, :], gi[:, c, hv], start=True, stop=True)
                ins.then_inc(h_sp, 1)
                pe.wait_ge(h_at, 8 * h + 8)
                pe.wait_ge(h_qb, h + 1)
                pe.wait_ge(h_st, 3 * h + 3)
                if h >= 2:
                    pe.wait_ge(h_os, h - 1)
                for c in range(TB):
                    cs = slice(c * P, (c + 1) * P)
                    ins = nc.tensor.matmul(ps[h % 2][:, cs], gi[:, c, hv], at_[h % 2][:, c, :], start=True, stop=(c == 0))
                    if c:
                        ins = nc.tensor.matmul(ps[h % 2][:, cs], st[:, c - 1, :], qb[:, cs], start=False, stop=True)
                ins.then_inc(h_o, 1)
            hr = [dd[0], dd[1], kt[0], kt[1]]
            for h in range(HG_H):
                pe.wait_ge(h_sq, h + 1)
                nc.tensor.matmul(ps[4 + h][:], ones, hr[h][:], start=True, stop=True).then_inc(h_sum, 1)
            for u, n in enumerate(range(*ranges("out"))):
                feature_unit(n, uH, uL, need=all_chunks_of(Q0["mix"]) if u == 0 else None)
            pe.wait_ge(m_n, 2)
            for j in range(KC):
                if j >= 2:
                    pe.wait_ge(op_lo, Q0["mem"] + j - 1)
                for mb in range(2):
                    ins = nc.tensor.transpose(ps[6 + j % 2][:, mb * P:(mb + 1) * P], mtok[:, mb, j * P:(j + 1) * P], ident)
                ins.then_inc(m_tr, 1)
            norm_sum("x")
            n = AT["xkv"][0]
            for u in range(4):
                feature_unit(n + u, memH, memL, M_MEM, need=chunks_of(Q0["mem"]) if u == 0 else None)
            for u in range(4, 8):
                token_unit(n + u, memH, memL, ((0,), (1,)))
            for u, n in enumerate(range(*ranges("xq"))):
                feature_unit(n, hnH, hnL, need=chunks_of(Q0["x_norm"]) if u == 0 else None)
            attention("cross")
            for u, n in enumerate(range(*ranges("xo"))):
                feature_unit(n, uH, uL, need=all_chunks_of(Q0["x_att"]) if u == 0 else None)
            norm_sum("ff1")
            n0, b0 = AT["ff1"]
            with pe.Fori(0, 4) as i:
                m = 0
                for u in range(8):
                    if u < 4:
                        feature_unit(n0 + u, hnH, hnL, need=chunks_of(Q0["ff1_norm"]) if u == 0 else None, i=i, du=8, dt=16)
                    else:
                        feature_unit(n0 + u, uH, uL, need=(lambda k: i * 8 + (Q0["ff1_u"] + k + 1)) if u == 4 else None,
                                     i=i, du=8, dt=16)
                    for _ in range(2 - u % 2):
                        pe.wait_ge(ada_acc, i * 12 + (m + 3))
                        if m == 0:
                            pe.wait_ge(mod_done, i + 1)
                        nc.tensor.matmul(ps[5][:, 2 * m:2 * m + 1], adacc[m % 2][:, 0:P], ones[:, 0:1], start=True, stop=True)
                        nc.tensor.matmul(ps[5][:, 2 * m + 1:2 * m + 2], adacc[m % 2][:, P:UC], ones[:, 0:1],
                                         start=True, stop=True).then_inc(ada_mm, 1)
                        m += 1
            norm_sum("final")
            norm_sum("ev")
            n = AT["ev_in"][0]
            for u in range(4):
                feature_unit(n + u, hnH, hnL, need=chunks_of(Q0["ev_norm"]) if u == 0 else None)
            n += 4
            unit_ready(n)
            b = BLOCK0[n]
            bank_free(b)
            for k in range(KC):
                ins = parts(ps[b % 4][:], (wH[n % 2][:, k, 0:P], wL[n % 2][:, k, 0:P]), (hnH[:, k, :], hnL[:, k, :]),
                            k == 0, k == KC - 1)
            ins.then_inc(blk_done, 1)
            token_block(n, b + 1, range(TB), hnH, hnL, P, P)
            pe.wait_ge(blk_taken, TAKEN[BLOCK0[AT["ev_out"][0]]])
            for j in range(5):
                pe.wait_ge(g_sq, j + 1)
                nc.tensor.matmul(ps[j][:], cst[:, C_HALF, :], gs[:, j, :], start=True, stop=True).then_inc(g_sum, 1)
            pe.wait_ge(g_rs, 5)
            for j in range(5):
                pe.wait_ge(g_n, j + 1)
                if j >= 2:
                    pe.wait_ge(g_roped, j - 1)
                nc.tensor.matmul(ps[4 + j % 2][:], cst[:, C_ROT, :], evq[:, j, :], start=True, stop=True).then_inc(g_rot, 1)
            pe.wait_ge(g_roped, 5)
            for j in range(2):
                nc.tensor.matmul(ps[6 + j][:], cst[:, C_DUP0 + j, :], evq[:, 4, :], start=True, stop=True).then_inc(g_dup, 1)
            attention("grid")
            for j in range(4):
                pe.wait_ge(p_done, j + 1)
                if j >= 2:
                    pe.wait_ge(op_lo, Q0["ev_mix"] + 4 + j - 1)
                nc.tensor.matmul(ps[2 + j % 2][:], wpool[:, j, :], pd[:, j, :], start=True, stop=True).then_inc(p_mm, 1)
            for u, n in enumerate(range(*ranges("ev_out"))):
                feature_unit(n, uH, uL, need=all_chunks_of(Q0["ev_mix"]) if u == 0 else None)

            def gated_ffn(layer):
                name = f"ff2_{layer}"
                n0, b0 = AT[name]
                q0 = Q0[name + "_u"]
                with pe.Fori(0, 2) as i:
                    for u in range(8):
                        feature_unit(n0 + u, hnH, hnL, need=chunks_of(Q0[name + "_norm"]) if u == 0 else None,
                                     i=i, du=12, dt=16, ds=8)
                    for u in range(8, 12):
                        feature_unit(n0 + u, uH, uL, need=(lambda k: i * 8 + (q0 + k + 1)) if u == 8 else None,
                                     i=i, du=12, dt=16, ds=8)
                for u in range(24, 30):
                    feature_unit(n0 + u, hnH, hnL)
                for u in range(30, 34):
                    feature_unit(n0 + u, uH, uL, need=chunks_of(q0 + 16) if u == 30 else None)

            norm_sum("ff2_0")
            gated_ffn(0)
            norm_sum("od")
            n = AT["od_in"][0]
            for u in range(4):
                feature_unit(n + u, hnH, hnL, need=chunks_of(Q0["od_norm"]) if u == 0 else None)
            for u in range(4, 12):
                token_unit(n + u, hnH, hnL)
            feature_unit(n + 12, hnH, hnL)
            pe.wait_ge(blk_taken, TAKEN[BLOCK0[AT["od_out"][0]]])
            for half in range(2):
                ins = nc.tensor.matmul(ps[4 + half][0:64, :], cst[96:128, C_GSEL, half * 64:(half + 1) * 64], grow[96:128, :],
                                       start=True, stop=True)
            ins.then_inc(r_sel, 1)
            pe.wait_ge(r_rows, 1)
            for tb in range(TB):
                ins = nc.tensor.transpose(ps[6][:, tb * 64:(tb + 1) * 64], irow[:, tb * P:(tb + 1) * P], ident[0:64, 0:64])
            ins.then_inc(r_tr, 1)
            pe.wait_ge(r_em, 1)
            for tb in range(TB):
                ins = nc.tensor.transpose(ps[7][:, tb * 64:(tb + 1) * 64], erow[:, tb * P:(tb + 1) * P], ident[0:64, 0:64])
            ins.then_inc(r_tr, 1)
            pe.wait_ge(r_rows, 2)
            pe.wait_ge(r_cols, 2)

            def out_rows(h, d):
                pe.wait_ge(l_a, 8 * h + 4 * d + 4)
                if 2 * h + d:
                    pe.wait_ge(l_h, 2 * h + d)
                for i in range(TB):
                    dst = ps[6 + i // 2][:, (i % 2) * 129:(i % 2) * 129 + 129]
                    js = range(0, i + 1) if d == 0 else range(i, TB)
                    for j in js:
                        ins = nc.tensor.matmul(dst, ma[d][:, j, i * P:(i + 1) * P], vx[:, j, h, :],
                                               start=(j == js[0]), stop=(j == js[-1]))
                ins.then_inc(l_o, 1)

            pe.wait_ge(c_silu, KC)
            for h in range(ML_H + 1):
                if h:
                    out_rows(h - 1, 0)
                if h < ML_H:
                    for d in range(2):
                        if h:
                            pe.wait_ge(l_w, 8 * (h - 1) + 4 * d + 4)
                        row = h + 32 * d
                        nc.tensor.matmul(ps[4 + d][:], ident[0:64, row:row + 1].to_broadcast([64, P]), Mrow[:],
                                         start=True, stop=True).then_inc(l_bc, 1)
                    hp = (h % 2) * 64
                    for j in range(TB):
                        if h:
                            pe.wait_ge(l_a, 8 * (h - 1) + 4 + j + 1)
                        nc.tensor.matmul(ps[j][:], cy[hp:hp + 64, 4 + h // 2, j * P:(j + 1) * P], cy[hp:hp + 64, h // 2, :],
                                         start=True, stop=True).then_inc(l_qk, 1)
                if h:
                    out_rows(h - 1, 1)
            pe.wait_ge(n_h, TB)
            for j in range(KC):
                if j >= 4:
                    pe.wait_ge(op_lo, Q0["od_mix"] + j - 3)
                for tb in range(TB):
                    ins = nc.tensor.transpose(ps[4 + j % 4][:, tb * P:(tb + 1) * P], hs[:, tb, j * P:(j + 1) * P], ident)
                ins.then_inc(n_tr, 1)
            for u, n in enumerate(range(*ranges("od_out"))):
                feature_unit(n, uH, uL, need=chunks_of(Q0["od_mix"]) if u == 0 else None)
            norm_sum("ff2_1")
            gated_ffn(1)
            pe.wait_ge(blk_taken, TAKEN[-1])
            for o in range(2 * TB):
                tb, half = o // 2, o % 2
                if o >= 4:
                    pe.wait_ge(o_cp, o - 3)
                for j in range(4):
                    ins = nc.tensor.transpose(ps[4 + o % 4][:, j * P:(j + 1) * P], xT[:, 4 * half + j, tb * P:(tb + 1) * P], ident)
                ins.then_inc(o_tr, 1)


def constants():
    c = np.zeros((N_CONST, P, P), np.float32)
    c[C_IDENT] = np.eye(P)
    c[C_ONES] = 1.0
    half = np.arange(P) // 64
    c[C_HALF] = half[:, None] == half[None, :]
    for i in range(0, P, 2):
        c[C_ROT, i + 1, i] = -1.0
        c[C_ROT, i, i + 1] = 1.0
    for kv in range(2):
        for m in range(P):
            c[C_DUP0 + kv, kv * 64 + m % 64, m] = 1.0
    for d in range(2):
        for h in range(ML_H):
            c[C_GSEL, 96 + 16 * d + h, 32 * d + h] = 1.0
            c[C_GSEL, 96 + 16 * d + 8 + h, 64 + 32 * d + h] = 1.0
    t, s = np.arange(P)[:, None], np.arange(P)[None, :]
    c[C_CAUSAL] = np.where(t >= s, 0.0, NEG)
    levels = np.zeros((8, P, P), np.float32)
    s, t = np.arange(P)[:, None], np.arange(P)[None, :]
    for l, L in enumerate(HG_LEVELS):
        levels[l] = (s // (2 * L) == t // (2 * L)) & (s % (2 * L) < L) & (t % (2 * L) >= L)
    levels[7] = s == t
    row, colm = np.repeat(np.arange(S // 64), 64).astype(np.float32), np.tile(np.arange(64), S // 64).astype(np.float32)
    inv = (np.float32(10000.0) ** (-np.arange(16, dtype=np.float32) / np.float32(16))).astype(np.float32)
    ang = np.concatenate([row[:, None] * inv, colm[:, None] * inv], axis=-1)
    lane = (np.arange(P) % 64) // 2
    rope = np.stack([np.cos(ang)[:, lane].T, np.sin(ang)[:, lane].T]).astype(np.float32)
    t = np.arange(S)
    icount = np.stack([1.0 / (np.clip(t + w - w // 2, 0, S) - np.clip(t - w // 2, 0, S)) for w in WINDOWS]).astype(np.float32)
    return {"const": c, "levels": levels, "rope": np.ascontiguousarray(rope), "icount": icount}


_INS = ["x", "mem", "norm_mix_g", "w_in", "fox_f_bias", "hgrn_lb_logits", "hgrn_norm_g", "w_out", "norm_x_g", "norm_mem_g",
        "w_xq", "w_xkv", "w_xo", "norm_ff_g", "w1", "w2", "final_norm_g", "c_2", "ada_w_2", "ada_b_2", "ev_w_in_2",
        "ev_w_pool_2", "ev_b_pool_2", "ev_pool_scale_2", "ev_q_gain_2", "ev_k_gain_2", "ev_w_out_2", "od_w_in_2",
        "od_conv_w_2", "od_conv_b_2", "od_gate_b_2", "od_head_gain_2", "od_w_out_2", "ffn_w1_2", "ffn_w3_2", "ffn_w2_2"]


def kernel(**inputs):
    import numpy as _np
    import concourse.bacc as _bacc
    from concourse import mybir as _mybir
    from concourse.bass_utils import run_bass_kernel_spmd as _run

    nc = _bacc.Bacc("TRN2", target_bir_lowering=False, num_devices=1)
    arrays, aps = {}, {}
    given = {name: _np.ascontiguousarray(inputs[name]) for name in _INS}
    given.update(constants())
    for name, value in given.items():
        arrays[f"in_{name}_dram"] = value
        aps[name] = nc.dram_tensor(f"in_{name}_dram", value.shape, _mybir.dt.from_np(value.dtype), kind="ExternalInput").ap()
    out = nc.dram_tensor("out_0_dram", (1, S, D), _mybir.dt.float32, kind="ExternalOutput").ap()
    bass_block_pair(nc, aps, out)
    r = _run(nc, [arrays], core_ids=[0])
    return r.results[0]["out_0_dram"]
```

```python
from contextlib import ExitStack

import numpy as np

import concourse.bass as bass
from concourse import mybir

F32 = mybir.dt.float32
F32R = mybir.dt.float32r
BF16 = mybir.dt.bfloat16
U32 = mybir.dt.uint32
ALU = mybir.AluOpType
ACT = mybir.ActivationFunctionType
AX = mybir.AxisListType.X

P = 128
D = 1024
S = 512
KC = D // P
TB = S // P
M_MEM = 256
EPS = 1e-6
UC = 256
FF1 = 4096
FF2 = 2816
FOX_H, FOX_D = 8, 64
HG_H = 4
HG_LEVELS = (1, 2, 4, 8, 16, 32, 64)
X_H = 4
GA_H = 8
ML_H, ML_V = 8, 128
WINDOWS = (2, 4, 8, 16)
CONV_K = 5
NEG = -1.0e30

C_IDENT, C_ONES, C_HALF, C_ROT, C_DUP0, C_DUP1, C_GSEL, C_CAUSAL = range(8)
N_CONST = 8

V_MIX, V_X, V_MEM, V_FF, V_FINAL, V_LB, V_HG, V_C, V_BPOOL, V_SPOOL, V_CW, V_CB, V_QG, V_KG = (
    0, 8, 16, 24, 32, 40, 48, 49, 57, 61, 65, 105, 113, 114)
V_ROWS = 115


def plan():
    units = []

    def add(w, k0, kc, c0, cols, blocks=2):
        units.append((w, k0, kc, c0, cols, blocks))

    at = {}

    def stage(name):
        at[name] = (len(units), sum(u[5] for u in units))

    stage("in")
    for c0 in (0, 256, 512, 768, 1024, 1280):
        add("w_in", 0, KC, c0, UC)
    add("w_in", 0, KC, 1536, P, 1)
    for c0 in range(1544, 3592, UC):
        add("w_in", 0, KC, c0, UC)
    stage("out")
    for c0 in range(0, D, UC):
        add("w_out", 0, KC, c0, UC)
    stage("xkv")
    for c0 in range(0, 2 * D, UC):
        add("w_xkv", 0, KC, c0, UC)
    stage("xq")
    for c0 in range(0, D, UC):
        add("w_xq", 0, KC, c0, UC)
    stage("xo")
    for c0 in range(0, D, UC):
        add("w_xo", 0, KC, c0, UC)
    stage("ff1")
    for g in range(FF1 // D):
        for c0 in range(g * D, (g + 1) * D, UC):
            add("w1", 0, KC, c0, UC)
        for c0 in range(0, D, UC):
            add("w2", g * KC, KC, c0, UC)
    stage("ev_in")
    for c0 in range(0, 1280, UC):
        add("ev_w_in_2", 0, KC, c0, UC)
    stage("ev_out")
    for c0 in range(0, D, UC):
        add("ev_w_out_2", 0, KC, c0, UC)
    for layer in range(2):
        if layer == 1:
            stage("od_in")
            for c0 in range(0, 3072, UC):
                add("od_w_in_2", 0, KC, c0, UC)
            add("od_w_in_2", 0, KC, 3104 - P, P, 1)
            stage("od_out")
            for c0 in range(0, D, UC):
                add("od_w_out_2", 0, KC, c0, UC)
        stage(f"ff2_{layer}")
        for g0 in range(0, FF2, D):
            for c0 in range(g0, min(g0 + D, FF2), UC):
                add(f"ffn_w1_2.{layer}", 0, KC, c0, UC)
                add(f"ffn_w3_2.{layer}", 0, KC, c0, UC)
            for c0 in range(0, D, UC):
                add(f"ffn_w2_2.{layer}", g0 // P, min(g0 + D, FF2) // P - g0 // P, c0, UC)
    stage("end")
    return units, at


UNITS, AT = plan()
N_UNITS = len(UNITS)
BLOCK0 = [sum(u[5] for u in UNITS[:n]) for n in range(N_UNITS + 1)]
BY_ACT = [u[0].startswith("ffn_w1") for u in UNITS for _ in range(u[5])]
TAKEN = [sum(not x for x in BY_ACT[:b]) for b in range(len(BY_ACT) + 1)]
SILUS = [sum(x for x in BY_ACT[:b]) for b in range(len(BY_ACT) + 1)]

Q0 = {}
_q = 0
for _name, _count in (("mix_norm", 8), ("mix", 8), ("mem", 8), ("x_norm", 8), ("x_att", 8), ("ff1_norm", 8),
                      ("ff1_u", 32), ("ev_norm", 8), ("ev_mix", 8), ("ff2_0_norm", 8), ("ff2_0_u", 22),
                      ("od_norm", 8), ("od_mix", 8), ("ff2_1_norm", 8), ("ff2_1_u", 22)):
    Q0[_name] = _q
    _q += _count

ATT = {
    "fox": dict(heads=FOX_H, step0=0, pv0=0, pvh=1, q0=Q0["mix"], col0=0),
    "cross": dict(heads=X_H, step0=32, pv0=8, pvh=2, q0=Q0["x_att"], col0=0),
    "grid": dict(heads=GA_H, step0=48, pv0=16, pvh=1, q0=Q0["ev_mix"], col0=4),
}
NORMS = {n: i for i, n in enumerate(("mix", "x", "ff1", "ev", "ff2_0", "od", "ff2_1"))}
SQ0 = {n: 8 * (i - 1) + (8 if i > NORMS["ev"] else 0) for n, i in NORMS.items() if i}


ADA_RING = 4
ADA_GROUP = (8, 12)
GA_SCALE = 64 ** -0.5
LB_SHIFTED = 3
POOL_STEPS = sum(g + 2 for g in range(len(WINDOWS)))


def ranges(name):
    starts = sorted(v[0] for v in AT.values())
    n = AT[name][0]
    return n, starts[starts.index(n) + 1]


def add(i, count):
    return count if i is None else i + count


def outputs(kind, t):
    h = t // TB
    if t % TB != TB - 1 or not 0 <= h < ATT[kind]["heads"]:
        return []
    return [2 * h, 2 * h + 1] if kind == "cross" else [h // 2] if h % 2 else []


def bass_block_pair(nc, a, out):
    BASE = 16512
    top = [0]

    def place(name, shape, dt, offset=None):
        size = int(np.prod(shape[1:])) * (2 if dt == BF16 else 4)
        if offset is None:
            offset = top[0]
            top[0] += -(-size // 32) * 32
        return nc.alloc_sbuf_tensor_at(name, shape, dt, offset=BASE + offset), offset

    raw = [place(f"raw{i}", [P, KC, UC], F32)[0] for i in range(2)]
    wH = [place(f"wH{i}", [P, KC, UC], F32R)[0] for i in range(2)]
    wL = [place(f"wL{i}", [P, KC, UC], F32R)[0] for i in range(2)]
    xT = place("xT", [P, KC, S], F32)[0]
    hnH, HN = place("hnH", [P, KC, S], F32R)
    hnL = place("hnL", [P, KC, S], F32R)[0]
    uH = place("uH", [P, KC, S], F32R)[0]
    uL = place("uL", [P, KC, S], F32R)[0]
    cst = place("cst", [P, N_CONST, P], F32)[0]
    identb = place("identb", [P, P], BF16)[0]
    causalb = place("causalb", [P, P], BF16)[0]
    cols = place("cols", [P, P], F32)[0]
    adab = place("adab", [P, 96], F32)[0]
    mod = place("mod", [P, 96], F32)[0]
    modp = place("modp", [P, 96], F32)[0]
    small = place("small", [P, 192], F32)[0]
    T, TOFF = [], []
    for i in range(2):
        t, o = place(f"T{i}", [P, S], F32)
        T.append(t)
        TOFF.append(o)
    R, ROFF = [], []
    for i in range(2):
        t, o = place(f"R{i}", [P, S], F32)
        R.append(t)
        ROFF.append(o)
    sq, SQOFF = [], []
    for i in range(2):
        t, o = place(f"sq{i}", [P, S], F32)
        sq.append(t)
        SQOFF.append(o)
    ssum, SSOFF = place("ssum", [P, S], F32)
    gsum, GSOFF = place("gsum", [P, S], F32)
    AR = top[0]
    assert BASE + AR + 57600 <= 229344, AR

    ident = cst[:, C_IDENT, :]
    ones = cst[:, C_ONES, :]

    eps = small[:, 0:1]
    nmax = small[:, 4:8]
    rsum = small[:, 8:12]
    rinv = small[:, 12:16]
    lb = small[:, 16:20]
    omlb = small[:, 20:24]
    lbt = small[:, 24:40]
    condc = small[:, 40:48]
    fbias = small[:, 48:49]
    gbias = small[:, 49:50]
    mstat = small[:, 56:64]
    mden = small[:, 64:72]
    hstat = small[:, 72:104]
    hrs = small[:, 104:136]
    nmraw = small[:, 136:140]
    warm = small[:, 140:141]
    root = small[:, 168:172]
    rootinv = small[:, 150:154]
    msq = small[:, 154:158]
    gm = small[:, 160:168]

    xtok = place("xtok", [P, TB, D], F32, AR)[0]
    vrow = place("vrow", [P, P], F32, AR + 16384)[0]
    brow = place("brow", [P, P], F32, AR + 16896)[0]
    fq = place("fq", [P, 4, S], F32, AR)[0]
    fk = place("fk", [P, 4, S], F32, AR + 8192)[0]
    fv = place("fv", [P, TB, 512], F32, AR + 16384)[0]
    gq = place("gq", [P, HG_H, S], F32, AR + 24576)[0]
    gk = place("gk", [P, HG_H, S], F32, AR + 32768)[0]
    gi = place("gi", [P, TB, 512], F32, AR + 40960)[0]
    gg = place("gg", [P, HG_H, S], F32, AR + 49152)[0]
    pr = [place(f"pr{i}", [P, S], F32, HN + 2048 * i)[0] for i in range(3)]
    pT = [place(f"pT{i}", [P, TB, S], F32, HN + 6144 + 8192 * i)[0] for i in range(2)]
    fbc = [place(f"fbc{i}", [P, S], F32, HN + 22528 + 2048 * i)[0] for i in range(2)]
    fz = place("fz", [FOX_H, S], F32, TOFF[0])[0]
    frow = [place(f"frow{i}", [FOX_H, S], F32, HN + 26624 + 2048 * i)[0] for i in range(3)]
    gb = place("gb", [P, HG_H, S], F32, AR)[0]
    lvl = place("lvl", [P, 8, P], F32, AR + 8192)[0]
    ho = place("ho", [P, HG_H, S], F32, AR + 12288)[0]
    hrsb = [place(f"hrsb{i}", [P, S], F32, AR + 20480 + 2048 * i)[0] for i in range(2)]
    dd = [place(f"dd{i}", [P, S], F32, HN + 2048 * i)[0] for i in range(2)]
    qt = [place(f"qt{i}", [P, S], F32, HN + 4096 + 2048 * i)[0] for i in range(2)]
    kt = [place(f"kt{i}", [P, S], F32, HN + 8192 + 2048 * i)[0] for i in range(2)]
    at_ = [place(f"at{i}", [P, TB, P], F32, HN + 12288 + 2048 * i)[0] for i in range(2)]
    qb = place("qb", [P, S], F32, HN + 16384)[0]
    kd = place("kd", [P, S], F32, HN + 18432)[0]
    eb = place("eb", [P, S], F32, HN + 20480)[0]
    ed = place("ed", [P, S], F32, HN + 22528)[0]
    kdT = place("kdT", [P, 3, P], F32, HN + 24576)[0]
    st = place("st", [P, 3, P], F32, HN + 26112)[0]
    rmask = place("rmask", [P, S], F32, HN + 27648)[0]
    memH = place("memH", [P, KC, M_MEM], F32R, AR)[0]
    memL = place("memL", [P, KC, M_MEM], F32R, AR + 8192)[0]
    mtok = place("mtok", [P, 2, D], F32, AR + 49152)[0]
    xk = place("xk", [P, KC, M_MEM], F32, AR + 16384)[0]
    xv = place("xv", [P, 2, D], F32, AR + 24576)[0]
    xq = place("xq", [P, KC, S], F32, AR + 32768)[0]
    mdump = place("mdump", [P, D], F32, HN)[0]
    xdump = place("xdump", [P, D], F32, AR + 20480)[0]
    mT = [place(f"mT{i}", [P, M_MEM], F32, ROFF[i])[0] for i in range(2)]
    adaw = [place(f"adaw{i}", [P, KC, UC], F32, AR + 8192 * i)[0] for i in range(ADA_RING)]
    adacc = [place(f"adacc{i}", [P, UC], F32, AR + 8192 * ADA_RING + 1024 * i)[0] for i in range(2)]
    pu = place("pu", [P, 4, S + 24], F32, AR)[0]
    evq = place("evq", [P, 5, S], F32, AR + 8704)[0]
    evv = place("evv", [P, TB, P], F32, AR + 18944)[0]
    kdup = place("kdup", [P, 2, S], F32, AR + 20992)[0]
    cosb = place("cosb", [P, S], F32, AR + 25088)[0]
    sinb = place("sinb", [P, S], F32, AR + 27136)[0]
    icnt = place("icnt", [P, 4, S], F32, AR + 29184)[0]
    gs = place("gs", [P, 5, S], F32, HN)[0]
    wpool = place("wpool", [P, 4, P], F32, AR + 37376)[0]
    pw = [place(f"pw{i}", [P, S + 24], F32, AR + 39424 + 2176 * i)[0] for i in range(2)]
    pd = place("pd", [P, 4, S], F32, AR + 43776)[0]
    cz = place("cz", [P, KC, S + 4], F32, AR)[0]
    hs = place("hs", [P, TB, D], F32, AR)[0]
    vx = place("vx", [P, TB, ML_H, ML_V + 1], F32, AR + 16512)[0]
    mo = place("mo", [P, TB, D], F32, AR + 33024)[0]
    hgain = place("hgain", [P, D], F32, AR + 49408)[0]
    wt = [place(f"wt{i}", [P, S], F32, AR + 53504 + 2048 * i)[0] for i in range(2)]
    cy = place("cy", [P, KC, S], F32, HN)[0]
    ma = [place(f"ma{i}", [P, TB, S], F32, HN + 16384 + 8192 * i)[0] for i in range(2)]
    hsq = place("hsq", [P, TB, D], F32, HN)[0]
    grow = place("grow", [P, S], F32, TOFF[0])[0]
    irow = place("irow", [64, S], F32, TOFF[1])[0]
    lrow = place("lrow", [64, S], F32, ROFF[0])[0]
    Frow = place("Frow", [64, S], F32, ROFF[1])[0]
    Mrow = place("Mrow", [64, S], F32, SQOFF[0])[0]
    erow = place("erow", [64, S], F32, SQOFF[1])[0]
    ccol = place("ccol", [P, TB, 64], F32, SSOFF)[0]
    ecol = place("ecol", [P, TB, 64], F32, GSOFF)[0]
    otok = place("otok", [P, TB, D], F32, AR)[0]

    with ExitStack() as ctx:
        ps = [ctx.enter_context(nc.psum_tensor(f"ps{i}", [P, S], F32)) for i in range(8)]

        def sem(name):
            return ctx.enter_context(nc.semaphore(name))

        raw_in = [sem(f"raw_in{i}") for i in range(2)]
        w_hi, w_lo = sem("w_hi"), sem("w_lo")
        blk_done = sem("blk_done")
        blk_taken = sem("blk_taken")
        op_t, op_hi, op_lo = sem("op_t"), sem("op_hi"), sem("op_lo")
        sq_done, sq_added, sum_done, root_done, inv_done, bc_done = (
            sem("sq_done"), sem("sq_added"), sem("sum_done"), sem("root_done"), sem("inv_done"), sem("bc_done"))
        cst_in, x_in, vec_in, vec_tr, vec_cols = sem("cst_in"), [sem(f"x_in{i}") for i in range(TB)], sem("vec_in"), sem("vec_tr"), sem("vec_cols")
        x_tr, x_cols = sem("x_tr"), sem("x_cols")
        setup, setup_d = sem("setup"), sem("setup_d")
        dstep = sem("dstep")
        astep = sem("astep")
        gstep = sem("gstep")
        sc_done, mx_done, ex_done, pn_done, tp_done, pt_done, pv_done = (
            sem("sc_done"), sem("mx_done"), sem("ex_done"), sem("pn_done"), sem("tp_done"), sem("pt_done"), sem("pv_done"))
        f_z, f_e, f_l, f_rows, f_bc, f_bcs = sem("f_z"), sem("f_e"), sem("f_l"), sem("f_rows"), sem("f_bc"), sem("f_bcs")
        lvl_in = sem("lvl_in")
        h_act, h_fk, h_ln, h_b = sem("h_act"), sem("h_fk"), sem("h_ln"), sem("h_b")
        h_d, h_e, h_q, h_k, h_pl, h_at = sem("h_d"), sem("h_e"), sem("h_q"), sem("h_k"), sem("h_pl"), sem("h_at")
        h_eb, h_qb, h_kd, h_kt, h_kts, h_sp, h_st, h_o, h_os = (
            sem("h_eb"), sem("h_qb"), sem("h_kd"), sem("h_kt"), sem("h_kts"), sem("h_sp"), sem("h_st"), sem("h_o"), sem("h_os"))
        h_sq, h_sum, h_rs, h_t = sem("h_sq"), sem("h_sum"), sem("h_rs"), sem("h_t")
        mem_in, m_root, m_n, m_tr, m_t = sem("mem_in"), sem("m_root"), sem("m_n"), sem("m_tr"), sem("m_t")
        ada_in = [sem(f"ada_in{i}") for i in range(ADA_RING)]
        ada_step = sem("ada_step")
        ada_acc, ada_mm, mod_done = sem("ada_acc"), sem("ada_mm"), sem("mod_done")
        relu_done, silu_done = sem("relu_done"), sem("silu_done")
        e_ms, e_root, e_inv = sem("e_ms"), sem("e_root"), sem("e_inv")
        ev_in, g_sq, g_sum, g_rs, g_n, g_rot, g_roped, g_dup, g_kd = (
            sem("ev_c_in"), sem("g_sq"), sem("g_sum"), sem("g_rs"), sem("g_n"), sem("g_rot"), sem("g_roped"), sem("g_dup"), sem("g_kd"))
        p_done, p_mm = sem("p_done"), sem("p_mm")
        gain_in, c_pad, c_y, c_silu, o_sig = sem("gain_in"), sem("c_pad"), sem("c_y"), sem("c_silu"), sem("o_sig")
        r_g, r_sel, r_i, r_abs, r_ln, r_rows, r_em, r_tr, r_cols = (
            sem("r_g"), sem("r_sel"), sem("r_i"), sem("r_abs"), sem("r_ln"), sem("r_rows"), sem("r_em"), sem("r_tr"), sem("r_cols"))
        l_bc, l_qk, l_w, l_a, l_wm, l_o, l_h = sem("l_bc"), sem("l_qk"), sem("l_w"), sem("l_a"), sem("l_wm"), sem("l_o"), sem("l_h")
        n_sq, n_sum, n_rs, n_h, n_tr = sem("n_sq"), sem("n_sum"), sem("n_rs"), sem("n_h"), sem("n_tr")
        o_tr, o_cp, o_out = sem("o_tr"), sem("o_cp"), sem("o_out")

        block = ctx.enter_context(nc.Block())

        def weight_view(name):
            if "." in name:
                name, layer = name.split(".")
                w = a[name][int(layer)]
            else:
                w = a[name][0]
            return w.rearrange("(k p) n -> p k n", p=P)

        @block.sync
        def _(sp):
            def load(n, value=None, src=None):
                w, k0, kc, c0, c, _ = UNITS[n]
                if n >= 2:
                    sp.wait_ge(w_lo, (n if value is None else value) - 1)
                if src is None:
                    src = weight_view(w)[:, k0:k0 + kc, c0:c0 + c]
                sp.dma_start(raw[n % 2][:, 0:kc, 0:c], src).then_inc(raw_in[n % 2], 16)

            def loads(first, last):
                for n in range(first, last):
                    load(n)

            sp.dma_start(cst[:], a["const"].rearrange("c p m -> p c m")).then_inc(cst_in, 16)
            rows = [("norm_mix_g", V_MIX, 8), ("norm_x_g", V_X, 8), ("norm_mem_g", V_MEM, 8), ("norm_ff_g", V_FF, 8),
                    ("final_norm_g", V_FINAL, 8), ("hgrn_lb_logits", V_LB, 8), ("hgrn_norm_g", V_HG, 1), ("c_2", V_C, 8),
                    ("ev_b_pool_2", V_BPOOL, 4), ("ev_pool_scale_2", V_SPOOL, 4), ("od_conv_w_2", V_CW, 40),
                    ("od_conv_b_2", V_CB, 8)]
            for tb in range(TB):
                sp.dma_start(xtok[:, tb, :], a["x"][0, tb * P:(tb + 1) * P, :]).then_inc(x_in[tb], 16)
            for name, r0, count in rows:
                src = a[name]
                nd = len(src.shape)
                flat = {1: "a -> a", 2: "a b -> (a b)", 3: "a b c -> (a b c)"}[nd]
                src = src if nd == 1 else src.rearrange(flat)
                sp.dma_start(vrow[r0:r0 + count, :], src.rearrange("(r m) -> r m", m=P)).then_inc(vec_in, 16)
            for name, r0 in (("ev_q_gain_2", V_QG), ("ev_k_gain_2", V_KG)):
                for half in range(2):
                    sp.dma_start(vrow[r0:r0 + 1, half * 64:half * 64 + 64], a[name][0:1, :]).then_inc(vec_in, 16)
            sp.dma_start(brow[0:96, :], a["ada_b_2"].rearrange("l (r m) -> (l r) m", m=P)).then_inc(vec_in, 16)
            sp.dma_start(fbias[0:8, :], a["fox_f_bias"].rearrange("a b -> b a")).then_inc(vec_in, 16)
            sp.dma_start(gbias[96:128, :], a["od_gate_b_2"].rearrange("a b -> b a")).then_inc(vec_in, 16)
            loads(0, AT["out"][0] + 1)
            sp.wait_ge(op_lo, Q0["mix"] + 4)
            sp.dma_start(lvl[:], a["levels"].rearrange("l s t -> s l t")).then_inc(lvl_in, 16)
            sp.wait_ge(op_lo, Q0["mix"] + 8)
            for mb in range(2):
                sp.dma_start(mtok[:, mb, :], a["mem"][0, mb * P:(mb + 1) * P, :]).then_inc(mem_in, 16)
            loads(AT["out"][0] + 1, AT["ff1"][0])

            def load_ada(layer, i, m):
                group = ADA_GROUP[layer]
                sp.wait_ge(ada_acc, i * group + (24 * layer + m + 1))
                adav = a["ada_w_2"][layer].rearrange("(k p) n -> p k n", p=P)
                sp.dma_start(adaw[m % ADA_RING][:], adav[:, :, bass.ds(i * (group * UC) + m * UC, UC)]).then_inc(
                    ada_in[m % ADA_RING], 16)

            n0 = AT["ff1"][0]
            w1v, w2v = weight_view("w1"), weight_view("w2")
            sp.wait_ge(op_lo, Q0["x_att"] + 8)
            with sp.Fori(0, 3) as i:
                for u in range(8):
                    if u < 4:
                        load(n0 + u, i * 8 + (n0 + u), w1v[:, :, bass.ds(i * D + u * UC, UC)])
                    else:
                        load(n0 + u, i * 8 + (n0 + u), w2v[:, bass.ds(i * KC, KC), (u - 4) * UC:(u - 3) * UC])
                    load_ada(0, i, u)
            loads(n0 + 24, n0 + 32)
            loads(AT["ev_in"][0], AT["ev_out"][0])
            sp.wait_ge(mod_done, 5)
            sp.dma_start(cosb[:], a["rope"][0]).then_inc(ev_in, 16)
            sp.dma_start(sinb[:], a["rope"][1]).then_inc(ev_in, 16)
            sp.dma_start(wpool[:], a["ev_w_pool_2"][0].rearrange("g c d -> c g d")).then_inc(ev_in, 16)
            sp.dma_start(icnt[:], a["icount"].rearrange("(o g) t -> o g t", o=1).to_broadcast([P, 4, S])).then_inc(ev_in, 16)
            loads(AT["ev_out"][0], AT["ff2_0"][0])

            def gated_ffn(layer):
                n0 = AT[f"ff2_{layer}"][0]
                w1v, w3v, w2v = (weight_view(f"ffn_w{j}_2.{layer}") for j in (1, 3, 2))
                with sp.Fori(0, 2) as i:
                    for u in range(12):
                        if u < 8:
                            src = (w1v, w3v)[u % 2][:, :, bass.ds(i * D + (u // 2) * UC, UC)]
                        else:
                            src = w2v[:, bass.ds(i * KC, KC), (u - 8) * UC:(u - 7) * UC]
                        load(n0 + u, i * 12 + (n0 + u), src)
                        if layer == 0:
                            load_ada(1, i, u)
                loads(n0 + 24, n0 + 34)

            sp.wait_ge(op_lo, Q0["ev_mix"] + 8)
            gated_ffn(0)
            loads(AT["od_in"][0], AT["od_in"][0] + 2)
            sp.wait_ge(op_lo, Q0["od_norm"] + 8)
            sp.dma_start(hgain[:], a["od_head_gain_2"].rearrange("o h v -> o (h v)").to_broadcast([P, D])).then_inc(gain_in, 16)
            loads(AT["od_in"][0] + 2, AT["ff2_1"][0])
            gated_ffn(1)
            for tb in range(TB):
                sp.wait_ge(o_cp, 2 * tb + 2)
                sp.dma_start(out[0, tb * P:(tb + 1) * P, :], otok[:, tb, :]).then_inc(o_out, 16)
            sp.wait_ge(o_out, 16 * TB)

        @block.gpsimd
        def _(pool):
            def low(n, value=None):
                _, _, kc, _, c, _ = UNITS[n]
                pool.wait_ge(w_hi, (n if value is None else value) + 1)
                nc.gpsimd.tensor_tensor(wL[n % 2][:, 0:kc, 0:c], raw[n % 2][:, 0:kc, 0:c],
                                        wH[n % 2][:, 0:kc, 0:c].bitcast(F32), ALU.subtract).then_inc(w_lo, 1)

            def lows(first, last):
                for n in range(first, last):
                    low(n)

            lows(0, AT["out"][0] + 1)
            v = 0
            for h in range(HG_H):
                for l in range(len(HG_LEVELS)):
                    pool.wait_ge(h_e, v + 1)
                    if v >= 2:
                        pool.wait_ge(h_pl, 8 * ((v - 2) // 7) + (v - 2) % 7 + 1)
                    nc.gpsimd.tensor_tensor(kt[v % 2][:], gk[:, h, :], dd[v % 2][:], ALU.mult).then_inc(h_k, 1)
                    v += 1
                pool.wait_ge(h_eb, 2 * h + 2)
                if h:
                    pool.wait_ge(h_kt, h)
                nc.gpsimd.tensor_tensor(kd[:], gk[:, h, :], ed[:], ALU.mult).then_inc(h_kd, 1)
            lows(AT["out"][0] + 1, AT["ff1"][0])
            n0 = AT["ff1"][0]
            with pool.Fori(0, 4) as i:
                for u in range(8):
                    low(n0 + u, i * 8 + (n0 + u))
            lows(AT["ev_in"][0], AT["ev_out"][0] + 1)
            pool.wait_ge(ev_in, 64)
            pool.wait_ge(blk_taken, TAKEN[BLOCK0[AT["ev_in"][0]] + 4])
            g = 0
            for grp, w in enumerate(WINDOWS):
                src, half = pu[:, grp, :], 1
                for lev in range(grp + 1):
                    n_out = S + 16 - 2 * half + 1
                    if g:
                        pool.wait_ge(gstep, g)
                    dst = pw[lev % 2]
                    nc.gpsimd.tensor_tensor(dst[:, 0:n_out], src[:, 0:n_out], src[:, half:half + n_out], ALU.add).then_inc(gstep, 1)
                    g += 1
                    src, half = dst[:], 2 * half
                off = 8 - w // 2
                pool.wait_ge(gstep, g)
                nc.gpsimd.tensor_tensor(pd[:, grp, :], src[:, off:off + S], icnt[:, grp, :], ALU.mult).then_inc(gstep, 1)
                g += 1
                pool.wait_ge(gstep, g)
                nc.gpsimd.tensor_tensor(pd[:, grp, :], pd[:, grp, :], pu[:, grp, 8:8 + S], ALU.subtract).then_inc(p_done, 1)

            def gated_ffn(layer):
                n0 = AT[f"ff2_{layer}"][0]
                with pool.Fori(0, 2) as i:
                    for u in range(12):
                        low(n0 + u, i * 12 + (n0 + u))
                lows(n0 + 24, n0 + 34)

            lows(AT["ev_out"][0] + 1, AT["ff2_0"][0])
            gated_ffn(0)
            lows(AT["od_in"][0], AT["od_out"][0] + 1)
            pool.wait_ge(gain_in, 16)
            pool.wait_ge(o_sig, 1)
            for tb in range(TB):
                nc.gpsimd.tensor_tensor(mo[:, tb, :], mo[:, tb, :], hgain[:], ALU.mult).then_inc(gstep, 1)
            for h in range(ML_H):
                for d in range(2):
                    for j in range(TB):
                        r = 8 * h + 4 * d + j
                        pool.wait_ge(l_w, r + 1)
                        diag = wt[r % 2][:, j * P:(j + 1) * P]
                        sign = 1 if d == 0 else -1
                        nc.gpsimd.affine_select(out=diag, in_=diag, compare_op=ALU.is_ge, fill=0.0, base=0,
                                                pattern=[[sign, P]], channel_multiplier=-sign).then_inc(l_wm, 1)
            lows(AT["od_out"][0] + 1, AT["ff2_1"][0])
            gated_ffn(1)

        @block.scalar
        def _(act):
            acts = [0]

            def chain(ins):
                acts[0] += 1
                ins.then_inc(astep, 1)
                act.wait_ge(astep, acts[0])

            def high(n, i=None, du=0, db=0):
                if n >= N_UNITS:
                    return
                _, _, kc, _, c, _ = UNITS[n]
                act.wait_ge(raw_in[n % 2], add(None if i is None else i * (8 * du), 16 * (n // 2 + 1)))
                if n >= 2:
                    act.wait_ge(blk_done, add(None if i is None else i * db, BLOCK0[n - 1]))
                nc.scalar.activation(wH[n % 2][:, 0:kc, 0:c], raw[n % 2][:, 0:kc, 0:c], ACT.Copy).then_inc(w_hi, 1)

            def squares(name, ready, gain=None):
                q = SQ0[name]
                for j in range(KC):
                    act.wait_ge(*ready(j))
                    for g in range(1 if gain is None else 2):
                        if q >= 2:
                            act.wait_ge(sq_added, q - 1)
                        scale = gain(j) if g else 1.0
                        nc.scalar.activation(sq[q % 2][:], xT[:, j, :], ACT.Square, scale=scale).then_inc(sq_done, 1)
                        q += 1
                nc.scalar.activation(warm, eps, ACT.Sqrt)

            def roots(name):
                act.wait_ge(sum_done, NORMS[name])
                act.wait_ge(inv_done, NORMS[name])
                nc.scalar.activation(root, ps[6][:, 0:4], ACT.Sqrt, bias=eps, scale=1.0 / D).then_inc(root_done, 1)

            def high_op(q, dstH, src, wait, bias=None):
                act.wait_ge(*wait)
                if bias is None:
                    nc.scalar.activation(dstH, src, ACT.Copy).then_inc(op_hi, 1)
                else:
                    nc.scalar.activation(dstH, src, ACT.Identity, bias=bias).then_inc(op_hi, 1)

            tq = [0]

            def norm_high(q0, j, shift=None):
                tq[0] += 1
                high_op(q0 + j, hnH[:, j, :], T[(q0 + j) % 2][:], (op_t, tq[0]), None if shift is None else shift(j))

            def norm_highs(q0, shift=None):
                for j in range(KC):
                    norm_high(q0, j, shift)

            def attention(kind):
                c = ATT[kind]
                ns = c["heads"] * TB
                width = {"fox": None, "cross": M_MEM, "grid": S}[kind]
                for s in range(ns + 6):
                    g = c["step0"] + s
                    if kind == "fox":
                        h = 0 if s == 0 else (s + 2) // 4 if s % 4 == 2 else FOX_H
                        if h < FOX_H:
                            act.wait_ge(f_bc, h + 1)
                            if h >= 2:
                                act.wait_ge(mx_done, 4 * (h - 1))
                            nc.scalar.activation(fbc[h % 2][:], ps[2 + h % 2][:], ACT.Copy).then_inc(f_bcs, 1)
                    if s < ns:
                        i = s % TB
                        w = (i + 1) * P if kind == "fox" else width
                        act.wait_ge(mx_done, g + 1)
                        if kind == "fox":
                            src = pr[g % 3][:, 0:w]
                        else:
                            src = ps[4 + g % 2][:, 0:w]
                            act.wait_ge(tp_done, g - 2)
                        nc.scalar.activation(pr[g % 3][:, 0:w], src, ACT.Exp, bias=nmax[:, g % 3:g % 3 + 1],
                                             accum_out=rsum[:, g % 3:g % 3 + 1]).then_inc(ex_done, 1)
                    if kind == "fox" and s == 8:
                        act.wait_ge(blk_taken, TAKEN[BLOCK0[AT["out"][0]]])
                        nc.scalar.activation(gq[:], gq[:], ACT.Silu).then_inc(h_act, 1)
                        nc.scalar.activation(gg[:], gg[:], ACT.Silu).then_inc(h_act, 1)
                        nc.scalar.activation(gk[:], gk[:], ACT.Sigmoid).then_inc(h_act, 1)
                    t = s - 2
                    if 0 <= t < ns:
                        h, i = t // TB, t % TB
                        nj = (i + 1) if kind == "fox" else width // P
                        act.wait_ge(tp_done, c["step0"] + t + 1)
                        if i == 0 and h >= 2:
                            act.wait_ge(pv_done, c["pv0"] + c["pvh"] * (h - 1))
                        nc.scalar.activation(pT[h % 2][:, 0:nj, i * P:(i + 1) * P],
                                             ps[6 + (c["step0"] + t) % 2][:, 0:nj * P].rearrange("p (j t) -> p j t", j=nj),
                                             ACT.Copy).then_inc(pt_done, 1)
                    if s >= 7 and (s - 7) % TB == 0 or s == ns + 5:
                        pass
                    for o in outputs(kind, s - 4):
                        act.wait_ge(pv_done, c["pv0"] + (o + 1 if kind == "cross" else 2 * o + 2))
                        nc.scalar.activation(uH[:, c["col0"] + o, :], ps[o % 2][:], ACT.Copy).then_inc(op_hi, 1)

            act.wait_ge(setup_d, 1)
            for tb in range(TB):
                act.wait_ge(x_in[tb], 16)
                chain(nc.scalar.activation(xdump[:], xtok[:, tb, :], ACT.Square, accum_out=msq[:, tb:tb + 1]))
            nc.scalar.activation(root, msq, ACT.Sqrt, bias=eps, scale=1.0 / D).then_inc(root_done, 1)
            high(0)
            norm_highs(Q0["mix_norm"])
            act.wait_ge(vec_cols, 2)
            nc.scalar.activation(condc, cols[:, V_C:V_C + 8], ACT.Silu).then_inc(setup, 1)
            act.wait_ge(dstep, LB_SHIFTED)
            nc.scalar.activation(lbt[:, 8:16], lbt[:, 0:8], ACT.Exp).then_inc(setup, 1)
            for n in range(*ranges("in")):
                high(n + 1)
            b = BLOCK0[AT["in"][0]] + 12
            act.wait_ge(f_z, 1)
            chain(nc.scalar.activation(frow[1][:], frow[0][:], ACT.Abs))
            chain(nc.scalar.activation(frow[1][:], frow[1][:], ACT.Exp, scale=-1.0))
            nc.scalar.activation(frow[1][:], frow[1][:], ACT.Ln, bias=ones[0:FOX_H, 0:1]).then_inc(f_l, 1)
            attention("fox")
            for h in range(HG_H):
                act.wait_ge(h_fk, h + 1)
                nc.scalar.activation(ho[:, h, :], ho[:, h, :], ACT.Ln).then_inc(h_ln, 1)
            v = 0
            for h in range(HG_H):
                for l in range(len(HG_LEVELS)):
                    act.wait_ge(h_d, v + 1)
                    chain(nc.scalar.activation(dd[v % 2][:], dd[v % 2][:], ACT.Abs))
                    nc.scalar.activation(dd[v % 2][:], dd[v % 2][:], ACT.Exp, scale=-1.0).then_inc(h_e, 1)
                    v += 1
                if h:
                    act.wait_ge(h_qb, h)
                    act.wait_ge(h_st, 3 * h)
                act.wait_ge(h_b, h + 1)
                nc.scalar.activation(eb[:], gb[:, h, :], ACT.Exp).then_inc(h_eb, 1)
                act.wait_ge(h_t, h + 1)
                nc.scalar.activation(ed[:], ed[:], ACT.Exp).then_inc(h_eb, 1)
                act.wait_ge(h_kt, h + 1)
                if h:
                    act.wait_ge(h_sp, h)
                nc.scalar.activation(kdT[:], ps[6][:, 0:384].rearrange("p (c d) -> p c d", c=3), ACT.Copy).then_inc(h_kts, 1)
            hr = [dd[0], dd[1], kt[0], kt[1]]
            act.wait_ge(h_pl, 8 * HG_H)
            act.wait_ge(h_q, 7 * HG_H)
            for h in range(HG_H):
                act.wait_ge(h_os, h + 1)
                nc.scalar.activation(hr[h][:], ho[:, h, :], ACT.Square).then_inc(h_sq, 1)
            for h in range(HG_H):
                act.wait_ge(h_sum, h + 1)
                chain(nc.scalar.activation(hr[h][:], ps[4 + h][:], ACT.Ln, bias=eps, scale=1.0 / P))
            for h in range(HG_H):
                nc.scalar.activation(hr[h][:], hr[h][:], ACT.Exp, scale=-0.5).then_inc(h_rs, 1)
            for h in range(HG_H):
                tq[0] += 1
                high_op(Q0["mix"] + 4 + h, uH[:, 4 + h, :], T[h % 2][:], (op_t, tq[0]))
            n = AT["out"][0]
            high(n + 1)
            act.wait_ge(mem_in, 32)
            for mb in range(2):
                chain(nc.scalar.activation(mdump[:], mtok[:, mb, :], ACT.Square, accum_out=mstat[:, mb:mb + 1]))
            nc.scalar.activation(mstat[:, 4:6], mstat[:, 0:2], ACT.Sqrt, bias=eps, scale=1.0 / D).then_inc(m_root, 1)
            high(n + 2)
            for half in range(2):
                high(n + 3 + half)
                for j in range(4 * half, 4 * half + 4):
                    high_op(Q0["mem"] + j, memH[:, j, :], mT[j % 2][:], (m_t, j + 1))
            b = BLOCK0[n]
            squares("x", lambda j: (blk_taken, TAKEN[b + j + 1]))
            n = AT["xkv"][0]
            high(n + 1)
            high(n + 2)
            roots("x")
            for u in range(2, 8):
                high(n + u + 1)
                if u >= 4:
                    norm_high(Q0["x_norm"], 2 * (u - 4))
                    norm_high(Q0["x_norm"], 2 * (u - 4) + 1)
            for n in range(*ranges("xq")):
                high(n + 1)
            attention("cross")
            for n in range(*ranges("xo")):
                high(n + 1)
            b = BLOCK0[AT["xo"][0]]
            squares("ff1", lambda j: (blk_taken, TAKEN[b + j + 1]))
            roots("ff1")
            norm_highs(Q0["ff1_norm"])
            n0, b0, q0 = AT["ff1"][0], AT["ff1"][1], Q0["ff1_u"]
            t0 = TAKEN[b0]
            def squared_relu(i):
                for u in range(8):
                    high(n0 + u + 1, i, 8, 16)
                    if u < 4:
                        for c in range(2):
                            act.wait_ge(blk_done, i * 16 + (b0 + 2 * u + c + 1))
                            act.wait_ge(blk_taken, i * 16 + (t0 + 2 * u + c - 1))
                            nc.scalar.activation(R[c][:], ps[(b0 + 2 * u + c) % 4][:], ACT.Relu).then_inc(relu_done, 1)
                        for c in range(2):
                            act.wait_ge(blk_taken, i * 16 + (t0 + 2 * u + c + 1))
                            nc.scalar.activation(uH[:, 2 * u + c, :], T[(q0 + c) % 2][:], ACT.Copy).then_inc(op_hi, 1)

            with act.Fori(0, 3) as i:
                squared_relu(i)
            squared_relu(3)
            squares("ev", lambda j: (blk_taken, TAKEN[AT["ff1"][1] + 64 - 8 + j + 1]),
                    lambda j: cols[:, V_FINAL + j:V_FINAL + j + 1])
            roots("ev")
            act.wait_ge(e_ms, 1)
            nc.scalar.activation(root, msq, ACT.Sqrt, bias=eps, scale=1.0).then_inc(e_root, 1)
            norm_highs(Q0["ev_norm"], lambda j: mod[:, j:j + 1])
            for n in range(*ranges("ev_in")):
                high(n + 1)
            b = TAKEN[BLOCK0[AT["ev_in"][0]]]
            act.wait_ge(blk_done, BLOCK0[AT["ev_out"][0]])
            for j in range(5):
                act.wait_ge(blk_taken, b + 4 + j + 1)
                nc.scalar.activation(gs[:, j, :], evq[:, j, :], ACT.Square).then_inc(g_sq, 1)
            for j in range(5):
                act.wait_ge(g_sum, j + 1)
                chain(nc.scalar.activation(gs[:, j, :], ps[j][:], ACT.Ln, bias=eps, scale=1.0 / 64))
            for j in range(5):
                nc.scalar.activation(gs[:, j, :], gs[:, j, :], ACT.Exp, scale=-0.5).then_inc(g_rs, 1)
            for j in range(2):
                act.wait_ge(g_dup, j + 1)
                nc.scalar.activation(kdup[:, j, :], ps[6 + j][:], ACT.Copy).then_inc(g_kd, 1)
            attention("grid")
            for j in range(4):
                tq[0] += 1
                high_op(Q0["ev_mix"] + 4 + j, uH[:, j, :], T[j % 2][:], (op_t, tq[0]))
            for n in range(*ranges("ev_out")):
                high(n + 1)

            def gated_ffn(layer):
                name = f"ff2_{layer}"
                n0, b0 = AT[name]
                q0 = Q0[name + "_u"]
                t0, s0 = TAKEN[b0], SILUS[b0]

                def pair(p, i=None):
                    last = 0 if i is not None else 1
                    n, b = n0 + 24 * last + 2 * p, b0 + 48 * last + 4 * p
                    taken = None if i is None else i * 16
                    high(n + 1, i, 12, 24)
                    for c in range(2):
                        act.wait_ge(blk_done, add(None if i is None else i * 24, b + c + 1))
                        act.wait_ge(blk_taken, add(taken, TAKEN[b] - 1 + c))
                        nc.scalar.activation(R[c][:], ps[(b + c) % 4][:], ACT.Silu).then_inc(silu_done, 1)
                    high(n + 2, i, 12, 24)
                    for c in range(2):
                        act.wait_ge(blk_taken, add(taken, TAKEN[b + 2 + c + 1]))
                        nc.scalar.activation(uH[:, 2 * p + c, :], T[(q0 + c) % 2][:], ACT.Copy).then_inc(op_hi, 1)

                with act.Fori(0, 2) as i:
                    for p in range(4):
                        pair(p, i)
                    for u in range(8, 12):
                        high(n0 + u + 1, i, 12, 24)
                for p in range(3):
                    pair(p)
                for n in range(n0 + 30, n0 + 34):
                    high(n + 1)

            def gated_norm(name, b, part, layer):
                squares(name, lambda j: (blk_taken, TAKEN[b + j + 1]))
                roots(name)
                norm_highs(Q0[name + "_norm"], lambda j: mod[:, layer * 48 + part * 8 + j:layer * 48 + part * 8 + j + 1])

            gated_norm("ff2_0", BLOCK0[AT["ev_out"][0]], 3, 0)
            gated_ffn(0)
            gated_norm("od", BLOCK0[AT["od_in"][0]] - 8, 0, 1)
            for n in range(*ranges("od_in")):
                high(n + 1)
            act.wait_ge(blk_taken, TAKEN[BLOCK0[AT["od_out"][0]]])
            nc.scalar.activation(mo[:], mo[:], ACT.Sigmoid).then_inc(o_sig, 1)
            act.wait_ge(r_sel, 1)
            chain(nc.scalar.activation(Frow[:], ps[5][0:64, :], ACT.Abs))
            chain(nc.scalar.activation(Frow[:], Frow[:], ACT.Exp, scale=-1.0))
            nc.scalar.activation(Frow[:], Frow[:], ACT.Ln, bias=ones[0:64, 0:1]).then_inc(r_ln, 1)
            for j in range(KC):
                act.wait_ge(c_y, j + 1)
                nc.scalar.activation(cy[:, j, :], cy[:, j, :], ACT.Silu).then_inc(c_silu, 1)
            act.wait_ge(r_rows, 1)
            nc.scalar.activation(erow[:], erow[:], ACT.Exp, scale=-1.0).then_inc(r_em, 1)
            act.wait_ge(r_tr, 2)
            nc.scalar.activation(ccol[:], ps[6][:, 0:256].rearrange("p (a b) -> p a b", a=TB), ACT.Copy).then_inc(r_cols, 1)
            nc.scalar.activation(ecol[:], ps[7][:, 0:256].rearrange("p (a b) -> p a b", a=TB), ACT.Copy).then_inc(r_cols, 1)
            act.wait_ge(r_cols, 2)
            for h in range(ML_H):
                for d in range(2):
                    for j in range(TB):
                        r = 8 * h + 4 * d + j
                        lo, hi = (j * P, S) if d == 0 else (0, (j + 1) * P)
                        act.wait_ge(l_bc, 2 * h + d + 1)
                        if r >= 2:
                            act.wait_ge(l_a, r - 1)
                        row = h + 32 * d
                        nc.scalar.activation(wt[r % 2][:, lo:hi], ps[4 + d][:, lo:hi], ACT.Exp,
                                             bias=ccol[:, j, row:row + 1]).then_inc(l_w, 1)
            act.wait_ge(l_h, 16)
            nc.scalar.activation(hsq[:], hs[:], ACT.Square).then_inc(n_sq, 1)
            act.wait_ge(n_sum, 1)
            chain(nc.scalar.activation(hrs, hstat, ACT.Ln, bias=eps, scale=1.0 / ML_V))
            nc.scalar.activation(hrs, hrs, ACT.Exp, scale=-0.5).then_inc(n_rs, 1)
            for j in range(KC):
                high_op(Q0["od_mix"] + j, uH[:, j, :], ps[4 + j % 4][:], (n_tr, j + 1))
            for n in range(*ranges("od_out")):
                high(n + 1)
            gated_norm("ff2_1", BLOCK0[AT["od_out"][0]], 3, 1)
            gated_ffn(1)

        @block.vector
        def _(dve):
            steps = [0]

            def chain(ins):
                steps[0] += 1
                ins.then_inc(dstep, 1)
                dve.wait_ge(dstep, steps[0])

            def norm_add(name, j, twice=False):
                for g in range(2 if twice else 1):
                    q = SQ0[name] + (2 * j + g if twice else j)
                    acc = (ssum, gsum)[g]
                    if j == 0 and g == 0:
                        dve.wait_ge(sum_done, NORMS[name] - 1)
                    dve.wait_ge(sq_done, q + 1)
                    if j == 0:
                        nc.vector.tensor_copy(acc[:], sq[q % 2][:]).then_inc(sq_added, 1)
                    else:
                        dve.wait_ge(sq_added, q)
                        nc.vector.tensor_tensor(acc[:], acc[:], sq[q % 2][:], ALU.add).then_inc(sq_added, 1)

            def residual_and_sums(b, name, gate=None, twice=False):
                for j in range(KC):
                    residual(b + j, j, gate)
                    if j == 5:
                        for jj in range(6):
                            norm_add(name, jj, twice)
                    elif j > 5:
                        norm_add(name, j, twice)

            def inverse_root(name):
                dve.wait_ge(root_done, NORMS[name] + 1)
                if NORMS[name]:
                    dve.wait_ge(bc_done, NORMS[name])
                nc.vector.reciprocal(rootinv, root).then_inc(inv_done, 1)

            def low_op(q, dstL, src, dstH, bias=None):
                dve.wait_ge(op_hi, q + 1)
                if bias is None:
                    nc.vector.tensor_tensor(dstL, src, dstH.bitcast(F32), ALU.subtract).then_inc(op_lo, 1)
                else:
                    nc.vector.scalar_tensor_tensor(out=dstL, in0=src, scalar=bias, in1=dstH.bitcast(F32),
                                                   op0=ALU.add, op1=ALU.subtract).then_inc(op_lo, 1)

            def normed_steps(name, gain, q0, shift=None, bank=4):
                dve.wait_ge(bc_done, NORMS[name] + 1)

                def low(j):
                    low_op(q0 + j, hnL[:, j, :], T[(q0 + j) % 2][:], hnH[:, j, :], None if shift is None else shift(j))

                for j in range(KC):
                    if q0 + j >= 2:
                        dve.wait_ge(op_lo, q0 + j - 1)
                    ins = nc.vector.scalar_tensor_tensor(out=T[(q0 + j) % 2][:], in0=xT[:, j, :], scalar=gain(j), in1=ps[bank][:],
                                                         op0=ALU.mult, op1=ALU.mult)
                    ins.then_inc(op_t, 1)
                    if j:
                        low(j - 1)
                    if j % 2:
                        yield
                low(KC - 1)
                yield

            def normed(name, gain, q0, shift=None, bank=4):
                inverse_root(name)
                for _ in normed_steps(name, gain, q0, shift, bank):
                    pass

            def col(c0):
                return lambda j: cols[:, c0 + j:c0 + j + 1]

            def take(b, out_ap, in_ap, scale=None):
                dve.wait_ge(blk_done, b + 1)
                if scale is None:
                    nc.vector.tensor_copy(out_ap, in_ap).then_inc(blk_taken, 1)
                else:
                    nc.vector.tensor_scalar(out_ap, in_ap, scale, None, ALU.mult).then_inc(blk_taken, 1)

            def residual(b, j, gate=None, value=None):
                dve.wait_ge(blk_done, (b if value is None else value) + 1)
                if gate is None:
                    nc.vector.tensor_tensor(xT[:, j, :], ps[b % 4][:], xT[:, j, :], ALU.add).then_inc(blk_taken, 1)
                else:
                    nc.vector.scalar_tensor_tensor(out=xT[:, j, :], in0=ps[b % 4][:], scalar=gate(j), in1=xT[:, j, :],
                                                   op0=ALU.mult, op1=ALU.add).then_inc(blk_taken, 1)

            def attention(kind):
                c = ATT[kind]
                ns = c["heads"] * TB
                width = {"fox": None, "cross": M_MEM, "grid": S}[kind]
                for s in range(ns + 7):
                    g = c["step0"] + s
                    if s < ns:
                        h, i = s // TB, s % TB
                        m = g % 3
                        dve.wait_ge(sc_done, g + 1)
                        if kind == "fox":
                            w = (i + 1) * P
                            if g >= 3:
                                dve.wait_ge(tp_done, g - 2)
                            dve.wait_ge(f_bcs, h + 1)
                            chain(nc.vector.tensor_tensor_reduce(pr[m][:, 0:w], ps[4 + g % 2][:, 0:w], fbc[h % 2][:, 0:w], 1.0, -3.0e38,
                                                                 ALU.subtract, ALU.max, nmraw[:, m:m + 1]))
                        else:
                            chain(nc.vector.tensor_reduce(nmraw[:, m:m + 1], ps[4 + g % 2][:, 0:width], AX, ALU.max))
                        nc.vector.tensor_scalar(nmax[:, m:m + 1], nmraw[:, m:m + 1], -1.0, None, ALU.mult).then_inc(mx_done, 1)
                    if 1 <= s <= ns:
                        m = (g - 1) % 3
                        w = ((s - 1) % TB + 1) * P if kind == "fox" else width
                        dve.wait_ge(ex_done, g)
                        chain(nc.vector.reciprocal(rinv[:, m:m + 1], rsum[:, m:m + 1]))
                        nc.vector.tensor_scalar(pr[m][:, 0:w], pr[m][:, 0:w], rinv[:, m:m + 1], None, ALU.mult).then_inc(pn_done, 1)
                    for o in outputs(kind, s - 5):
                        low_op(c["q0"] + o, uL[:, c["col0"] + o, :], ps[o % 2][:], uH[:, c["col0"] + o, :])

            nc.vector.memset(eps, EPS).then_inc(setup_d, 1)
            dve.wait_ge(cst_in, 16)
            nc.vector.tensor_copy(identb[:], ident).then_inc(setup_d, 1)
            nc.vector.tensor_copy(causalb[:], cst[:, C_CAUSAL, :]).then_inc(setup_d, 1)
            for j in range(KC):
                dve.wait_ge(x_tr, j + 1)
                nc.vector.tensor_copy(xT[:, j, :], ps[6 + j % 2][:]).then_inc(x_cols, 1)
            dve.wait_ge(vec_tr, 2)
            nc.vector.tensor_copy(cols[:, 0:V_ROWS], ps[5][:, 0:V_ROWS]).then_inc(vec_cols, 1)
            nc.vector.tensor_copy(adab[:], ps[5][:, 128:224]).then_inc(vec_cols, 1)
            dve.wait_ge(vec_cols, 2)
            dve.wait_ge(x_cols, KC)
            normed("mix", col(V_MIX), Q0["mix_norm"])
            dve.sem_inc(ada_acc, ADA_RING)
            dve.sem_inc(mod_done, 1)
            l0, l1 = cols[:, V_LB:V_LB + 4], cols[:, V_LB + 4:V_LB + 8]
            chain(nc.vector.tensor_tensor(lbt[:, 8:12], l0, l1, ALU.max))
            chain(nc.vector.tensor_tensor(lbt[:, 0:4], l0, lbt[:, 8:12], ALU.subtract))
            chain(nc.vector.tensor_tensor(lbt[:, 4:8], l1, lbt[:, 8:12], ALU.subtract))
            assert steps[0] == LB_SHIFTED
            dve.wait_ge(setup, 2)
            chain(nc.vector.tensor_tensor(lbt[:, 0:4], lbt[:, 8:12], lbt[:, 12:16], ALU.add))
            chain(nc.vector.reciprocal(lbt[:, 4:8], lbt[:, 0:4]))
            chain(nc.vector.tensor_tensor(lb, lbt[:, 8:12], lbt[:, 4:8], ALU.mult))
            chain(nc.vector.tensor_scalar(omlb, lb, -1.0, 1.0, ALU.mult, ALU.add))
            chain(nc.vector.tensor_scalar(small[:, 148:149], cols[:, V_QG:V_QG + 1], GA_SCALE, None, ALU.mult))

            n, b = AT["in"]
            for j in range(4):
                take(b + j, fq[:, j, :], ps[(b + j) % 4][:], FOX_D ** -0.5)
            for j in range(4):
                take(b + 4 + j, fk[:, j, :], ps[(b + 4 + j) % 4][:])

            def take_tokens(b, dst, c0, width=UC):
                for half in range(2):
                    take(b + half, dst[:, 2 * half:2 * half + 2, c0:c0 + width],
                         ps[(b + half) % 4][:, 0:2 * width].rearrange("p (a c) -> p a c", a=2))

            for u in range(2):
                take_tokens(b + 8 + 2 * u, fv, u * UC)
            fb = b + 12
            dve.wait_ge(blk_done, fb + 1)
            nc.vector.tensor_scalar(fz[:], ps[fb % 4][0:FOX_H, :], fbias[0:FOX_H, :], None, ALU.add).then_inc(blk_taken, 1)
            for j in range(4):
                take(fb + 1 + j, gq[:, j, :], ps[(fb + 1 + j) % 4][:])
            for j in range(4):
                take(fb + 5 + j, gk[:, j, :], ps[(fb + 5 + j) % 4][:])
            for u in range(2):
                take_tokens(fb + 9 + 2 * u, gi, u * UC)
            for j in range(4):
                take(fb + 13 + j, gg[:, j, :], ps[(fb + 13 + j) % 4][:])
            dve.wait_ge(blk_taken, TAKEN[fb + 1])
            nc.vector.tensor_copy(frow[0][:], fz[:]).then_inc(f_z, 1)
            dve.wait_ge(f_z, 1)
            dve.wait_ge(f_l, 1)
            chain(nc.vector.tensor_scalar(frow[2][:], frow[0][:], 0.0, None, ALU.min))
            chain(nc.vector.tensor_tensor(frow[2][:], frow[2][:], frow[1][:], ALU.subtract))
            nc.vector.tensor_tensor_scan(frow[0][:], ones[0:FOX_H, 0:1].to_broadcast([FOX_H, S]), frow[2][:], 0.0,
                                         ALU.mult, ALU.add).then_inc(f_rows, 1)
            attention("fox")
            nc.vector.memset(rmask[:], 1.0).then_inc(dstep, 1)
            steps[0] += 1
            dve.wait_ge(dstep, steps[0])
            chain(nc.vector.memset(rmask[:].rearrange("p (c t) -> p c t", c=TB)[:, :, 0:1], 0.0))
            for i in range(2):
                chain(nc.vector.memset(at_[i][:], 0.0))
            dve.wait_ge(h_act, 3)
            for h in range(HG_H):
                chain(nc.vector.tensor_scalar(ho[:, h, :], gk[:, h, :], omlb[:, h:h + 1], lb[:, h:h + 1], ALU.mult, ALU.add))
                nc.vector.tensor_scalar(gk[:, h, :], ho[:, h, :], -1.0, 1.0, ALU.mult, ALU.add).then_inc(h_fk, 1)
            for h in range(HG_H):
                dve.wait_ge(h_ln, h + 1)
                nc.vector.tensor_tensor_scan(gb[:, h, :], rmask[:], ho[:, h, :], 0.0, ALU.mult, ALU.add).then_inc(h_b, 1)
            levels = [(h, l) for h in range(HG_H) for l in range(len(HG_LEVELS))]

            def level_exponent(v):
                h, l = levels[v]
                L = HG_LEVELS[l]
                if v >= 2:
                    dve.wait_ge(h_q, v - 1)
                    dve.wait_ge(h_k, v - 1)
                dve.wait_ge(h_b, h + 1)
                x = gb[:, h, :].rearrange("p (n t) -> p n t", t=2 * L)
                nc.vector.tensor_tensor(dd[v % 2][:].rearrange("p (n t) -> p n t", t=2 * L), x,
                                        x[:, :, L - 1:L].to_broadcast([P, S // (2 * L), 2 * L]), ALU.subtract).then_inc(h_d, 1)

            def level_q(v):
                h, l = levels[v]
                dve.wait_ge(h_e, v + 1)
                if v >= 2:
                    dve.wait_ge(h_pl, 8 * levels[v - 2][0] + levels[v - 2][1] + 1)
                nc.vector.tensor_tensor(qt[v % 2][:], gq[:, h, :], dd[v % 2][:], ALU.mult).then_inc(h_q, 1)

            def level_scores(e):
                h, l = e // 8, e % 8
                dve.wait_ge(h_pl, e + 1)
                if e:
                    dve.wait_ge(h_at, e)
                if l == 0 and h >= 2:
                    dve.wait_ge(h_o, h - 1)
                nc.vector.copy_predicated(at_[h % 2][:],
                                          lvl[:, l, :].bitcast(U32).rearrange("p (a c) -> p a c", a=1).to_broadcast([P, TB, P]),
                                          ps[4 + e % 2][:].rearrange("p (c t) -> p c t", c=TB)).then_inc(h_at, 1)

            dve.wait_ge(lvl_in, 16)
            level_exponent(0)
            v = 0
            for h in range(HG_H):
                for l in range(len(HG_LEVELS)):
                    if v + 1 < len(levels):
                        level_exponent(v + 1)
                    level_q(v)
                    if l:
                        level_scores(8 * h + l - 1)
                    v += 1
                if h:
                    dve.wait_ge(h_kd, h)
                x = gb[:, h, :].rearrange("p (c t) -> p c t", c=TB)
                nc.vector.tensor_tensor(ed[:].rearrange("p (c t) -> p c t", c=TB), x[:, :, P - 1:P].to_broadcast([P, TB, P]), x,
                                        ALU.subtract).then_inc(h_t, 1)
                level_scores(8 * h + 6)
                level_scores(8 * h + 7)
                if h:
                    dve.wait_ge(h_o, h)
                dve.wait_ge(h_eb, 2 * h + 1)
                nc.vector.tensor_tensor(qb[:], gq[:, h, :], eb[:], ALU.mult).then_inc(h_qb, 1)
                dve.wait_ge(h_sp, h + 1)
                for c in range(3):
                    part = ps[7][:, c * P:(c + 1) * P]
                    if c == 0:
                        nc.vector.tensor_copy(st[:, 0, :], part).then_inc(h_st, 1)
                    else:
                        dve.wait_ge(h_st, 3 * h + c)
                        nc.vector.scalar_tensor_tensor(out=st[:, c, :], in0=st[:, c - 1, :], scalar=eb[:, c * P + P - 1:c * P + P],
                                                       in1=part, op0=ALU.mult, op1=ALU.add).then_inc(h_st, 1)
                dve.wait_ge(h_o, h + 1)
                nc.vector.tensor_copy(ho[:, h, :], ps[h % 2][:]).then_inc(h_os, 1)
            hr = [dd[0], dd[1], kt[0], kt[1]]
            for h in range(HG_H):
                dve.wait_ge(h_rs, h + 1)
                chain(nc.vector.scalar_tensor_tensor(out=ho[:, h, :], in0=ho[:, h, :], scalar=cols[:, V_HG:V_HG + 1], in1=hr[h][:],
                                                     op0=ALU.mult, op1=ALU.mult))
                nc.vector.tensor_tensor(T[h % 2][:], ho[:, h, :], gg[:, h, :], ALU.mult).then_inc(op_t, 1)
                low_op(Q0["mix"] + 4 + h, uL[:, 4 + h, :], T[h % 2][:], uH[:, 4 + h, :])
            n, b = AT["out"]

            def memory_chunk(j):
                dve.wait_ge(m_tr, j + 1)
                if j >= 2:
                    dve.wait_ge(op_lo, Q0["mem"] + j - 1)
                nc.vector.tensor_scalar(mT[j % 2][:], ps[4 + j % 4][:, 0:M_MEM], cols[:, V_MEM + j:V_MEM + j + 1], None,
                                        ALU.mult).then_inc(m_t, 1)
                low_op(Q0["mem"] + j, memL[:, j, :], mT[j % 2][:], memH[:, j, :])

            for j in range(KC):
                residual(b + j, j)
                if j == 1:
                    dve.wait_ge(m_root, 1)
                    chain(nc.vector.reciprocal(mstat[:, 2:4], mstat[:, 4:6]))
                    for mb in range(2):
                        nc.vector.tensor_scalar(mtok[:, mb, :], mtok[:, mb, :], mstat[:, 2 + mb:3 + mb], None, ALU.mult).then_inc(m_n, 1)
                if j in (3, 5):
                    for jj in range(2 * j - 6, 2 * j - 2):
                        memory_chunk(jj)
                if j == 5:
                    for jj in range(6):
                        norm_add("x", jj)
                elif j > 5:
                    norm_add("x", j)
            n, b = AT["xkv"]
            steps_x = normed_steps("x", col(V_X), Q0["x_norm"])
            for u in range(8):
                for c in range(2):
                    bb = b + 2 * u + c
                    if u < 4:
                        take(bb, xk[:, 2 * u + c, :], ps[bb % 4][:, 0:M_MEM])
                    else:
                        take(bb, xv[:, c, (u - 4) * UC:(u - 3) * UC], ps[bb % 4][:, 0:UC])
                if u == 1:
                    inverse_root("x")
                if u >= 3:
                    next(steps_x)
            n, b = AT["xq"]
            for j in range(KC):
                take(b + j, xq[:, j, :], ps[(b + j) % 4][:], 1.0 / 16)
            attention("cross")
            n, b = AT["xo"]
            residual_and_sums(b, "ff1")
            normed("ff1", col(V_FF), Q0["ff1_norm"])
            n0, b0 = AT["ff1"]
            q0 = Q0["ff1_u"]
            dve.wait_ge(setup, 1)
            def conditioning(layer, i, m):
                group = ADA_GROUP[layer]
                acc = adacc[m % 2][:]
                dve.wait_ge(ada_in[m % ADA_RING], i * (16 * group // ADA_RING) + 16 * (24 * layer // ADA_RING + m // ADA_RING + 1))
                dve.wait_ge(ada_mm, i * group + (24 * layer + m + 1))
                for k in range(KC):
                    if k == 0:
                        ins = nc.vector.tensor_scalar(acc, adaw[m % ADA_RING][:, 0, :], condc[:, 0:1], None, ALU.mult)
                    else:
                        dve.wait_ge(ada_step, i * (7 * group) + (7 * (24 * layer + m) + k))
                        ins = nc.vector.scalar_tensor_tensor(out=acc, in0=adaw[m % ADA_RING][:, k, :], scalar=condc[:, k:k + 1],
                                                             in1=acc, op0=ALU.mult, op1=ALU.add)
                    ins.then_inc(ada_acc if k == KC - 1 else ada_step, 1)

            def modulations(layer, i):
                n = 2 * ADA_GROUP[layer]
                dve.wait_ge(ada_mm, i * (n // 2) + (24 * layer + n // 2 + 2))
                at = bass.ds(i * n + 48 * layer, n)
                nc.vector.tensor_tensor(mod[:, at], ps[5][:, 0:n], adab[:, at], ALU.add).then_inc(mod_done, 1)

            def plus_one(layer):
                done = (4, 7)[layer]
                dve.wait_ge(mod_done, done)
                half = slice(48 * layer, 48 * layer + 48)
                nc.vector.tensor_scalar(modp[:, half], mod[:, half], 1.0, None, ALU.add).then_inc(mod_done, 1)
                dve.wait_ge(mod_done, done + 1)

            def hidden(u, i):
                for c in range(2):
                    b, q = b0 + 2 * u + c, q0 + 2 * u + c
                    dve.wait_ge(relu_done, i * 8 + (2 * u + c + 1))
                    dve.wait_ge(op_lo, i * 8 + (q - 1))
                    nc.vector.scalar_tensor_tensor(out=T[q % 2][:], in0=ps[b % 4][:], scalar=0.0, in1=R[c][:],
                                                   op0=ALU.max, op1=ALU.mult).then_inc(blk_taken, 1)
                for c in range(2):
                    q = q0 + 2 * u + c
                    dve.wait_ge(op_hi, i * 8 + (q + 1))
                    nc.vector.tensor_tensor(uL[:, 2 * u + c, :], T[q % 2][:], uH[:, 2 * u + c, :].bitcast(F32),
                                            ALU.subtract).then_inc(op_lo, 1)

            with dve.Fori(0, 3) as i:
                for u in range(8):
                    conditioning(0, i, u)
                    if u < 4:
                        hidden(u, i)
                    else:
                        for c in range(2):
                            b = b0 + 2 * u + c
                            residual(b, 2 * (u - 4) + c, None, i * 16 + b)
                modulations(0, i)
            plus_one(0)
            chain(nc.vector.tensor_tensor(gm, modp[:, 8:16], cols[:, V_FINAL:V_FINAL + 8], ALU.mult))
            for u in range(4):
                hidden(u, 3)
            residual_and_sums(b0 + 56, "ev", None, True)

            def mcol(t, layer, part):
                return lambda j: t[:, layer * 48 + part * 8 + j:layer * 48 + part * 8 + j + 1]

            inverse_root("ev")
            dve.wait_ge(inv_done, NORMS["ev"] + 1)
            chain(nc.vector.tensor_tensor(msq, rootinv, rootinv, ALU.mult))
            nc.vector.scalar_tensor_tensor(out=msq, in0=ps[6][:, 4:8], scalar=1.0 / D, in1=msq, op0=ALU.mult,
                                           op1=ALU.mult).then_inc(e_ms, 1)
            dve.wait_ge(e_root, 1)
            chain(nc.vector.reciprocal(msq, root))
            nc.vector.tensor_tensor(msq, msq, rootinv, ALU.mult).then_inc(e_inv, 1)
            for _ in normed_steps("ev", lambda j: gm[:, j:j + 1], Q0["ev_norm"], mcol(mod, 0, 0), 5):
                pass
            for j in range(KC):
                nc.vector.scalar_tensor_tensor(out=xT[:, j, :], in0=xT[:, j, :], scalar=cols[:, V_FINAL + j:V_FINAL + j + 1],
                                               in1=ps[4][:], op0=ALU.mult, op1=ALU.mult).then_inc(dstep, 1)
                steps[0] += 1
            dve.wait_ge(dstep, steps[0])
            chain(nc.vector.memset(pu[:, :, 0:8], 0.0))
            chain(nc.vector.memset(pu[:, :, 8 + S:S + 24], 0.0))
            n, b = AT["ev_in"]
            for j in range(4):
                take(b + j, pu[:, j, 8:8 + S], ps[(b + j) % 4][:])
            for j in range(5):
                take(b + 4 + j, evq[:, j, :], ps[(b + 4 + j) % 4][:])
            take(b + 9, evv[:], ps[(b + 9) % 4][:].rearrange("p (a c) -> p a c", a=TB))
            dve.wait_ge(ev_in, 64)
            for j in range(5):
                dve.wait_ge(g_rs, j + 1)
                gain = small[:, 148:149] if j < 4 else cols[:, V_KG:V_KG + 1]
                nc.vector.scalar_tensor_tensor(out=evq[:, j, :], in0=evq[:, j, :], scalar=gain, in1=gs[:, j, :],
                                               op0=ALU.mult, op1=ALU.mult).then_inc(g_n, 1)
            for j in range(5):
                dve.wait_ge(g_rot, j + 1)
                chain(nc.vector.tensor_tensor(T[j % 2][:], ps[4 + j % 2][:], sinb[:], ALU.mult))
                chain(nc.vector.tensor_tensor(evq[:, j, :], evq[:, j, :], cosb[:], ALU.mult))
                nc.vector.tensor_tensor(evq[:, j, :], evq[:, j, :], T[j % 2][:], ALU.add).then_inc(g_roped, 1)
            attention("grid")
            for j in range(4):
                dve.wait_ge(p_mm, j + 1)
                nc.vector.tensor_scalar(T[j % 2][:], ps[2 + j % 2][:], cols[:, V_BPOOL + j:V_BPOOL + j + 1],
                                        cols[:, V_SPOOL + j:V_SPOOL + j + 1], ALU.add, ALU.mult).then_inc(op_t, 1)
                low_op(Q0["ev_mix"] + 4 + j, uL[:, j, :], T[j % 2][:], uH[:, j, :])
            n, b = AT["ev_out"]
            residual_and_sums(b, "ff2_0", mcol(mod, 0, 2))

            def gated_ffn(layer):
                name = f"ff2_{layer}"
                n0, b0 = AT[name]
                q0 = Q0[name + "_u"]

                def pair(p, i=None):
                    last = 0 if i is not None else 1
                    blocks, chunks = (None, None) if i is None else (i * 24, i * 8)
                    for c in range(2):
                        b, q = b0 + 48 * last + 4 * p + 2 + c, q0 + 16 * last + 2 * p + c
                        dve.wait_ge(silu_done, add(chunks, SILUS[b - 2] + 1))
                        dve.wait_ge(blk_done, add(blocks, b + 1))
                        dve.wait_ge(op_lo, add(chunks, q - 1))
                        nc.vector.tensor_tensor(T[(q0 + c) % 2][:], ps[b % 4][:], R[c][:], ALU.mult).then_inc(blk_taken, 1)
                    for c in range(2):
                        q = q0 + 16 * last + 2 * p + c
                        dve.wait_ge(op_hi, add(chunks, q + 1))
                        nc.vector.tensor_tensor(uL[:, 2 * p + c, :], T[(q0 + c) % 2][:], uH[:, 2 * p + c, :].bitcast(F32),
                                                ALU.subtract).then_inc(op_lo, 1)

                def cond(i, m):
                    if layer == 0:
                        conditioning(1, i, m)

                with dve.Fori(0, 2) as i:
                    for p in range(4):
                        cond(i, 2 * p)
                        cond(i, 2 * p + 1)
                        pair(p, i)
                    for j in range(KC):
                        if j % 2 == 0:
                            cond(i, 8 + j // 2)
                        residual(b0 + 16 + j, j, mcol(mod, layer, 5), i * 24 + (b0 + 16 + j))
                    if layer == 0:
                        modulations(1, i)
                if layer == 0:
                    plus_one(1)
                for p in range(3):
                    pair(p)
                if layer == 0:
                    residual_and_sums(b0 + 60, "od", mcol(mod, layer, 5))
                else:
                    for j in range(KC):
                        residual(b0 + 60 + j, j, mcol(mod, layer, 5))

            def gated_norm(name, part, layer):
                normed(name, mcol(modp, layer, part + 1), Q0[name + "_norm"], mcol(mod, layer, part))

            gated_norm("ff2_0", 3, 0)
            gated_ffn(0)
            gated_norm("od", 0, 1)
            chain(nc.vector.memset(cz[:, :, 0:2], 0.0))
            chain(nc.vector.memset(cz[:, :, 2 + S:4 + S], 0.0))
            chain(nc.vector.memset(vx[:, :, :, ML_V:ML_V + 1], 1.0))
            n, b = AT["od_in"]
            for j in range(KC):
                take(b + j, cz[:, j, 2:2 + S], ps[(b + j) % 4][:])
            for u in range(4):
                for half in range(2):
                    bb = b + 8 + 2 * u + half
                    dve.wait_ge(blk_done, bb + 1)
                    for tb in range(2):
                        src = ps[bb % 4][:, tb * UC:(tb + 1) * UC].rearrange("p (h v) -> p h v", h=2)
                        ins = nc.vector.tensor_copy(vx[:, 2 * half + tb, 2 * u:2 * u + 2, 0:ML_V], src)
                    ins.then_inc(blk_taken, 1)
            for u in range(4):
                take_tokens(b + 16 + 2 * u, mo, u * UC)
            gb_ = b + 24
            dve.wait_ge(blk_done, gb_ + 1)
            dve.wait_ge(op_lo, Q0["od_norm"] + 8)
            nc.vector.tensor_scalar(grow[96:128, :], ps[gb_ % 4][96:128, :], gbias[96:128, :], None, ALU.add).then_inc(blk_taken, 1)
            dve.wait_ge(r_sel, 1)
            chain(nc.vector.tensor_copy(irow[:], ps[4][0:64, :]))
            dve.wait_ge(r_ln, 1)
            chain(nc.vector.tensor_scalar(lrow[:], ps[5][0:64, :], 0.0, None, ALU.min))
            chain(nc.vector.tensor_tensor(lrow[:], lrow[:], Frow[:], ALU.subtract))
            chain(nc.vector.memset(Mrow[:], 0.0))
            one8 = [ones[32 * d:32 * d + 8, 0:1].to_broadcast([8, S]) for d in range(2)]
            chain(nc.vector.tensor_tensor_scan(Frow[0:8, :], one8[0], lrow[0:8, :], 0.0, ALU.mult, ALU.add))
            chain(nc.vector.tensor_tensor_scan(Frow[32:40, ::-1], one8[1], lrow[32:40, ::-1], 0.0, ALU.mult, ALU.add))
            chain(nc.vector.tensor_tensor(irow[:], irow[:], Frow[:], ALU.subtract))
            chain(nc.vector.tensor_tensor_scan(Mrow[0:8, :], irow[0:8, :], irow[0:8, :], 0.0, ALU.max, ALU.max))
            chain(nc.vector.tensor_tensor_scan(Mrow[32:40, ::-1], irow[32:40, ::-1], irow[32:40, ::-1], 0.0, ALU.max, ALU.max))
            nc.vector.tensor_tensor(erow[:], Frow[:], Mrow[:], ALU.add).then_inc(r_rows, 1)
            dve.wait_ge(r_rows, 1)
            nc.vector.tensor_scalar(Mrow[:], Mrow[:], -1.0, None, ALU.mult).then_inc(r_rows, 1)
            for j in range(KC):
                for k in range(CONV_K):
                    tap = cols[:, V_CW + 8 * k + j:V_CW + 8 * k + j + 1]
                    src = cz[:, j, k:k + S]
                    if k == 0:
                        chain(nc.vector.tensor_scalar(cy[:, j, :], src, tap, cols[:, V_CB + j:V_CB + j + 1], ALU.mult, ALU.add))
                    else:
                        ins = nc.vector.scalar_tensor_tensor(out=cy[:, j, :], in0=src, scalar=tap, in1=cy[:, j, :],
                                                             op0=ALU.mult, op1=ALU.add)
                        if k < CONV_K - 1:
                            chain(ins)
                        else:
                            ins.then_inc(c_y, 1)
            dve.wait_ge(c_y, KC)

            def decayed(r):
                h, d, j = r // 8, r // 4 % 2, r % 4
                lo, hi = (j * P, S) if d == 0 else (0, (j + 1) * P)
                dve.wait_ge(l_wm, r + 1)
                dve.wait_ge(l_qk, 4 * h + j + 1)
                if h:
                    dve.wait_ge(l_o, 2 * h - 2 + d + 1)
                nc.vector.scalar_tensor_tensor(out=ma[d][:, j, lo:hi], in0=ps[j][:, lo:hi], scalar=FOX_D ** -0.5,
                                               in1=wt[r % 2][:, lo:hi], op0=ALU.mult, op1=ALU.mult).then_inc(l_a, 1)

            def heads_out(h, d):
                dve.wait_ge(l_o, 2 * h + d + 1)
                row = h + 32 * d
                for p in range(2):
                    den = ps[6 + p][:, 0:258].rearrange("p (a c) -> p a c", a=2)[:, :, ML_V]
                    chain(nc.vector.scalar_tensor_tensor(out=mden[:, 2 * p:2 * p + 2], in0=den, scalar=-1.0,
                                                         in1=ecol[:, 2 * p:2 * p + 2, row], op0=ALU.mult, op1=ALU.max))
                    chain(nc.vector.tensor_tensor(mden[:, 2 * p:2 * p + 2], den, mden[:, 2 * p:2 * p + 2], ALU.max))
                chain(nc.vector.reciprocal(mden[:, 4:8], mden[:, 0:4]))
                for i in range(TB):
                    num = ps[6 + i // 2][:, (i % 2) * 129:(i % 2) * 129 + ML_V]
                    dst = hs[:, i, h * P:(h + 1) * P]
                    if d == 0:
                        ins = nc.vector.tensor_scalar(dst, num, mden[:, 4 + i:5 + i], None, ALU.mult)
                    else:
                        ins = nc.vector.scalar_tensor_tensor(out=dst, in0=num, scalar=mden[:, 4 + i:5 + i], in1=dst,
                                                             op0=ALU.mult, op1=ALU.add)
                ins.then_inc(l_h, 1)
                dve.wait_ge(l_h, 2 * h + d + 1)

            for h in range(ML_H):
                for d in range(2):
                    for j in range(TB):
                        decayed(8 * h + 4 * d + j)
                    if d == 0 and h:
                        heads_out(h - 1, 1)
                    if d == 1:
                        heads_out(h, 0)
            heads_out(ML_H - 1, 1)
            dve.wait_ge(n_sq, 1)
            nc.vector.tensor_reduce(hstat, hsq[:].rearrange("p t (h v) -> p (t h) v", v=ML_V), AX, ALU.add).then_inc(n_sum, 1)
            dve.wait_ge(n_rs, 1)
            dve.wait_ge(gstep, POOL_STEPS + TB)
            for tb in range(TB):
                x = hs[:, tb, :].rearrange("p (h v) -> p h v", v=ML_V)
                chain(nc.vector.tensor_tensor(x, x, hrs[:, 8 * tb:8 * tb + 8].rearrange("p (h o) -> p h o", o=1)
                                              .to_broadcast([P, ML_H, ML_V]), ALU.mult))
                nc.vector.tensor_tensor(hs[:, tb, :], hs[:, tb, :], mo[:, tb, :], ALU.mult).then_inc(n_h, 1)
            for j in range(KC):
                low_op(Q0["od_mix"] + j, uL[:, j, :], ps[4 + j % 4][:], uH[:, j, :])
            n, b = AT["od_out"]
            residual_and_sums(b, "ff2_1", mcol(mod, 1, 2))
            gated_norm("ff2_1", 3, 1)
            gated_ffn(1)
            for o in range(2 * TB):
                tb, half = o // 2, o % 2
                dve.wait_ge(o_tr, o + 1)
                nc.vector.tensor_copy(otok[:, tb, half * 512:(half + 1) * 512], ps[4 + o % 4][:]).then_inc(o_cp, 1)

        @block.tensor
        def _(pe):
            def bank_free(b, taken=None, silus=None):
                if b < 4:
                    return
                if BY_ACT[b - 4]:
                    pe.wait_ge(silu_done, add(silus, SILUS[b - 3]))
                else:
                    pe.wait_ge(blk_taken, add(taken, TAKEN[b - 3]))

            def parts(out_ap, wa, xa, first, last):
                (wh, wl), (xh, xl) = wa, xa
                nc.tensor.matmul(out_ap, wh, xh, start=first, stop=False)
                nc.tensor.matmul(out_ap, wh, xl, start=False, stop=False)
                return nc.tensor.matmul(out_ap, wl, xh, start=False, stop=last)

            def unit_ready(n, units=None):
                pe.wait_ge(w_hi, add(units, n + 1))
                pe.wait_ge(w_lo, add(units, n + 1))

            def feature_unit(n, xh, xl, tokens=S, need=None, i=None, du=0, dt=0, ds=0):
                units, taken, silus = (None,) * 3 if i is None else (i * du, i * dt, i * ds)
                unit_ready(n, units)
                kc = UNITS[n][2]
                blocks = range(UNITS[n][5])

                def chunk(c, k):
                    cs = slice(c * P, (c + 1) * P)
                    ins = parts(ps[(BLOCK0[n] + c) % 4][:, 0:tokens], (wH[n % 2][:, k, cs], wL[n % 2][:, k, cs]),
                                (xh[:, k, :], xl[:, k, :]), k == 0, k == kc - 1)
                    if k == kc - 1:
                        ins.then_inc(blk_done, 1)

                if need is None:
                    for c in blocks:
                        bank_free(BLOCK0[n] + c, taken, silus)
                        for k in range(kc):
                            chunk(c, k)
                else:
                    for c in blocks:
                        bank_free(BLOCK0[n] + c, taken, silus)
                    for k in range(kc):
                        pe.wait_ge(op_lo, need(k))
                        for c in blocks:
                            chunk(c, k)

            def token_block(n, b, tbs, xh, xl, c0=0, width=UC):
                bank_free(b)
                for pos, tb in enumerate(tbs):
                    for k in range(KC):
                        ts = slice(tb * P, (tb + 1) * P)
                        ins = parts(ps[b % 4][:, pos * width:(pos + 1) * width], (xh[:, k, ts], xl[:, k, ts]),
                                    (wH[n % 2][:, k, c0:c0 + width], wL[n % 2][:, k, c0:c0 + width]), k == 0, k == KC - 1)
                ins.then_inc(blk_done, 1)

            def token_unit(n, xh, xl, blocks=((0, 1), (2, 3))):
                unit_ready(n)
                for c, tbs in enumerate(blocks):
                    token_block(n, BLOCK0[n] + c, tbs, xh, xl)

            def norm_sum(name, twice=False):
                pe.wait_ge(sq_added, SQ0[name] + (16 if twice else 8))
                for g in range(2 if twice else 1):
                    for tb in range(TB):
                        ins = nc.tensor.matmul(ps[6][:, 4 * g + tb:4 * g + tb + 1], (ssum, gsum)[g][:, tb * P:(tb + 1) * P],
                                               ones[:, 0:1], start=True, stop=True)
                ins.then_inc(sum_done, 1)

            def broadcast(src, bank):
                for tb in range(TB):
                    ins = nc.tensor.matmul(ps[bank][:, tb * P:(tb + 1) * P], src[:, tb:tb + 1].to_broadcast([P, P]), ident,
                                           start=True, stop=True)
                return ins

            def norm_broadcast(name):
                pe.wait_ge(inv_done, NORMS[name] + 1)
                broadcast(rootinv, 4).then_inc(bc_done, 1)

            def norm(name):
                norm_sum(name)
                norm_broadcast(name)

            def chunks_of(q0):
                return lambda k: q0 + k + 1

            def all_chunks_of(q0):
                return lambda k: q0 + KC

            def attention(kind):
                c = ATT[kind]
                ns = c["heads"] * TB
                pe.wait_ge(blk_taken, TAKEN[BLOCK0[AT[{"fox": "out", "cross": "xo", "grid": "ev_out"}[kind]][0]]])

                def gates_everywhere(h):
                    if h >= 2:
                        pe.wait_ge(f_bcs, h - 1)
                    nc.tensor.matmul(ps[2 + h % 2][:], ident[0:FOX_H, h:h + 1].to_broadcast([FOX_H, P]), frow[0][:],
                                     start=True, stop=True).then_inc(f_bc, 1)

                def scores(g, h, i):
                    hp, blk, ts = (h % 2) * 64, h // 2, slice(i * P, (i + 1) * P)
                    dst = ps[4 + g % 2]
                    if g >= 2:
                        pe.wait_ge(mx_done if kind == "fox" else ex_done, g - 1)
                    if kind == "fox":
                        nc.tensor.matmul(dst[:, 0:(i + 1) * P], fq[hp:hp + 64, blk, ts], fk[hp:hp + 64, blk, 0:(i + 1) * P],
                                         start=True, stop=False)
                        ins = nc.tensor.matmul(dst[:, ts], identb[:], causalb[:], start=False, stop=True)
                    elif kind == "cross":
                        nc.tensor.matmul(dst[:, 0:M_MEM], xq[:, 2 * h, ts], xk[:, 2 * h, :], start=True, stop=False)
                        ins = nc.tensor.matmul(dst[:, 0:M_MEM], xq[:, 2 * h + 1, ts], xk[:, 2 * h + 1, :], start=False, stop=True)
                    else:
                        ins = nc.tensor.matmul(dst[:], evq[hp:hp + 64, blk, ts], kdup[hp:hp + 64, h // 4, :], start=True, stop=True)
                    ins.then_inc(sc_done, 1)

                def values(h):
                    hp = (h % 2) * 64
                    pe.wait_ge(pt_done, c["step0"] + TB * h + TB)
                    if kind == "cross":
                        for cc in range(2):
                            if h:
                                pe.wait_ge(op_lo, c["q0"] + 2 * (h - 1) + cc + 1)
                            for m in range(2):
                                ins = nc.tensor.matmul(ps[cc][:], xv[:, m, h * UC + cc * P:h * UC + (cc + 1) * P],
                                                       pT[h % 2][:, m, :], start=(m == 0), stop=(m == 1))
                            ins.then_inc(pv_done, 1)
                        return
                    if h % 2 == 0 and h >= 4:
                        pe.wait_ge(op_lo, c["q0"] + h // 2 - 1)
                    for j in range(TB):
                        t0 = j * P if kind == "fox" else 0
                        v = fv[:, j, h * 64:(h + 1) * 64] if kind == "fox" else evv[:, j, (h // 4) * 64:(h // 4) * 64 + 64]
                        ins = nc.tensor.matmul(ps[h // 2 % 2][hp:hp + 64, t0:S], v, pT[h % 2][:, j, t0:S],
                                               start=(j == 0), stop=(j == TB - 1))
                    ins.then_inc(pv_done, 1)

                if kind == "fox":
                    pe.wait_ge(f_rows, 1)
                    gates_everywhere(0)
                if kind == "grid":
                    pe.wait_ge(g_kd, 2)
                for s in range(ns + 3):
                    if kind == "fox" and s % 4 == 1 and s // 4 + 1 < FOX_H:
                        gates_everywhere(s // 4 + 1)
                    if s < ns:
                        scores(c["step0"] + s, s // TB, s % TB)
                    t = s - 2
                    if 0 <= t < ns:
                        g, i = c["step0"] + t, t % TB
                        nj = {"fox": i + 1, "cross": 2, "grid": TB}[kind]
                        pe.wait_ge(pn_done, g + 1)
                        if g >= 2:
                            pe.wait_ge(pt_done, g - 1)
                        for j in range(nj):
                            ins = nc.tensor.transpose(ps[6 + g % 2][:, j * P:(j + 1) * P], pr[g % 3][:, j * P:(j + 1) * P], ident)
                        ins.then_inc(tp_done, 1)
                    if s >= 3 and (s - 3) % TB == TB - 1:
                        values((s - 3) // TB)

            pe.wait_ge(cst_in, 16)
            for tb in range(TB):
                pe.wait_ge(x_in[tb], 16)
            for j in range(KC):
                if j >= 2:
                    pe.wait_ge(x_cols, j - 1)
                for tb in range(TB):
                    ins = nc.tensor.transpose(ps[6 + j % 2][:, tb * P:(tb + 1) * P], xtok[:, tb, j * P:(j + 1) * P], ident)
                ins.then_inc(x_tr, 1)
            pe.wait_ge(vec_in, 16 * 19)
            nc.tensor.transpose(ps[5][:, 0:V_ROWS], vrow[0:V_ROWS, :], ident[0:V_ROWS, 0:V_ROWS]).then_inc(vec_tr, 1)
            nc.tensor.transpose(ps[5][:, 128:224], brow[0:96, :], ident[0:96, 0:96]).then_inc(vec_tr, 1)
            pe.sem_inc(ada_mm, 2)
            norm_broadcast("mix")

            n = AT["in"][0]
            for u in range(4):
                feature_unit(n + u, hnH, hnL, need=chunks_of(Q0["mix_norm"]) if u == 0 else None)
            for u in range(4, 6):
                token_unit(n + u, hnH, hnL)
            for u in range(6, 11):
                feature_unit(n + u, hnH, hnL)
            for u in range(11, 13):
                token_unit(n + u, hnH, hnL)
            for u in range(13, 15):
                feature_unit(n + u, hnH, hnL)
            attention("fox")
            v = 0
            for h in range(HG_H):
                for l in range(8):
                    e = 8 * h + l
                    if l < 7:
                        pe.wait_ge(h_q, v + 1)
                        pe.wait_ge(h_k, v + 1)
                    if e >= 2:
                        pe.wait_ge(h_at, e - 1)
                    for c in range(TB):
                        cs = slice(c * P, (c + 1) * P)
                        k_, q_ = (kt[v % 2][:, cs], qt[v % 2][:, cs]) if l < 7 else (gk[:, h, cs], gq[:, h, cs])
                        ins = nc.tensor.matmul(ps[4 + e % 2][:, cs], k_, q_, start=True, stop=True)
                    ins.then_inc(h_pl, 1)
                    v += l < 7
                pe.wait_ge(h_kd, h + 1)
                if h:
                    pe.wait_ge(h_kts, h)
                for c in range(3):
                    ins = nc.tensor.transpose(ps[6][:, c * P:(c + 1) * P], kd[:, c * P:(c + 1) * P], ident)
                ins.then_inc(h_kt, 1)
                pe.wait_ge(h_kts, h + 1)
                if h:
                    pe.wait_ge(h_st, 3 * h)
                hv = slice(h * P, (h + 1) * P)
                for c in range(3):
                    ins = nc.tensor.matmul(ps[7][:, c * P:(c + 1) * P], kdT[:, c, :], gi[:, c, hv], start=True, stop=True)
                ins.then_inc(h_sp, 1)
                pe.wait_ge(h_at, 8 * h + 8)
                pe.wait_ge(h_qb, h + 1)
                pe.wait_ge(h_st, 3 * h + 3)
                if h >= 2:
                    pe.wait_ge(h_os, h - 1)
                for c in range(TB):
                    cs = slice(c * P, (c + 1) * P)
                    ins = nc.tensor.matmul(ps[h % 2][:, cs], gi[:, c, hv], at_[h % 2][:, c, :], start=True, stop=(c == 0))
                    if c:
                        ins = nc.tensor.matmul(ps[h % 2][:, cs], st[:, c - 1, :], qb[:, cs], start=False, stop=True)
                ins.then_inc(h_o, 1)
            hr = [dd[0], dd[1], kt[0], kt[1]]
            for h in range(HG_H):
                pe.wait_ge(h_sq, h + 1)
                nc.tensor.matmul(ps[4 + h][:], ones, hr[h][:], start=True, stop=True).then_inc(h_sum, 1)
            n = AT["out"][0]
            feature_unit(n, uH, uL, need=all_chunks_of(Q0["mix"]))
            for u in range(1, 4):
                feature_unit(n + u, uH, uL)
                if u == 3:
                    break
                pe.wait_ge(m_n, 2)
                for j in range(4 * u - 4, 4 * u):
                    if j >= 4:
                        pe.wait_ge(op_lo, Q0["mem"] + j - 3)
                    for mb in range(2):
                        ins = nc.tensor.transpose(ps[4 + j % 4][:, mb * P:(mb + 1) * P], mtok[:, mb, j * P:(j + 1) * P], ident)
                    ins.then_inc(m_tr, 1)
            n = AT["xkv"][0]
            for u in range(8):
                if u < 4:
                    feature_unit(n + u, memH, memL, M_MEM, need=chunks_of(Q0["mem"]) if u == 0 else None)
                else:
                    token_unit(n + u, memH, memL, ((0,), (1,)))
                if u == 1:
                    norm_sum("x")
                if u == 2:
                    norm_broadcast("x")
            for u, n in enumerate(range(*ranges("xq"))):
                feature_unit(n, hnH, hnL, need=chunks_of(Q0["x_norm"]) if u == 0 else None)
            attention("cross")
            for u, n in enumerate(range(*ranges("xo"))):
                feature_unit(n, uH, uL, need=all_chunks_of(Q0["x_att"]) if u == 0 else None)
            norm("ff1")
            n0, b0 = AT["ff1"]

            def conditioning_sums(layer, i, m):
                group = ADA_GROUP[layer]
                pe.wait_ge(ada_acc, i * group + (24 * layer + m + 1 + ADA_RING))
                if m == 0:
                    pe.wait_ge(mod_done, i + (1, 5)[layer])
                nc.tensor.matmul(ps[5][:, 2 * m:2 * m + 1], adacc[m % 2][:, 0:P], ones[:, 0:1], start=True, stop=True)
                nc.tensor.matmul(ps[5][:, 2 * m + 1:2 * m + 2], adacc[m % 2][:, P:UC], ones[:, 0:1],
                                 start=True, stop=True).then_inc(ada_mm, 1)

            def squared_relu(i, last=False):
                for u in range(8):
                    if u < 4:
                        feature_unit(n0 + u, hnH, hnL, need=chunks_of(Q0["ff1_norm"]) if u == 0 else None, i=i, du=8, dt=16)
                    else:
                        feature_unit(n0 + u, uH, uL, need=(lambda k: i * 8 + (Q0["ff1_u"] + k + 1)) if u == 4 else None,
                                     i=i, du=8, dt=16)
                    if not last:
                        conditioning_sums(0, i, u)

            with pe.Fori(0, 3) as i:
                squared_relu(i)
            squared_relu(3, True)
            norm_sum("ev", True)
            pe.wait_ge(e_inv, 1)
            broadcast(rootinv, 4)
            broadcast(msq, 5).then_inc(bc_done, 1)
            n = AT["ev_in"][0]
            for u in range(4):
                feature_unit(n + u, hnH, hnL, need=chunks_of(Q0["ev_norm"]) if u == 0 else None)
            n += 4
            unit_ready(n)
            b = BLOCK0[n]
            bank_free(b)
            for k in range(KC):
                ins = parts(ps[b % 4][:], (wH[n % 2][:, k, 0:P], wL[n % 2][:, k, 0:P]), (hnH[:, k, :], hnL[:, k, :]),
                            k == 0, k == KC - 1)
            ins.then_inc(blk_done, 1)
            token_block(n, b + 1, range(TB), hnH, hnL, P, P)
            pe.wait_ge(blk_taken, TAKEN[BLOCK0[AT["ev_out"][0]]])
            for j in range(5):
                pe.wait_ge(g_sq, j + 1)
                nc.tensor.matmul(ps[j][:], cst[:, C_HALF, :], gs[:, j, :], start=True, stop=True).then_inc(g_sum, 1)
            pe.wait_ge(g_rs, 5)
            for j in range(5):
                pe.wait_ge(g_n, j + 1)
                if j >= 2:
                    pe.wait_ge(g_roped, j - 1)
                nc.tensor.matmul(ps[4 + j % 2][:], cst[:, C_ROT, :], evq[:, j, :], start=True, stop=True).then_inc(g_rot, 1)
            pe.wait_ge(g_roped, 5)
            for j in range(2):
                nc.tensor.matmul(ps[6 + j][:], cst[:, C_DUP0 + j, :], evq[:, 4, :], start=True, stop=True).then_inc(g_dup, 1)
            attention("grid")
            for j in range(4):
                pe.wait_ge(p_done, j + 1)
                if j >= 2:
                    pe.wait_ge(op_lo, Q0["ev_mix"] + 4 + j - 1)
                nc.tensor.matmul(ps[2 + j % 2][:], wpool[:, j, :], pd[:, j, :], start=True, stop=True).then_inc(p_mm, 1)
            for u, n in enumerate(range(*ranges("ev_out"))):
                feature_unit(n, uH, uL, need=all_chunks_of(Q0["ev_mix"]) if u == 0 else None)

            def gated_ffn(layer):
                name = f"ff2_{layer}"
                n0, b0 = AT[name]
                q0 = Q0[name + "_u"]
                with pe.Fori(0, 2) as i:
                    for u in range(12):
                        if u < 8:
                            feature_unit(n0 + u, hnH, hnL, need=chunks_of(Q0[name + "_norm"]) if u == 0 else None,
                                         i=i, du=12, dt=16, ds=8)
                        else:
                            feature_unit(n0 + u, uH, uL, need=(lambda k: i * 8 + (q0 + k + 1)) if u == 8 else None,
                                         i=i, du=12, dt=16, ds=8)
                        if layer == 0:
                            conditioning_sums(1, i, u)
                for u in range(24, 30):
                    feature_unit(n0 + u, hnH, hnL)
                for u in range(30, 34):
                    feature_unit(n0 + u, uH, uL, need=chunks_of(q0 + 16) if u == 30 else None)

            norm("ff2_0")
            gated_ffn(0)
            norm("od")
            n = AT["od_in"][0]
            for u in range(4):
                feature_unit(n + u, hnH, hnL, need=chunks_of(Q0["od_norm"]) if u == 0 else None)
            for u in range(4, 12):
                token_unit(n + u, hnH, hnL)
            feature_unit(n + 12, hnH, hnL)
            pe.wait_ge(blk_taken, TAKEN[BLOCK0[AT["od_out"][0]]])
            for half in range(2):
                ins = nc.tensor.matmul(ps[4 + half][0:64, :], cst[96:128, C_GSEL, half * 64:(half + 1) * 64], grow[96:128, :],
                                       start=True, stop=True)
            ins.then_inc(r_sel, 1)
            pe.wait_ge(r_rows, 1)
            for tb in range(TB):
                ins = nc.tensor.transpose(ps[6][:, tb * 64:(tb + 1) * 64], irow[:, tb * P:(tb + 1) * P], ident[0:64, 0:64])
            ins.then_inc(r_tr, 1)
            pe.wait_ge(r_em, 1)
            for tb in range(TB):
                ins = nc.tensor.transpose(ps[7][:, tb * 64:(tb + 1) * 64], erow[:, tb * P:(tb + 1) * P], ident[0:64, 0:64])
            ins.then_inc(r_tr, 1)
            pe.wait_ge(r_rows, 2)
            pe.wait_ge(r_cols, 2)

            def out_rows(h, d):
                pe.wait_ge(l_a, 8 * h + 4 * d + 4)
                if 2 * h + d:
                    pe.wait_ge(l_h, 2 * h + d)
                for i in range(TB):
                    dst = ps[6 + i // 2][:, (i % 2) * 129:(i % 2) * 129 + 129]
                    js = range(0, i + 1) if d == 0 else range(i, TB)
                    for j in js:
                        ins = nc.tensor.matmul(dst, ma[d][:, j, i * P:(i + 1) * P], vx[:, j, h, :],
                                               start=(j == js[0]), stop=(j == js[-1]))
                ins.then_inc(l_o, 1)

            pe.wait_ge(c_silu, KC)
            for h in range(ML_H + 1):
                if h:
                    out_rows(h - 1, 0)
                if h < ML_H:
                    for d in range(2):
                        if h:
                            pe.wait_ge(l_w, 8 * (h - 1) + 4 * d + 4)
                        row = h + 32 * d
                        nc.tensor.matmul(ps[4 + d][:], ident[0:64, row:row + 1].to_broadcast([64, P]), Mrow[:],
                                         start=True, stop=True).then_inc(l_bc, 1)
                    hp = (h % 2) * 64
                    for j in range(TB):
                        if h:
                            pe.wait_ge(l_a, 8 * (h - 1) + 4 + j + 1)
                        nc.tensor.matmul(ps[j][:], cy[hp:hp + 64, 4 + h // 2, j * P:(j + 1) * P], cy[hp:hp + 64, h // 2, :],
                                         start=True, stop=True).then_inc(l_qk, 1)
                if h:
                    out_rows(h - 1, 1)
            pe.wait_ge(n_h, TB)
            for j in range(KC):
                if j >= 4:
                    pe.wait_ge(op_lo, Q0["od_mix"] + j - 3)
                for tb in range(TB):
                    ins = nc.tensor.transpose(ps[4 + j % 4][:, tb * P:(tb + 1) * P], hs[:, tb, j * P:(j + 1) * P], ident)
                ins.then_inc(n_tr, 1)
            for u, n in enumerate(range(*ranges("od_out"))):
                feature_unit(n, uH, uL, need=chunks_of(Q0["od_mix"]) if u == 0 else None)
            norm("ff2_1")
            gated_ffn(1)
            pe.wait_ge(blk_taken, TAKEN[-1])
            for o in range(2 * TB):
                tb, half = o // 2, o % 2
                if o >= 4:
                    pe.wait_ge(o_cp, o - 3)
                for j in range(4):
                    ins = nc.tensor.transpose(ps[4 + o % 4][:, j * P:(j + 1) * P], xT[:, 4 * half + j, tb * P:(tb + 1) * P], ident)
                ins.then_inc(o_tr, 1)


def constants():
    c = np.zeros((N_CONST, P, P), np.float32)
    c[C_IDENT] = np.eye(P)
    c[C_ONES] = 1.0
    half = np.arange(P) // 64
    c[C_HALF] = half[:, None] == half[None, :]
    for i in range(0, P, 2):
        c[C_ROT, i + 1, i] = -1.0
        c[C_ROT, i, i + 1] = 1.0
    for kv in range(2):
        for m in range(P):
            c[C_DUP0 + kv, kv * 64 + m % 64, m] = 1.0
    for d in range(2):
        for h in range(ML_H):
            c[C_GSEL, 96 + 16 * d + h, 32 * d + h] = 1.0
            c[C_GSEL, 96 + 16 * d + 8 + h, 64 + 32 * d + h] = 1.0
    t, s = np.arange(P)[:, None], np.arange(P)[None, :]
    c[C_CAUSAL] = np.where(t >= s, 0.0, NEG)
    levels = np.zeros((8, P, P), np.float32)
    s, t = np.arange(P)[:, None], np.arange(P)[None, :]
    for l, L in enumerate(HG_LEVELS):
        levels[l] = (s // (2 * L) == t // (2 * L)) & (s % (2 * L) < L) & (t % (2 * L) >= L)
    levels[7] = s == t
    row, colm = np.repeat(np.arange(S // 64), 64).astype(np.float32), np.tile(np.arange(64), S // 64).astype(np.float32)
    inv = (np.float32(10000.0) ** (-np.arange(16, dtype=np.float32) / np.float32(16))).astype(np.float32)
    ang = np.concatenate([row[:, None] * inv, colm[:, None] * inv], axis=-1)
    lane = (np.arange(P) % 64) // 2
    rope = np.stack([np.cos(ang)[:, lane].T, np.sin(ang)[:, lane].T]).astype(np.float32)
    t = np.arange(S)
    icount = np.stack([1.0 / (np.clip(t + w - w // 2, 0, S) - np.clip(t - w // 2, 0, S)) for w in WINDOWS]).astype(np.float32)
    return {"const": c, "levels": levels, "rope": np.ascontiguousarray(rope), "icount": icount}


_INS = ["x", "mem", "norm_mix_g", "w_in", "fox_f_bias", "hgrn_lb_logits", "hgrn_norm_g", "w_out", "norm_x_g", "norm_mem_g",
        "w_xq", "w_xkv", "w_xo", "norm_ff_g", "w1", "w2", "final_norm_g", "c_2", "ada_w_2", "ada_b_2", "ev_w_in_2",
        "ev_w_pool_2", "ev_b_pool_2", "ev_pool_scale_2", "ev_q_gain_2", "ev_k_gain_2", "ev_w_out_2", "od_w_in_2",
        "od_conv_w_2", "od_conv_b_2", "od_gate_b_2", "od_head_gain_2", "od_w_out_2", "ffn_w1_2", "ffn_w3_2", "ffn_w2_2"]


def kernel(**inputs):
    import numpy as _np
    import concourse.bacc as _bacc
    from concourse import mybir as _mybir
    from concourse.bass_utils import run_bass_kernel_spmd as _run

    nc = _bacc.Bacc("TRN2", target_bir_lowering=False, num_devices=1)
    arrays, aps = {}, {}
    given = {name: _np.ascontiguousarray(inputs[name]) for name in _INS}
    given.update(constants())
    for name, value in given.items():
        arrays[f"in_{name}_dram"] = value
        aps[name] = nc.dram_tensor(f"in_{name}_dram", value.shape, _mybir.dt.from_np(value.dtype), kind="ExternalInput").ap()
    out = nc.dram_tensor("out_0_dram", (1, S, D), _mybir.dt.float32, kind="ExternalOutput").ap()
    bass_block_pair(nc, aps, out)
    r = _run(nc, [arrays], core_ids=[0])
    return r.results[0]["out_0_dram"]
```

```python
from contextlib import ExitStack

import numpy as np

import concourse.bass as bass
from concourse import mybir

F32 = mybir.dt.float32
F32R = mybir.dt.float32r
BF16 = mybir.dt.bfloat16
U32 = mybir.dt.uint32
ALU = mybir.AluOpType
ACT = mybir.ActivationFunctionType
AX = mybir.AxisListType.X

P = 128
D = 1024
S = 512
KC = D // P
TB = S // P
M_MEM = 256
EPS = 1e-6
UC = 256
FF1 = 4096
FF2 = 2816
FOX_H, FOX_D = 8, 64
HG_H = 4
HG_LEVELS = (1, 2, 4, 8, 16, 32, 64)
X_H = 4
GA_H = 8
ML_H, ML_V = 8, 128
WINDOWS = (2, 4, 8, 16)
CONV_K = 5
NEG = -1.0e30

C_IDENT, C_ONES, C_HALF, C_ROT, C_DUP0, C_DUP1, C_GSEL, C_CAUSAL = range(8)
N_CONST = 8

V_MIX, V_X, V_MEM, V_FF, V_FINAL, V_LB, V_HG, V_C, V_BPOOL, V_SPOOL, V_CW, V_CB, V_QG, V_KG = (
    0, 8, 16, 24, 32, 40, 48, 49, 57, 61, 65, 105, 113, 114)
V_ROWS = 115


def plan():
    units = []

    def add(w, k0, kc, c0, cols, blocks=2):
        units.append((w, k0, kc, c0, cols, blocks))

    at = {}

    def stage(name):
        at[name] = (len(units), sum(u[5] for u in units))

    stage("in")
    for c0 in (0, 256, 512, 768, 1024, 1280):
        add("w_in", 0, KC, c0, UC)
    add("w_in", 0, KC, 1536, P, 1)
    for c0 in range(1544, 3592, UC):
        add("w_in", 0, KC, c0, UC)
    stage("out")
    for c0 in range(0, D, UC):
        add("w_out", 0, KC, c0, UC)
    stage("xkv")
    for c0 in range(0, 2 * D, UC):
        add("w_xkv", 0, KC, c0, UC)
    stage("xq")
    for c0 in range(0, D, UC):
        add("w_xq", 0, KC, c0, UC)
    stage("xo")
    for c0 in range(0, D, UC):
        add("w_xo", 0, KC, c0, UC)
    stage("ff1")
    for g in range(FF1 // D):
        for c0 in range(g * D, (g + 1) * D, UC):
            add("w1", 0, KC, c0, UC)
        for c0 in range(0, D, UC):
            add("w2", g * KC, KC, c0, UC)
    stage("ev_in")
    for c0 in (512, 768, 1024, 0, 256):
        add("ev_w_in_2", 0, KC, c0, UC)
    stage("ev_out")
    for c0 in range(0, D, UC):
        add("ev_w_out_2", 0, KC, c0, UC)
    for layer in range(2):
        if layer == 1:
            stage("od_in")
            for c0 in range(0, D, UC):
                add("od_w_in_2", 0, KC, c0, UC)
            add("od_w_in_2", 0, KC, 3104 - P, P, 1)
            for c0 in range(D, 3 * D, UC):
                add("od_w_in_2", 0, KC, c0, UC)
            stage("od_out")
            for c0 in range(0, D, UC):
                add("od_w_out_2", 0, KC, c0, UC)
        stage(f"ff2_{layer}")
        for g0 in range(0, FF2, D):
            for c0 in range(g0, min(g0 + D, FF2), UC):
                add(f"ffn_w1_2.{layer}", 0, KC, c0, UC)
                add(f"ffn_w3_2.{layer}", 0, KC, c0, UC)
            for c0 in range(0, D, UC):
                add(f"ffn_w2_2.{layer}", g0 // P, min(g0 + D, FF2) // P - g0 // P, c0, UC)
    stage("end")
    return units, at


UNITS, AT = plan()
N_UNITS = len(UNITS)
BLOCK0 = [sum(u[5] for u in UNITS[:n]) for n in range(N_UNITS + 1)]
BY_ACT = [u[0].startswith("ffn_w1") for u in UNITS for _ in range(u[5])]
TAKEN = [sum(not x for x in BY_ACT[:b]) for b in range(len(BY_ACT) + 1)]
SILUS = [sum(x for x in BY_ACT[:b]) for b in range(len(BY_ACT) + 1)]

Q0 = {}
_q = 0
for _name, _count in (("mix_norm", 8), ("mix", 8), ("mem", 8), ("x_norm", 8), ("x_att", 8), ("ff1_norm", 8),
                      ("ff1_u", 32), ("ev_norm", 8), ("ev_mix", 8), ("ff2_0_norm", 8), ("ff2_0_u", 22),
                      ("od_norm", 8), ("od_mix", 8), ("ff2_1_norm", 8), ("ff2_1_u", 22)):
    Q0[_name] = _q
    _q += _count

ATT = {
    "fox": dict(heads=FOX_H, step0=0, pv0=0, pvh=1, q0=Q0["mix"], col0=0),
    "cross": dict(heads=X_H, step0=32, pv0=8, pvh=2, q0=Q0["x_att"], col0=0),
    "grid": dict(heads=GA_H, step0=48, pv0=16, pvh=1, q0=Q0["ev_mix"], col0=4),
}
NORMS = {n: i for i, n in enumerate(("mix", "x", "ff1", "ev", "ff2_0", "od", "ff2_1"))}
SQ0 = {n: 8 * (i - 1) + (8 if i > NORMS["ev"] else 0) for n, i in NORMS.items() if i}


PR_RING = 4
HG_BY_POOL = (2, 5)
HG_RING = 4
WT_RING = 8
ADA_RING = 4
ADA_GROUP = (8, 12)
GA_SCALE = 64 ** -0.5
ROPE_ORDER = (0, 1, 2, 4, 3)
ROPE_BANK = (5, 6, 7, 5, 6)
LB_SHIFTED = 7
POOL_STEPS = sum(g + 2 for g in range(len(WINDOWS)))


def ranges(name):
    starts = sorted(v[0] for v in AT.values())
    n = AT[name][0]
    return n, starts[starts.index(n) + 1]


def queries(v):
    return sum(u % len(HG_LEVELS) not in HG_BY_POOL for u in range(v + 1))


def products(v):
    return 8 * (v // len(HG_LEVELS)) + v % len(HG_LEVELS) + 1


def add(i, count):
    return count if i is None else i + count


def outputs(kind, t):
    h = t // TB
    if t % TB != TB - 1 or not 0 <= h < ATT[kind]["heads"]:
        return []
    return [2 * h, 2 * h + 1] if kind == "cross" else [h // 2] if h % 2 else []


def bass_block_pair(nc, a, out):
    BASE = 16512
    top = [0]

    def place(name, shape, dt, offset=None):
        size = int(np.prod(shape[1:])) * (2 if dt == BF16 else 4)
        if offset is None:
            offset = top[0]
            top[0] += -(-size // 32) * 32
        return nc.alloc_sbuf_tensor_at(name, shape, dt, offset=BASE + offset), offset

    raw = [place(f"raw{i}", [P, KC, UC], F32)[0] for i in range(2)]
    wH = [place(f"wH{i}", [P, KC, UC], F32R)[0] for i in range(2)]
    wL = [place(f"wL{i}", [P, KC, UC], F32R)[0] for i in range(2)]
    xT = place("xT", [P, KC, S], F32)[0]
    hnH, HN = place("hnH", [P, KC, S], F32R)
    hnL = place("hnL", [P, KC, S], F32R)[0]
    uH, UHOFF = place("uH", [P, KC, S], F32R)
    uL, ULOFF = place("uL", [P, KC, S], F32R)
    cst = place("cst", [P, N_CONST, P], F32)[0]
    identb = place("identb", [P, P], BF16)[0]
    causalb = place("causalb", [P, P], BF16)[0]
    cols = place("cols", [P, P], F32)[0]
    adab = place("adab", [P, 96], F32)[0]
    mod = place("mod", [P, 96], F32)[0]
    modp = place("modp", [P, 96], F32)[0]
    small = place("small", [P, 192], F32)[0]
    T, TOFF = [], []
    for i in range(2):
        t, o = place(f"T{i}", [P, S], F32)
        T.append(t)
        TOFF.append(o)
    R, ROFF = [], []
    for i in range(2):
        t, o = place(f"R{i}", [P, S], F32)
        R.append(t)
        ROFF.append(o)
    sq, SQOFF = [], []
    for i in range(2):
        t, o = place(f"sq{i}", [P, S], F32)
        sq.append(t)
        SQOFF.append(o)
    ssum, SSOFF = place("ssum", [P, S], F32)
    gsum, GSOFF = place("gsum", [P, S], F32)
    AR = top[0]
    assert BASE + AR + 57600 <= 229344, AR

    ident = cst[:, C_IDENT, :]
    ones = cst[:, C_ONES, :]

    eps = small[:, 0:1]
    nmax = small[:, 4:8]
    rsum = small[:, 8:12]
    rinv = small[:, 12:16]
    lb = small[:, 16:20]
    omlb = small[:, 20:24]
    lbt = small[:, 24:40]
    condc = small[:, 40:48]
    fbias = small[:, 48:49]
    gbias = small[:, 49:50]
    mstat = small[:, 56:64]
    mden = small[:, 64:72]
    hstat = small[:, 72:104]
    hrs = small[:, 104:136]
    nmraw = small[:, 136:140]
    warm = small[:, 140:141]
    root = small[:, 168:172]
    rootinv = small[:, 150:154]
    msq = small[:, 154:158]
    nt1 = small[:, 172:176]
    nt2 = small[:, 176:180]
    hnt = adab[:, 0:64]
    gm = small[:, 160:168]

    xtok = place("xtok", [P, TB, D], F32, AR)[0]
    vrow = place("vrow", [P, P], F32, AR + 16384)[0]
    brow = place("brow", [P, P], F32, AR + 16896)[0]
    fq = place("fq", [P, 4, S], F32, AR)[0]
    fk = place("fk", [P, 4, S], F32, AR + 8192)[0]
    fv = place("fv", [P, TB, 512], F32, AR + 16384)[0]
    gq = place("gq", [P, HG_H, S], F32, AR + 24576)[0]
    gk = place("gk", [P, HG_H, S], F32, AR + 32768)[0]
    gi = place("gi", [P, TB, 512], F32, AR + 40960)[0]
    gg = place("gg", [P, HG_H, S], F32, AR + 49152)[0]
    pr = [place(f"pr{i}", [P, S], F32, HN + (26624 if i == 3 else 2048 * i))[0] for i in range(PR_RING)]
    pT = [place(f"pT{i}", [P, TB, S], F32, HN + 6144 + 8192 * i)[0] for i in range(2)]
    fbc = [place(f"fbc{i}", [P, S], F32, HN + 22528 + 2048 * i)[0] for i in range(2)]
    fz = place("fz", [FOX_H, S], F32, TOFF[0])[0]
    frow = [place(f"frow{i}", [FOX_H, S], F32, o)[0] for i, o in enumerate((SQOFF[0], SQOFF[1], TOFF[1]))]
    gb = place("gb", [P, HG_H, S], F32, UHOFF + 8192)[0]
    lnf = place("lnf", [P, HG_H, S], F32, ULOFF + 8192)[0]
    lvl = place("lvl", [P, 8, P], F32, AR + 8192)[0]
    ho = place("ho", [P, HG_H, S], F32, AR + 12288)[0]
    dd = R + [place(f"dd{i}", [P, S], F32, HN + 2048 * i)[0] for i in range(2)]
    qt = [place(f"qt{i}", [P, S], F32, HN + 4096 + 2048 * i)[0] for i in range(2)] + sq
    kt = [place(f"kt{i}", [P, S], F32, HN + 8192 + 2048 * i)[0] for i in range(2)] + [ssum, gsum]
    at_ = [place(f"at{i}", [P, TB, P], F32, HN + 12288 + 2048 * i)[0] for i in range(2)]
    qb = place("qb", [P, S], F32, HN + 16384)[0]
    kd = place("kd", [P, S], F32, HN + 18432)[0]
    eb = place("eb", [P, S], F32, HN + 20480)[0]
    ed = place("ed", [P, S], F32, HN + 22528)[0]
    kdT = place("kdT", [P, 3, P], F32, HN + 24576)[0]
    st = place("st", [P, 3, P], F32, HN + 26112)[0]
    rmask = place("rmask", [P, S], F32, ROFF[0])[0]
    memH = place("memH", [P, KC, M_MEM], F32R, AR)[0]
    memL = place("memL", [P, KC, M_MEM], F32R, AR + 8192)[0]
    mtok = place("mtok", [P, 2, D], F32, AR + 49152)[0]
    xk = place("xk", [P, KC, M_MEM], F32, AR + 16384)[0]
    xv = place("xv", [P, 2, D], F32, AR + 24576)[0]
    xq = place("xq", [P, KC, S], F32, AR + 32768)[0]
    mdump = place("mdump", [P, D], F32, HN)[0]
    xdump = place("xdump", [P, D], F32, AR + 20480)[0]
    mT = [place(f"mT{i}", [P, M_MEM], F32, ROFF[i])[0] for i in range(2)]
    adaw = [place(f"adaw{i}", [P, KC, UC], F32, AR + 8192 * i)[0] for i in range(ADA_RING)]
    adacc = [place(f"adacc{i}", [P, UC], F32, AR + 8192 * ADA_RING + 1024 * i)[0] for i in range(2)]
    pu = place("pu", [P, 4, S + 24], F32, AR)[0]
    evq = place("evq", [P, 5, S], F32, AR + 8704)[0]
    evv = place("evv", [P, TB, P], F32, AR + 18944)[0]
    kdup = place("kdup", [P, 2, S], F32, AR + 20992)[0]
    cosb = place("cosb", [P, S], F32, AR + 25088)[0]
    sinb = place("sinb", [P, S], F32, AR + 27136)[0]
    icnt = place("icnt", [P, 4, S], F32, AR + 29184)[0]
    gs = place("gs", [P, 5, S], F32, UHOFF)[0]
    wpool = place("wpool", [P, 4, P], F32, AR + 37376)[0]
    pw = [place(f"pw{i}", [P, S + 24], F32, AR + 39424 + 2176 * i)[0] for i in range(2)]
    pd = place("pd", [P, 4, S], F32, AR + 43776)[0]
    cz = place("cz", [P, KC, S + 4], F32, AR)[0]
    hs = place("hs", [P, TB, D], F32, AR)[0]
    vx = place("vx", [P, TB, ML_H, ML_V + 1], F32, AR + 16512)[0]
    mo = place("mo", [P, TB, D], F32, AR + 33024)[0]
    hgain = place("hgain", [P, D], F32, AR + 49408)[0]
    wt = [place(f"wt{i}", [P, S], F32, ULOFF + 2048 * i)[0] for i in range(WT_RING)]
    cy = place("cy", [P, KC, S], F32, UHOFF)[0]
    ma = [[place(f"ma{i}{d}", [P, TB, S], F32, HN + 8192 * (2 * i + d))[0] for d in range(2)] for i in range(2)]
    hsq = T
    grow = place("grow", [P, S], F32, TOFF[0])[0]
    irow = place("irow", [64, S], F32, TOFF[1])[0]
    lrow = place("lrow", [64, S], F32, ROFF[0])[0]
    Frow = place("Frow", [64, S], F32, ROFF[1])[0]
    Mrow = place("Mrow", [64, S], F32, SQOFF[0])[0]
    erow = place("erow", [64, S], F32, SQOFF[1])[0]
    ccol = place("ccol", [P, TB, 64], F32, SSOFF)[0]
    ecol = place("ecol", [P, TB, 64], F32, GSOFF)[0]
    otok = place("otok", [P, TB, D], F32, AR)[0]

    with ExitStack() as ctx:
        ps = [ctx.enter_context(nc.psum_tensor(f"ps{i}", [P, S], F32)) for i in range(8)]

        def sem(name):
            return ctx.enter_context(nc.semaphore(name))

        raw_in = [sem(f"raw_in{i}") for i in range(2)]
        w_hi, w_lo = sem("w_hi"), sem("w_lo")
        blk_done = sem("blk_done")
        blk_taken = sem("blk_taken")
        op_t, op_hi, op_lo = sem("op_t"), sem("op_hi"), sem("op_lo")
        sq_done, sq_added, sum_done, root_done, inv_done, bc_done = (
            sem("sq_done"), sem("sq_added"), sem("sum_done"), sem("root_done"), sem("inv_done"), sem("bc_done"))
        cst_in, x_in, vec_in, vec_tr, vec_cols = sem("cst_in"), [sem(f"x_in{i}") for i in range(TB)], sem("vec_in"), sem("vec_tr"), sem("vec_cols")
        x_tr, x_cols = sem("x_tr"), sem("x_cols")
        setup, setup_d = sem("setup"), sem("setup_d")
        dstep = sem("dstep")
        astep = sem("astep")
        gstep = sem("gstep")
        sc_done, mx_done, ex_done, pn_done, tp_done, pt_done, pv_done = (
            sem("sc_done"), sem("mx_done"), sem("ex_done"), sem("pn_done"), sem("tp_done"), sem("pt_done"), sem("pv_done"))
        f_l, f_rows, f_bc, f_bcs = sem("f_l"), sem("f_rows"), sem("f_bc"), sem("f_bcs")
        lvl_in = sem("lvl_in")
        h_act, h_fk, h_ln, h_b = sem("h_act"), sem("h_fk"), sem("h_ln"), sem("h_b")
        h_d, h_e, h_q, h_k, h_pl, h_at = sem("h_d"), sem("h_e"), sem("h_q"), sem("h_k"), sem("h_pl"), sem("h_at")
        h_eb, h_qb, h_kd, h_kt, h_kts, h_sp, h_st, h_o, h_os = (
            sem("h_eb"), sem("h_qb"), sem("h_kd"), sem("h_kt"), sem("h_kts"), sem("h_sp"), sem("h_st"), sem("h_o"), sem("h_os"))
        h_sq, h_sum, h_rs, h_t, h_inv, h_bc = sem("h_sq"), sem("h_sum"), sem("h_rs"), sem("h_t"), sem("h_inv"), sem("h_bc")
        mem_in, m_root, m_n, m_tr, m_t = sem("mem_in"), sem("m_root"), sem("m_n"), sem("m_tr"), sem("m_t")
        ada_in = [sem(f"ada_in{i}") for i in range(ADA_RING)]
        ada_step = sem("ada_step")
        ada_acc, ada_mm, mod_done = sem("ada_acc"), sem("ada_mm"), sem("mod_done")
        relu_done, silu_done = sem("relu_done"), sem("silu_done")
        e_ms, e_root, e_inv = sem("e_ms"), sem("e_root"), sem("e_inv")
        ev_in, g_sq, g_sum, g_rs, g_n, g_rot, g_roped, g_dup, g_kd = (
            sem("ev_c_in"), sem("g_sq"), sem("g_sum"), sem("g_rs"), sem("g_n"), sem("g_rot"), sem("g_roped"), sem("g_dup"), sem("g_kd"))
        p_done, p_mm = sem("p_done"), sem("p_mm")
        gain_in, c_pad, c_y, c_silu, o_sig = sem("gain_in"), sem("c_pad"), sem("c_y"), sem("c_silu"), sem("o_sig")
        r_g, r_sel, r_i, r_abs, r_ln, r_rows, r_em, r_tr, r_cols = (
            sem("r_g"), sem("r_sel"), sem("r_i"), sem("r_abs"), sem("r_ln"), sem("r_rows"), sem("r_em"), sem("r_tr"), sem("r_cols"))
        l_bc, l_qk, l_w, l_a, l_wm, l_o, l_h = sem("l_bc"), sem("l_qk"), sem("l_w"), sem("l_a"), sem("l_wm"), sem("l_o"), sem("l_h")
        n_sq, n_sum, n_rs, n_h, n_tr, n_g = sem("n_sq"), sem("n_sum"), sem("n_rs"), sem("n_h"), sem("n_tr"), sem("n_g")
        o_tr, o_cp, o_out = sem("o_tr"), sem("o_cp"), sem("o_out")

        block = ctx.enter_context(nc.Block())

        def weight_view(name):
            if "." in name:
                name, layer = name.split(".")
                w = a[name][int(layer)]
            else:
                w = a[name][0]
            return w.rearrange("(k p) n -> p k n", p=P)

        @block.sync
        def _(sp):
            def load(n, value=None, src=None):
                w, k0, kc, c0, c, _ = UNITS[n]
                if n >= 2:
                    sp.wait_ge(w_lo, (n if value is None else value) - 1)
                if src is None:
                    src = weight_view(w)[:, k0:k0 + kc, c0:c0 + c]
                sp.dma_start(raw[n % 2][:, 0:kc, 0:c], src).then_inc(raw_in[n % 2], 16)

            def loads(first, last):
                for n in range(first, last):
                    load(n)

            sp.dma_start(cst[:], a["const"].rearrange("c p m -> p c m")).then_inc(cst_in, 16)
            rows = [("norm_mix_g", V_MIX, 8), ("norm_x_g", V_X, 8), ("norm_mem_g", V_MEM, 8), ("norm_ff_g", V_FF, 8),
                    ("final_norm_g", V_FINAL, 8), ("hgrn_lb_logits", V_LB, 8), ("hgrn_norm_g", V_HG, 1), ("c_2", V_C, 8),
                    ("ev_b_pool_2", V_BPOOL, 4), ("ev_pool_scale_2", V_SPOOL, 4), ("od_conv_w_2", V_CW, 40),
                    ("od_conv_b_2", V_CB, 8)]
            for tb in range(TB):
                sp.dma_start(xtok[:, tb, :], a["x"][0, tb * P:(tb + 1) * P, :]).then_inc(x_in[tb], 16)
            for name, r0, count in rows:
                src = a[name]
                nd = len(src.shape)
                flat = {1: "a -> a", 2: "a b -> (a b)", 3: "a b c -> (a b c)"}[nd]
                src = src if nd == 1 else src.rearrange(flat)
                sp.dma_start(vrow[r0:r0 + count, :], src.rearrange("(r m) -> r m", m=P)).then_inc(vec_in, 16)
            for name, r0 in (("ev_q_gain_2", V_QG), ("ev_k_gain_2", V_KG)):
                for half in range(2):
                    sp.dma_start(vrow[r0:r0 + 1, half * 64:half * 64 + 64], a[name][0:1, :]).then_inc(vec_in, 16)
            sp.dma_start(brow[0:96, :], a["ada_b_2"].rearrange("l (r m) -> (l r) m", m=P)).then_inc(vec_in, 16)
            sp.dma_start(fbias[0:8, :], a["fox_f_bias"].rearrange("a b -> b a")).then_inc(vec_in, 16)
            sp.dma_start(gbias[96:128, :], a["od_gate_b_2"].rearrange("a b -> b a")).then_inc(vec_in, 16)
            loads(0, AT["out"][0] + 1)
            sp.wait_ge(op_lo, Q0["mix"] + 4)
            sp.dma_start(lvl[:], a["levels"].rearrange("l s t -> s l t")).then_inc(lvl_in, 16)
            sp.wait_ge(op_lo, Q0["mix"] + 8)
            for mb in range(2):
                sp.dma_start(mtok[:, mb, :], a["mem"][0, mb * P:(mb + 1) * P, :]).then_inc(mem_in, 16)
            loads(AT["out"][0] + 1, AT["ff1"][0])

            def load_ada(layer, i, m):
                group = ADA_GROUP[layer]
                sp.wait_ge(ada_acc, i * group + (24 * layer + m + 1))
                adav = a["ada_w_2"][layer].rearrange("(k p) n -> p k n", p=P)
                sp.dma_start(adaw[m % ADA_RING][:], adav[:, :, bass.ds(i * (group * UC) + m * UC, UC)]).then_inc(
                    ada_in[m % ADA_RING], 16)

            n0 = AT["ff1"][0]
            w1v, w2v = weight_view("w1"), weight_view("w2")
            sp.wait_ge(op_lo, Q0["x_att"] + 8)
            with sp.Fori(0, 3) as i:
                for u in range(8):
                    if u < 4:
                        load(n0 + u, i * 8 + (n0 + u), w1v[:, :, bass.ds(i * D + u * UC, UC)])
                    else:
                        load(n0 + u, i * 8 + (n0 + u), w2v[:, bass.ds(i * KC, KC), (u - 4) * UC:(u - 3) * UC])
                    load_ada(0, i, u)
            loads(n0 + 24, n0 + 32)
            loads(AT["ev_in"][0], AT["ev_out"][0])
            sp.wait_ge(mod_done, 5)
            sp.dma_start(cosb[:], a["rope"][0]).then_inc(ev_in, 16)
            sp.dma_start(sinb[:], a["rope"][1]).then_inc(ev_in, 16)
            sp.dma_start(wpool[:], a["ev_w_pool_2"][0].rearrange("g c d -> c g d")).then_inc(ev_in, 16)
            sp.dma_start(icnt[:], a["icount"].rearrange("(o g) t -> o g t", o=1).to_broadcast([P, 4, S])).then_inc(ev_in, 16)
            loads(AT["ev_out"][0], AT["ff2_0"][0])

            def gated_ffn(layer):
                n0 = AT[f"ff2_{layer}"][0]
                w1v, w3v, w2v = (weight_view(f"ffn_w{j}_2.{layer}") for j in (1, 3, 2))
                with sp.Fori(0, 2) as i:
                    for u in range(12):
                        if u < 8:
                            src = (w1v, w3v)[u % 2][:, :, bass.ds(i * D + (u // 2) * UC, UC)]
                        else:
                            src = w2v[:, bass.ds(i * KC, KC), (u - 8) * UC:(u - 7) * UC]
                        load(n0 + u, i * 12 + (n0 + u), src)
                        if layer == 0:
                            load_ada(1, i, u)
                loads(n0 + 24, n0 + 34)

            sp.wait_ge(op_lo, Q0["ev_mix"] + 8)
            gated_ffn(0)
            loads(AT["od_in"][0], AT["od_in"][0] + 2)
            sp.wait_ge(op_lo, Q0["od_norm"] + 8)
            sp.dma_start(hgain[:], a["od_head_gain_2"].rearrange("o h v -> o (h v)").to_broadcast([P, D])).then_inc(gain_in, 16)
            loads(AT["od_in"][0] + 2, AT["ff2_1"][0])
            gated_ffn(1)
            for tb in range(TB):
                sp.wait_ge(o_cp, 2 * tb + 2)
                sp.dma_start(out[0, tb * P:(tb + 1) * P, :], otok[:, tb, :]).then_inc(o_out, 16)
            sp.wait_ge(o_out, 16 * TB)

        @block.gpsimd
        def _(pool):
            def low(n, value=None):
                _, _, kc, _, c, _ = UNITS[n]
                pool.wait_ge(w_hi, (n if value is None else value) + 1)
                nc.gpsimd.tensor_tensor(wL[n % 2][:, 0:kc, 0:c], raw[n % 2][:, 0:kc, 0:c],
                                        wH[n % 2][:, 0:kc, 0:c].bitcast(F32), ALU.subtract).then_inc(w_lo, 1)

            def lows(first, last):
                for n in range(first, last):
                    low(n)

            lows(0, AT["out"][0] + 1)
            v = 0
            for h in range(HG_H):
                for l in range(len(HG_LEVELS)):
                    pool.wait_ge(h_e, v + 1)
                    if v >= HG_RING:
                        pool.wait_ge(h_pl, products(v - HG_RING))
                    ins = nc.gpsimd.tensor_tensor(kt[v % HG_RING][:], gk[:, h, :], dd[v % HG_RING][:], ALU.mult)
                    if l in HG_BY_POOL:
                        ins = nc.gpsimd.tensor_tensor(qt[v % HG_RING][:], gq[:, h, :], dd[v % HG_RING][:], ALU.mult)
                    ins.then_inc(h_k, 1)
                    v += 1
                    if l == 3:
                        pool.wait_ge(h_eb, 2 * h + 2)
                        if h:
                            pool.wait_ge(h_kt, h)
                        nc.gpsimd.tensor_tensor(kd[:], gk[:, h, :], ed[:], ALU.mult).then_inc(h_kd, 1)
            lows(AT["out"][0] + 1, AT["ff1"][0])
            n0 = AT["ff1"][0]
            with pool.Fori(0, 4) as i:
                for u in range(8):
                    low(n0 + u, i * 8 + (n0 + u))
            lows(AT["ev_in"][0], AT["ev_out"][0] + 1)
            pool.wait_ge(ev_in, 64)
            pool.wait_ge(blk_taken, TAKEN[BLOCK0[AT["ev_in"][0]] + 10])
            g = 0
            for grp, w in enumerate(WINDOWS):
                src, half = pu[:, grp, :], 1
                for lev in range(grp + 1):
                    n_out = S + 16 - 2 * half + 1
                    if g:
                        pool.wait_ge(gstep, g)
                    dst = pw[lev % 2]
                    nc.gpsimd.tensor_tensor(dst[:, 0:n_out], src[:, 0:n_out], src[:, half:half + n_out], ALU.add).then_inc(gstep, 1)
                    g += 1
                    src, half = dst[:], 2 * half
                off = 8 - w // 2
                pool.wait_ge(gstep, g)
                nc.gpsimd.tensor_tensor(pd[:, grp, :], src[:, off:off + S], icnt[:, grp, :], ALU.mult).then_inc(gstep, 1)
                g += 1
                pool.wait_ge(gstep, g)
                nc.gpsimd.tensor_tensor(pd[:, grp, :], pd[:, grp, :], pu[:, grp, 8:8 + S], ALU.subtract).then_inc(p_done, 1)

            def gated_ffn(layer):
                n0 = AT[f"ff2_{layer}"][0]
                with pool.Fori(0, 2) as i:
                    for u in range(12):
                        low(n0 + u, i * 12 + (n0 + u))
                lows(n0 + 24, n0 + 34)

            lows(AT["ev_out"][0] + 1, AT["ff2_0"][0])
            gated_ffn(0)
            lows(AT["od_in"][0], AT["od_out"][0] + 1)
            pool.wait_ge(gain_in, 16)
            pool.wait_ge(o_sig, 4)
            for h in range(ML_H + 1):
                for r in range(8 * h, 8 * h + 8 if h < ML_H else 8 * h):
                    d, j = r // 4 % 2, r % 4
                    pool.wait_ge(l_w, r + 1)
                    diag = wt[r % WT_RING][:, j * P:(j + 1) * P]
                    sign = 1 if d == 0 else -1
                    nc.gpsimd.affine_select(out=diag, in_=diag, compare_op=ALU.is_ge, fill=0.0, base=0,
                                            pattern=[[sign, P]], channel_multiplier=-sign).then_inc(l_wm, 1)
                if h < ML_H:
                    hv = slice(h * P, (h + 1) * P)
                    nc.gpsimd.tensor_tensor(mo[:, :, hv], mo[:, :, hv],
                                            hgain[:, hv].rearrange("p (a c) -> p a c", a=1).to_broadcast([P, TB, P]),
                                            ALU.mult).then_inc(gstep, 1)
                if h:
                    hv = slice((h - 1) * P, h * P)
                    pool.wait_ge(n_sq, h)
                    pool.wait_ge(gstep, POOL_STEPS + h)
                    nc.gpsimd.tensor_tensor(hs[:, :, hv], hs[:, :, hv], mo[:, :, hv], ALU.mult).then_inc(n_g, 1)
            lows(AT["od_out"][0] + 1, AT["ff2_1"][0])
            gated_ffn(1)

        @block.scalar
        def _(act):
            acts = [0]

            def chain(ins):
                acts[0] += 1
                ins.then_inc(astep, 1)
                act.wait_ge(astep, acts[0])

            def high(n, i=None, du=0, db=0):
                if n >= N_UNITS:
                    return
                _, _, kc, _, c, _ = UNITS[n]
                act.wait_ge(raw_in[n % 2], add(None if i is None else i * (8 * du), 16 * (n // 2 + 1)))
                if n >= 2:
                    act.wait_ge(blk_done, add(None if i is None else i * db, BLOCK0[n - 1]))
                nc.scalar.activation(wH[n % 2][:, 0:kc, 0:c], raw[n % 2][:, 0:kc, 0:c], ACT.Copy).then_inc(w_hi, 1)

            def squares(name, ready, gain=None):
                q = SQ0[name]
                for j in range(KC):
                    act.wait_ge(*ready(j))
                    for g in range(1 if gain is None else 2):
                        if q >= 2:
                            act.wait_ge(sq_added, q - 1)
                        scale = gain(j) if g else 1.0
                        nc.scalar.activation(sq[q % 2][:], xT[:, j, :], ACT.Square, scale=scale).then_inc(sq_done, 1)
                        q += 1
                nc.scalar.activation(warm, eps, ACT.Sqrt)

            def roots(name):
                act.wait_ge(sum_done, NORMS[name])
                act.wait_ge(inv_done, NORMS[name])
                nc.scalar.activation(root, ps[6][:, 0:4], ACT.Sqrt, bias=eps, scale=1.0 / D).then_inc(root_done, 1)

            def high_op(q, dstH, src, wait, bias=None):
                act.wait_ge(*wait)
                if bias is None:
                    nc.scalar.activation(dstH, src, ACT.Copy).then_inc(op_hi, 1)
                else:
                    nc.scalar.activation(dstH, src, ACT.Identity, bias=bias).then_inc(op_hi, 1)

            tq = [0]

            def norm_high(q0, j, shift=None):
                tq[0] += 1
                high_op(q0 + j, hnH[:, j, :], T[(q0 + j) % 2][:], (op_t, tq[0]), None if shift is None else shift(j))

            def norm_highs(q0, shift=None):
                for j in range(KC):
                    norm_high(q0, j, shift)

            def attention(kind):
                c = ATT[kind]
                ns = c["heads"] * TB
                width = {"fox": None, "cross": M_MEM, "grid": S}[kind]
                for s in range(ns + 7):
                    g = c["step0"] + s
                    if kind == "fox":
                        h = 0 if s == 0 else (s + 2) // 4 if s % 4 == 2 else FOX_H
                        if h < FOX_H:
                            act.wait_ge(f_bc, h + 1)
                            if h >= 2:
                                act.wait_ge(mx_done, 4 * (h - 1))
                            nc.scalar.activation(fbc[h % 2][:], ps[2 + h % 2][:], ACT.Copy).then_inc(f_bcs, 1)
                    if s < ns:
                        i = s % TB
                        w = (i + 1) * P if kind == "fox" else width
                        act.wait_ge(mx_done, g + 1)
                        if kind == "fox":
                            src = pr[g % PR_RING][:, 0:w]
                        else:
                            src = ps[4 + g % 2][:, 0:w]
                            act.wait_ge(tp_done, g - PR_RING + 1)
                        m = g % PR_RING
                        nc.scalar.activation(pr[m][:, 0:w], src, ACT.Exp, bias=nmax[:, m:m + 1],
                                             accum_out=rsum[:, m:m + 1]).then_inc(ex_done, 1)
                    if kind == "fox" and s == 8:
                        act.wait_ge(blk_taken, TAKEN[BLOCK0[AT["out"][0]]])
                        nc.scalar.activation(gq[:], gq[:], ACT.Silu).then_inc(h_act, 1)
                        nc.scalar.activation(gg[:], gg[:], ACT.Silu).then_inc(h_act, 1)
                        nc.scalar.activation(gk[:], gk[:], ACT.Sigmoid).then_inc(h_act, 1)
                    if kind == "fox" and s == 16:
                        for hh in range(HG_H):
                            act.wait_ge(h_fk, hh + 1)
                            nc.scalar.activation(lnf[:, hh, :], lnf[:, hh, :], ACT.Ln).then_inc(h_ln, 1)
                    t = s - 3
                    if 0 <= t < ns:
                        h, i = t // TB, t % TB
                        nj = (i + 1) if kind == "fox" else width // P
                        act.wait_ge(tp_done, c["step0"] + t + 1)
                        if i == 0 and h >= 2:
                            act.wait_ge(pv_done, c["pv0"] + c["pvh"] * (h - 1))
                        nc.scalar.activation(pT[h % 2][:, 0:nj, i * P:(i + 1) * P],
                                             ps[6 + (c["step0"] + t) % 2][:, 0:nj * P].rearrange("p (j t) -> p j t", j=nj),
                                             ACT.Copy).then_inc(pt_done, 1)
                    for o in outputs(kind, s - 5):
                        act.wait_ge(pv_done, c["pv0"] + (o + 1 if kind == "cross" else 2 * o + 2))
                        nc.scalar.activation(uH[:, c["col0"] + o, :], ps[o % 2][:], ACT.Copy).then_inc(op_hi, 1)

            act.wait_ge(setup_d, 1)
            for tb in range(TB):
                act.wait_ge(x_in[tb], 16)
                chain(nc.scalar.activation(xdump[:], xtok[:, tb, :], ACT.Square, accum_out=msq[:, tb:tb + 1]))
            nc.scalar.activation(root, msq, ACT.Sqrt, bias=eps, scale=1.0 / D).then_inc(root_done, 1)
            high(0)
            norm_highs(Q0["mix_norm"])
            act.wait_ge(vec_cols, 2)
            nc.scalar.activation(condc, cols[:, V_C:V_C + 8], ACT.Silu).then_inc(setup, 1)
            act.wait_ge(dstep, LB_SHIFTED)
            nc.scalar.activation(lbt[:, 8:16], lbt[:, 0:8], ACT.Exp).then_inc(setup, 1)
            for u, n in enumerate(range(*ranges("in"))):
                high(n + 1)
                if u == 8:
                    act.wait_ge(blk_taken, TAKEN[BLOCK0[AT["in"][0]] + 13])
                    chain(nc.scalar.activation(frow[1][:], fz[:], ACT.Abs))
                    chain(nc.scalar.activation(frow[1][:], frow[1][:], ACT.Exp, scale=-1.0))
                    nc.scalar.activation(frow[1][:], frow[1][:], ACT.Ln, bias=ones[0:FOX_H, 0:1]).then_inc(f_l, 1)
            attention("fox")
            v = 0
            for h in range(HG_H):
                for l in range(len(HG_LEVELS)):
                    act.wait_ge(h_d, v + 1)
                    nc.scalar.activation(dd[v % HG_RING][:], dd[v % HG_RING][:], ACT.Exp).then_inc(h_e, 1)
                    v += 1
                    if l == 2:
                        if h:
                            act.wait_ge(h_qb, h)
                            act.wait_ge(h_st, 3 * h)
                        nc.scalar.activation(eb[:], gb[:, h, :], ACT.Exp).then_inc(h_eb, 1)
                        act.wait_ge(h_t, h + 1)
                        nc.scalar.activation(ed[:], ed[:], ACT.Exp).then_inc(h_eb, 1)
                act.wait_ge(h_kt, h + 1)
                if h:
                    act.wait_ge(h_sp, h)
                nc.scalar.activation(kdT[:], ps[6][:, 0:384].rearrange("p (c d) -> p c d", c=3), ACT.Copy).then_inc(h_kts, 1)
            hr = [dd[0], dd[1], kt[0], kt[1]]
            act.wait_ge(h_pl, 8 * HG_H)
            act.wait_ge(h_q, queries(len(HG_LEVELS) * HG_H - 1))
            for h in range(HG_H):
                act.wait_ge(h_os, h + 1)
                nc.scalar.activation(hr[h][:], ho[:, h, :], ACT.Square).then_inc(h_sq, 1)
            nc.scalar.activation(warm, eps, ACT.Sqrt)
            act.wait_ge(h_sum, HG_H)
            nc.scalar.activation(hstat[:, 0:16], ps[4][:, 0:16], ACT.Sqrt, bias=eps, scale=1.0 / P).then_inc(h_rs, 1)
            for h in range(HG_H):
                tq[0] += 1
                high_op(Q0["mix"] + 4 + h, uH[:, 4 + h, :], T[h % 2][:], (op_t, tq[0]))
            n = AT["out"][0]
            high(n + 1)
            act.wait_ge(mem_in, 32)
            for mb in range(2):
                chain(nc.scalar.activation(mdump[:], mtok[:, mb, :], ACT.Square, accum_out=mstat[:, mb:mb + 1]))
            nc.scalar.activation(mstat[:, 4:6], mstat[:, 0:2], ACT.Sqrt, bias=eps, scale=1.0 / D).then_inc(m_root, 1)
            high(n + 2)
            for half in range(2):
                high(n + 3 + half)
                for j in range(4 * half, 4 * half + 4):
                    high_op(Q0["mem"] + j, memH[:, j, :], mT[j % 2][:], (m_t, j + 1))
            b = BLOCK0[n]
            squares("x", lambda j: (blk_taken, TAKEN[b + j + 1]))
            n = AT["xkv"][0]
            high(n + 1)
            high(n + 2)
            roots("x")
            for u in range(2, 8):
                high(n + u + 1)
                if u >= 4:
                    norm_high(Q0["x_norm"], 2 * (u - 4))
                    norm_high(Q0["x_norm"], 2 * (u - 4) + 1)
            for n in range(*ranges("xq")):
                high(n + 1)
            attention("cross")
            for n in range(*ranges("xo")):
                high(n + 1)
            b = BLOCK0[AT["xo"][0]]
            squares("ff1", lambda j: (blk_taken, TAKEN[b + j + 1]))
            high(AT["ff1"][0] + 1)
            roots("ff1")
            norm_highs(Q0["ff1_norm"])
            n0, b0, q0 = AT["ff1"][0], AT["ff1"][1], Q0["ff1_u"]
            t0 = TAKEN[b0]
            def squared_relu(i, last=False):
                for u in range(8):
                    if u < 4:
                        for c in range(2):
                            act.wait_ge(blk_done, i * 16 + (b0 + 2 * u + c + 1))
                            act.wait_ge(blk_taken, i * 16 + (t0 + 2 * u + c - 1))
                            nc.scalar.activation(R[c][:], ps[(b0 + 2 * u + c) % 4][:], ACT.Relu).then_inc(relu_done, 1)
                    if not (last and u == 7):
                        high(n0 + u + 2, i, 8, 16)
                    if u < 4:
                        for c in range(2):
                            act.wait_ge(blk_taken, i * 16 + (t0 + 2 * u + c + 1))
                            nc.scalar.activation(uH[:, 2 * u + c, :], T[(q0 + c) % 2][:], ACT.Copy).then_inc(op_hi, 1)

            with act.Fori(0, 3) as i:
                squared_relu(i)
            squared_relu(3, True)
            squares("ev", lambda j: (blk_taken, TAKEN[AT["ff1"][1] + 64 - 8 + j + 1]),
                    lambda j: cols[:, V_FINAL + j:V_FINAL + j + 1])
            high(AT["ev_in"][0] + 1)
            roots("ev")
            act.wait_ge(e_ms, 1)
            nc.scalar.activation(root, nt1, ACT.Sqrt).then_inc(e_root, 1)
            norm_highs(Q0["ev_norm"], lambda j: mod[:, j:j + 1])
            n = AT["ev_in"][0]
            b = TAKEN[BLOCK0[n]]

            def head_norm_square(j):
                act.wait_ge(blk_taken, b + j + 1)
                nc.scalar.activation(gs[:, j, :], evq[:, j, :], ACT.Square).then_inc(g_sq, 1)

            def head_norm_roots(js):
                for j in js:
                    act.wait_ge(g_sum, j + 1)
                    chain(nc.scalar.activation(gs[:, j, :], ps[4 + j % 4][:], ACT.Ln, bias=eps, scale=1.0 / 64))
                for j in js:
                    nc.scalar.activation(gs[:, j, :], gs[:, j, :], ACT.Exp, scale=-0.5).then_inc(g_rs, 1)

            for u in range(1, 3):
                high(n + u + 1)
            for j in range(4):
                head_norm_square(j)
            high(n + 4)
            head_norm_square(4)
            head_norm_roots(range(4))
            high(n + 5)
            head_norm_roots(range(4, 5))
            for j in range(2):
                act.wait_ge(g_dup, j + 1)
                nc.scalar.activation(kdup[:, j, :], ps[(7, 4)[j]][:], ACT.Copy).then_inc(g_kd, 1)
            attention("grid")
            for j in range(4):
                tq[0] += 1
                high_op(Q0["ev_mix"] + 4 + j, uH[:, j, :], T[j % 2][:], (op_t, tq[0]))
            for n in range(*ranges("ev_out")):
                high(n + 1)

            def gated_ffn(layer):
                name = f"ff2_{layer}"
                n0, b0 = AT[name]
                q0 = Q0[name + "_u"]
                t0, s0 = TAKEN[b0], SILUS[b0]

                def pair(p, i=None):
                    last = 0 if i is not None else 1
                    n, b = n0 + 24 * last + 2 * p, b0 + 48 * last + 4 * p
                    taken = None if i is None else i * 16
                    for c in range(2):
                        act.wait_ge(blk_done, add(None if i is None else i * 24, b + c + 1))
                        act.wait_ge(blk_taken, add(taken, TAKEN[b] - 1 + c))
                        nc.scalar.activation(R[c][:], ps[(b + c) % 4][:], ACT.Silu).then_inc(silu_done, 1)
                    high(n + 2, i, 12, 24)
                    for c in range(2):
                        act.wait_ge(blk_taken, add(taken, TAKEN[b + 2 + c + 1]))
                        nc.scalar.activation(uH[:, 2 * p + c, :], T[(q0 + c) % 2][:], ACT.Copy).then_inc(op_hi, 1)
                    high(n + 3, i, 12, 24)

                with act.Fori(0, 2) as i:
                    for p in range(4):
                        pair(p, i)
                    for u in range(8, 12):
                        high(n0 + u + 2, i, 12, 24)
                for p in range(3):
                    pair(p)
                for n in range(n0 + 30, n0 + 33):
                    high(n + 2)

            def gated_norm(name, b, part, layer):
                squares(name, lambda j: (blk_taken, TAKEN[b + j + 1]))
                high(AT[{"od": "od_in"}.get(name, name)][0] + 1)
                roots(name)
                norm_highs(Q0[name + "_norm"], lambda j: mod[:, layer * 48 + part * 8 + j:layer * 48 + part * 8 + j + 1])

            gated_norm("ff2_0", BLOCK0[AT["ev_out"][0]], 3, 0)
            gated_ffn(0)
            gated_norm("od", BLOCK0[AT["od_in"][0]] - 8, 0, 1)
            n = AT["od_in"][0]

            def conv_silus(js):
                for j in js:
                    act.wait_ge(c_y, j + 1)
                    nc.scalar.activation(cy[:, j, :], cy[:, j, :], ACT.Silu).then_inc(c_silu, 1)

            def output_gate(u):
                act.wait_ge(blk_taken, TAKEN[BLOCK0[n + 9 + u] + 2])
                nc.scalar.activation(mo[:, :, u * UC:(u + 1) * UC], mo[:, :, u * UC:(u + 1) * UC], ACT.Sigmoid).then_inc(o_sig, 1)

            for u in range(2, 8):
                high(n + u)
            act.wait_ge(r_sel, 1)
            chain(nc.scalar.activation(Frow[:], ps[5][0:64, :], ACT.Abs))
            chain(nc.scalar.activation(Frow[:], Frow[:], ACT.Exp, scale=-1.0))
            nc.scalar.activation(Frow[:], Frow[:], ACT.Ln, bias=ones[0:64, 0:1]).then_inc(r_ln, 1)
            high(n + 8)
            act.wait_ge(r_rows, 1)
            nc.scalar.activation(erow[:], erow[:], ACT.Exp, scale=-1.0).then_inc(r_em, 1)
            high(n + 9)
            conv_silus(range(0, 2))
            high(n + 10)
            act.wait_ge(r_tr, 2)
            nc.scalar.activation(ccol[:], ps[6][:, 0:256].rearrange("p (a b) -> p a b", a=TB), ACT.Copy).then_inc(r_cols, 1)
            nc.scalar.activation(ecol[:], ps[7][:, 0:256].rearrange("p (a b) -> p a b", a=TB), ACT.Copy).then_inc(r_cols, 1)
            conv_silus(range(2, 5))
            high(n + 11)
            conv_silus(range(5, 8))
            high(n + 12)
            output_gate(0)
            output_gate(1)
            high(n + 13)
            output_gate(2)
            output_gate(3)
            act.wait_ge(r_cols, 2)

            def head_squares(h):
                act.wait_ge(l_h, 2 * h + 2)
                if h >= 2:
                    act.wait_ge(n_sum, h - 1)
                nc.scalar.activation(hsq[h % 2][:].rearrange("p (t v) -> p t v", t=TB), hs[:, :, h * P:(h + 1) * P],
                                     ACT.Square).then_inc(n_sq, 1)

            for h in range(ML_H):
                for d in range(2):
                    for j in range(TB):
                        r = 8 * h + 4 * d + j
                        lo, hi = (j * P, S) if d == 0 else (0, (j + 1) * P)
                        act.wait_ge(l_bc, 2 * h + d + 1)
                        if r >= WT_RING:
                            act.wait_ge(l_a, r - WT_RING + 1)
                        row = h + 32 * d
                        nc.scalar.activation(wt[r % WT_RING][:, lo:hi], ps[4 + d][:, lo:hi], ACT.Exp,
                                             bias=ccol[:, j, row:row + 1]).then_inc(l_w, 1)
                if h >= 2:
                    head_squares(h - 2)
            head_squares(ML_H - 2)
            head_squares(ML_H - 1)
            nc.scalar.activation(warm, eps, ACT.Sqrt)
            act.wait_ge(n_sum, ML_H)
            nc.scalar.activation(hrs, hstat, ACT.Sqrt, bias=eps, scale=1.0 / ML_V).then_inc(n_rs, 1)
            for j in range(KC):
                high_op(Q0["od_mix"] + j, uH[:, j, :], ps[4 + j % 4][:], (n_tr, j + 1))
            for n in range(*ranges("od_out")):
                high(n + 1)
            gated_norm("ff2_1", BLOCK0[AT["od_out"][0]], 3, 1)
            gated_ffn(1)

        @block.vector
        def _(dve):
            steps = [0]

            def chain(ins):
                steps[0] += 1
                ins.then_inc(dstep, 1)
                dve.wait_ge(dstep, steps[0])

            def norm_add(name, j, twice=False):
                for g in range(2 if twice else 1):
                    q = SQ0[name] + (2 * j + g if twice else j)
                    acc = (ssum, gsum)[g]
                    if j == 0 and g == 0:
                        dve.wait_ge(sum_done, NORMS[name] - 1)
                    dve.wait_ge(sq_done, q + 1)
                    if j == 0:
                        nc.vector.tensor_copy(acc[:], sq[q % 2][:]).then_inc(sq_added, 1)
                    else:
                        dve.wait_ge(sq_added, q)
                        nc.vector.tensor_tensor(acc[:], acc[:], sq[q % 2][:], ALU.add).then_inc(sq_added, 1)

            def residual_and_sums(b, name, gate=None, twice=False):
                for j in range(KC):
                    residual(b + j, j, gate)
                    if j == 5:
                        for jj in range(6):
                            norm_add(name, jj, twice)
                    elif j > 5:
                        norm_add(name, j, twice)

            def newton(r, mean, t):
                chain(nc.vector.tensor_tensor(t, r, r, ALU.mult))
                chain(nc.vector.scalar_tensor_tensor(out=t, in0=mean, scalar=-0.5, in1=t, op0=ALU.mult, op1=ALU.mult))
                return nc.vector.scalar_tensor_tensor(out=r, in0=t, scalar=1.5, in1=r, op0=ALU.add, op1=ALU.mult)

            def inverse_root(name):
                if NORMS[name]:
                    dve.wait_ge(root_done, NORMS[name] + 1)
                    dve.wait_ge(bc_done, NORMS[name])
                else:
                    dve.wait_ge(astep, TB)
                mean = (ps[6][:, 0:4] if NORMS[name] else msq, 1.0 / D)
                chain(nc.vector.tensor_scalar(nt1, *mean, EPS, ALU.mult, ALU.add))
                dve.wait_ge(root_done, NORMS[name] + 1)
                chain(nc.vector.reciprocal(rootinv, root))
                newton(rootinv, nt1, nt2).then_inc(inv_done, 1)

            def low_op(q, dstL, src, dstH, bias=None):
                dve.wait_ge(op_hi, q + 1)
                if bias is None:
                    nc.vector.tensor_tensor(dstL, src, dstH.bitcast(F32), ALU.subtract).then_inc(op_lo, 1)
                else:
                    nc.vector.scalar_tensor_tensor(out=dstL, in0=src, scalar=bias, in1=dstH.bitcast(F32),
                                                   op0=ALU.add, op1=ALU.subtract).then_inc(op_lo, 1)

            def normed_steps(name, gain, q0, shift=None, bank=4):
                dve.wait_ge(bc_done, NORMS[name] + 1)

                def low(j):
                    low_op(q0 + j, hnL[:, j, :], T[(q0 + j) % 2][:], hnH[:, j, :], None if shift is None else shift(j))

                for j in range(KC):
                    if q0 + j >= 2:
                        dve.wait_ge(op_lo, q0 + j - 1)
                    ins = nc.vector.scalar_tensor_tensor(out=T[(q0 + j) % 2][:], in0=xT[:, j, :], scalar=gain(j), in1=ps[bank][:],
                                                         op0=ALU.mult, op1=ALU.mult)
                    ins.then_inc(op_t, 1)
                    if j:
                        low(j - 1)
                    if j % 2:
                        yield
                low(KC - 1)
                yield

            def normed(name, gain, q0, shift=None, bank=4):
                inverse_root(name)
                for _ in normed_steps(name, gain, q0, shift, bank):
                    pass

            def col(c0):
                return lambda j: cols[:, c0 + j:c0 + j + 1]

            def take(b, out_ap, in_ap, scale=None):
                dve.wait_ge(blk_done, b + 1)
                if scale is None:
                    nc.vector.tensor_copy(out_ap, in_ap).then_inc(blk_taken, 1)
                else:
                    nc.vector.tensor_scalar(out_ap, in_ap, scale, None, ALU.mult).then_inc(blk_taken, 1)

            def residual(b, j, gate=None, value=None):
                dve.wait_ge(blk_done, (b if value is None else value) + 1)
                if gate is None:
                    nc.vector.tensor_tensor(xT[:, j, :], ps[b % 4][:], xT[:, j, :], ALU.add).then_inc(blk_taken, 1)
                else:
                    nc.vector.scalar_tensor_tensor(out=xT[:, j, :], in0=ps[b % 4][:], scalar=gate(j), in1=xT[:, j, :],
                                                   op0=ALU.mult, op1=ALU.add).then_inc(blk_taken, 1)

            def attention(kind):
                c = ATT[kind]
                ns = c["heads"] * TB
                width = {"fox": None, "cross": M_MEM, "grid": S}[kind]
                for s in range(ns + 8):
                    g = c["step0"] + s
                    if s < ns:
                        h, i = s // TB, s % TB
                        m = g % PR_RING
                        dve.wait_ge(sc_done, g + 1)
                        if kind == "fox":
                            w = (i + 1) * P
                            if g >= PR_RING:
                                dve.wait_ge(tp_done, g - PR_RING + 1)
                            dve.wait_ge(f_bcs, h + 1)
                            chain(nc.vector.tensor_tensor_reduce(pr[m][:, 0:w], ps[4 + g % 2][:, 0:w], fbc[h % 2][:, 0:w], 1.0, -3.0e38,
                                                                 ALU.subtract, ALU.max, nmraw[:, m:m + 1]))
                        else:
                            chain(nc.vector.tensor_reduce(nmraw[:, m:m + 1], ps[4 + g % 2][:, 0:width], AX, ALU.max))
                        nc.vector.tensor_scalar(nmax[:, m:m + 1], nmraw[:, m:m + 1], -1.0, None, ALU.mult).then_inc(mx_done, 1)
                    if 1 <= s <= ns:
                        m = (g - 1) % PR_RING
                        w = ((s - 1) % TB + 1) * P if kind == "fox" else width
                        dve.wait_ge(ex_done, g)
                        chain(nc.vector.reciprocal(rinv[:, m:m + 1], rsum[:, m:m + 1]))
                        nc.vector.tensor_scalar(pr[m][:, 0:w], pr[m][:, 0:w], rinv[:, m:m + 1], None, ALU.mult).then_inc(pn_done, 1)
                    if kind == "fox" and s >= 10:
                        next(hgrn_gates, None)
                    for o in outputs(kind, s - 6):
                        low_op(c["q0"] + o, uL[:, c["col0"] + o, :], ps[o % 2][:], uH[:, c["col0"] + o, :])

            nc.vector.memset(eps, EPS).then_inc(setup_d, 1)
            dve.wait_ge(cst_in, 16)
            nc.vector.tensor_copy(identb[:], ident).then_inc(setup_d, 1)
            nc.vector.tensor_copy(causalb[:], cst[:, C_CAUSAL, :]).then_inc(setup_d, 1)
            for j in range(KC):
                dve.wait_ge(x_tr, j + 1)
                nc.vector.tensor_copy(xT[:, j, :], ps[6 + j % 2][:]).then_inc(x_cols, 1)
            dve.wait_ge(vec_tr, 2)
            nc.vector.tensor_copy(cols[:, 0:V_ROWS], ps[5][:, 0:V_ROWS]).then_inc(vec_cols, 1)
            nc.vector.tensor_copy(adab[:], ps[5][:, 128:224]).then_inc(vec_cols, 1)
            dve.wait_ge(vec_cols, 2)
            dve.wait_ge(x_cols, KC)
            normed("mix", col(V_MIX), Q0["mix_norm"])
            dve.sem_inc(ada_acc, ADA_RING)
            dve.sem_inc(mod_done, 1)
            l0, l1 = cols[:, V_LB:V_LB + 4], cols[:, V_LB + 4:V_LB + 8]
            chain(nc.vector.tensor_tensor(lbt[:, 8:12], l0, l1, ALU.max))
            chain(nc.vector.tensor_tensor(lbt[:, 0:4], l0, lbt[:, 8:12], ALU.subtract))
            chain(nc.vector.tensor_tensor(lbt[:, 4:8], l1, lbt[:, 8:12], ALU.subtract))
            assert steps[0] == LB_SHIFTED
            dve.wait_ge(setup, 2)
            chain(nc.vector.tensor_tensor(lbt[:, 0:4], lbt[:, 8:12], lbt[:, 12:16], ALU.add))
            chain(nc.vector.reciprocal(lbt[:, 4:8], lbt[:, 0:4]))
            chain(nc.vector.tensor_tensor(lb, lbt[:, 8:12], lbt[:, 4:8], ALU.mult))
            chain(nc.vector.tensor_scalar(omlb, lb, -1.0, 1.0, ALU.mult, ALU.add))
            chain(nc.vector.tensor_scalar(small[:, 148:149], cols[:, V_QG:V_QG + 1], GA_SCALE, None, ALU.mult))

            n, b = AT["in"]
            for j in range(4):
                take(b + j, fq[:, j, :], ps[(b + j) % 4][:], FOX_D ** -0.5)
            for j in range(4):
                take(b + 4 + j, fk[:, j, :], ps[(b + 4 + j) % 4][:])

            def take_tokens(b, dst, c0, width=UC):
                for half in range(2):
                    take(b + half, dst[:, 2 * half:2 * half + 2, c0:c0 + width],
                         ps[(b + half) % 4][:, 0:2 * width].rearrange("p (a c) -> p a c", a=2))

            for u in range(2):
                take_tokens(b + 8 + 2 * u, fv, u * UC)
            fb = b + 12
            dve.wait_ge(blk_done, fb + 1)
            nc.vector.tensor_scalar(fz[:], ps[fb % 4][0:FOX_H, :], fbias[0:FOX_H, :], None, ALU.add).then_inc(blk_taken, 1)
            for j in range(4):
                take(fb + 1 + j, gq[:, j, :], ps[(fb + 1 + j) % 4][:])
            for j in range(4):
                take(fb + 5 + j, gk[:, j, :], ps[(fb + 5 + j) % 4][:])
            dve.wait_ge(f_l, 1)
            chain(nc.vector.tensor_scalar(frow[2][:], fz[:], 0.0, None, ALU.min))
            chain(nc.vector.tensor_tensor(frow[2][:], frow[2][:], frow[1][:], ALU.subtract))
            nc.vector.tensor_tensor_scan(frow[0][:], ones[0:FOX_H, 0:1].to_broadcast([FOX_H, S]), frow[2][:], 0.0,
                                         ALU.mult, ALU.add).then_inc(f_rows, 1)
            for u in range(2):
                take_tokens(fb + 9 + 2 * u, gi, u * UC)
            for j in range(4):
                take(fb + 13 + j, gg[:, j, :], ps[(fb + 13 + j) % 4][:])

            def gate_steps():
                chain(nc.vector.memset(rmask[:], 1.0))
                chain(nc.vector.memset(rmask[:].rearrange("p (c t) -> p c t", c=TB)[:, :, 0:1], 0.0))
                yield
                dve.wait_ge(h_act, 3)
                for h in range(HG_H):
                    chain(nc.vector.tensor_scalar(lnf[:, h, :], gk[:, h, :], omlb[:, h:h + 1], lb[:, h:h + 1], ALU.mult, ALU.add))
                    nc.vector.tensor_scalar(gk[:, h, :], lnf[:, h, :], -1.0, 1.0, ALU.mult, ALU.add).then_inc(h_fk, 1)
                    yield
                for _ in range(6):
                    yield
                for h in range(HG_H):
                    dve.wait_ge(h_ln, h + 1)
                    nc.vector.tensor_tensor_scan(gb[:, h, :], rmask[:], lnf[:, h, :], 0.0, ALU.mult, ALU.add).then_inc(h_b, 1)
                    yield

            hgrn_gates = gate_steps()
            attention("fox")
            for _ in hgrn_gates:
                pass
            levels = [(h, l) for h in range(HG_H) for l in range(len(HG_LEVELS))]

            def level_exponent(v):
                if v >= len(levels):
                    return
                h, l = levels[v]
                L = HG_LEVELS[l]
                if v >= HG_RING:
                    dve.wait_ge(h_q, queries(v - HG_RING))
                    dve.wait_ge(h_k, v - HG_RING + 1)
                dve.wait_ge(h_b, h + 1)
                x = gb[:, h, :].rearrange("p (n t) -> p n t", t=2 * L)
                to = dd[v % HG_RING][:].rearrange("p (n t) -> p n t", t=2 * L)
                mid = x[:, :, L - 1:L].to_broadcast([P, S // (2 * L), L])
                nc.vector.tensor_tensor(to[:, :, 0:L], mid, x[:, :, 0:L], ALU.subtract)
                nc.vector.tensor_tensor(to[:, :, L:2 * L], x[:, :, L:2 * L], mid, ALU.subtract).then_inc(h_d, 1)

            def level_q(v):
                h, l = levels[v]
                if l in HG_BY_POOL:
                    return
                dve.wait_ge(h_e, v + 1)
                if v >= HG_RING:
                    dve.wait_ge(h_pl, products(v - HG_RING))
                nc.vector.tensor_tensor(qt[v % HG_RING][:], gq[:, h, :], dd[v % HG_RING][:], ALU.mult).then_inc(h_q, 1)

            def level_scores(e):
                h, l = e // 8, e % 8
                dve.wait_ge(h_pl, e + 1)
                if e:
                    dve.wait_ge(h_at, e)
                if l == 0 and h >= 2:
                    dve.wait_ge(h_o, h - 1)
                nc.vector.copy_predicated(at_[h % 2][:],
                                          lvl[:, l, :].bitcast(U32).rearrange("p (a c) -> p a c", a=1).to_broadcast([P, TB, P]),
                                          ps[2 + e % 4][:].rearrange("p (c t) -> p c t", c=TB)).then_inc(h_at, 1)

            def states(h):
                dve.wait_ge(h_sp, h + 1)
                for c in range(3):
                    part = ps[7][:, c * P:(c + 1) * P]
                    if c == 0:
                        nc.vector.tensor_copy(st[:, 0, :], part).then_inc(h_st, 1)
                    else:
                        dve.wait_ge(h_st, 3 * h + c)
                        nc.vector.scalar_tensor_tensor(out=st[:, c, :], in0=st[:, c - 1, :], scalar=eb[:, c * P + P - 1:c * P + P],
                                                       in1=part, op0=ALU.mult, op1=ALU.add).then_inc(h_st, 1)

            def head_done(h):
                dve.wait_ge(h_o, h + 1)
                nc.vector.tensor_copy(ho[:, h, :], ps[h % 2][:]).then_inc(h_os, 1)

            level_exponent(0)
            level_exponent(1)
            v = 0
            for h in range(HG_H):
                for l in range(len(HG_LEVELS)):
                    level_exponent(v + 2)
                    level_q(v)
                    if v == 0:
                        for i in range(2):
                            chain(nc.vector.memset(at_[i][:], 0.0))
                        dve.wait_ge(lvl_in, 16)
                    if l == 0 and h:
                        level_scores(8 * h - 2)
                        level_scores(8 * h - 1)
                        states(h - 1)
                    elif l:
                        level_scores(8 * h + l - 1)
                    v += 1
                    if l == 1:
                        if h:
                            dve.wait_ge(h_kd, h)
                        x = gb[:, h, :].rearrange("p (c t) -> p c t", c=TB)
                        nc.vector.tensor_tensor(ed[:].rearrange("p (c t) -> p c t", c=TB), x[:, :, P - 1:P].to_broadcast([P, TB, P]),
                                                x, ALU.subtract).then_inc(h_t, 1)
                    if l == 3:
                        if h:
                            head_done(h - 1)
                        dve.wait_ge(h_eb, 2 * h + 1)
                        nc.vector.tensor_tensor(qb[:], gq[:, h, :], eb[:], ALU.mult).then_inc(h_qb, 1)
            level_scores(8 * HG_H - 2)
            level_scores(8 * HG_H - 1)
            states(HG_H - 1)
            head_done(HG_H - 1)
            for h in range(HG_H):
                dve.wait_ge(h_os, h + 1)
                chain(nc.vector.scalar_tensor_tensor(out=gg[:, h, :], in0=ho[:, h, :], scalar=cols[:, V_HG:V_HG + 1],
                                                     in1=gg[:, h, :], op0=ALU.mult, op1=ALU.mult))
            dve.wait_ge(h_rs, 1)
            chain(nc.vector.tensor_scalar(hstat[:, 16:32], ps[4][:, 0:16], 1.0 / P, EPS, ALU.mult, ALU.add))
            chain(nc.vector.reciprocal(hrs[:, 0:16], hstat[:, 0:16]))
            newton(hrs[:, 0:16], hstat[:, 16:32], hrs[:, 16:32]).then_inc(h_inv, 1)
            for h in range(HG_H):
                dve.wait_ge(h_bc, h + 1)
                if h >= 2:
                    dve.wait_ge(op_lo, Q0["mix"] + 4 + h - 1)
                nc.vector.tensor_tensor(T[h % 2][:], ps[(5, 6, 7, 2)[h]][:], gg[:, h, :], ALU.mult).then_inc(op_t, 1)
                low_op(Q0["mix"] + 4 + h, uL[:, 4 + h, :], T[h % 2][:], uH[:, 4 + h, :])
            n, b = AT["out"]

            def memory_chunk(j):
                dve.wait_ge(m_tr, j + 1)
                if j >= 2:
                    dve.wait_ge(op_lo, Q0["mem"] + j - 1)
                nc.vector.tensor_scalar(mT[j % 2][:], ps[4 + j % 4][:, 0:M_MEM], cols[:, V_MEM + j:V_MEM + j + 1], None,
                                        ALU.mult).then_inc(m_t, 1)
                low_op(Q0["mem"] + j, memL[:, j, :], mT[j % 2][:], memH[:, j, :])

            for j in range(KC):
                residual(b + j, j)
                if j == 1:
                    dve.wait_ge(m_root, 1)
                    chain(nc.vector.reciprocal(mstat[:, 2:4], mstat[:, 4:6]))
                    for mb in range(2):
                        nc.vector.tensor_scalar(mtok[:, mb, :], mtok[:, mb, :], mstat[:, 2 + mb:3 + mb], None, ALU.mult).then_inc(m_n, 1)
                if j in (3, 5):
                    for jj in range(2 * j - 6, 2 * j - 2):
                        memory_chunk(jj)
                if j == 5:
                    for jj in range(6):
                        norm_add("x", jj)
                elif j > 5:
                    norm_add("x", j)
            n, b = AT["xkv"]
            steps_x = normed_steps("x", col(V_X), Q0["x_norm"])
            for u in range(8):
                for c in range(2):
                    bb = b + 2 * u + c
                    if u < 4:
                        take(bb, xk[:, 2 * u + c, :], ps[bb % 4][:, 0:M_MEM])
                    else:
                        take(bb, xv[:, c, (u - 4) * UC:(u - 3) * UC], ps[bb % 4][:, 0:UC])
                if u == 1:
                    inverse_root("x")
                if u >= 3:
                    next(steps_x)
            n, b = AT["xq"]
            for j in range(KC):
                take(b + j, xq[:, j, :], ps[(b + j) % 4][:], 1.0 / 16)
            attention("cross")
            n, b = AT["xo"]
            residual_and_sums(b, "ff1")
            normed("ff1", col(V_FF), Q0["ff1_norm"])
            n0, b0 = AT["ff1"]
            q0 = Q0["ff1_u"]
            dve.wait_ge(setup, 1)
            def conditioning(layer, i, m):
                group = ADA_GROUP[layer]
                acc = adacc[m % 2][:]
                dve.wait_ge(ada_in[m % ADA_RING], i * (16 * group // ADA_RING) + 16 * (24 * layer // ADA_RING + m // ADA_RING + 1))
                dve.wait_ge(ada_mm, i * group + (24 * layer + m + 1))
                for k in range(KC):
                    if k == 0:
                        ins = nc.vector.tensor_scalar(acc, adaw[m % ADA_RING][:, 0, :], condc[:, 0:1], None, ALU.mult)
                    else:
                        dve.wait_ge(ada_step, i * (7 * group) + (7 * (24 * layer + m) + k))
                        ins = nc.vector.scalar_tensor_tensor(out=acc, in0=adaw[m % ADA_RING][:, k, :], scalar=condc[:, k:k + 1],
                                                             in1=acc, op0=ALU.mult, op1=ALU.add)
                    ins.then_inc(ada_acc if k == KC - 1 else ada_step, 1)

            def modulations(layer, i):
                n = 2 * ADA_GROUP[layer]
                dve.wait_ge(ada_mm, i * (n // 2) + (24 * layer + n // 2 + 2))
                at = bass.ds(i * n + 48 * layer, n)
                nc.vector.tensor_tensor(mod[:, at], ps[5][:, 0:n], adab[:, at], ALU.add).then_inc(mod_done, 1)

            def plus_one(layer):
                done = (4, 7)[layer]
                dve.wait_ge(mod_done, done)
                half = slice(48 * layer, 48 * layer + 48)
                nc.vector.tensor_scalar(modp[:, half], mod[:, half], 1.0, None, ALU.add).then_inc(mod_done, 1)
                dve.wait_ge(mod_done, done + 1)

            def hidden(u, i):
                for c in range(2):
                    b, q = b0 + 2 * u + c, q0 + 2 * u + c
                    dve.wait_ge(relu_done, i * 8 + (2 * u + c + 1))
                    dve.wait_ge(op_lo, i * 8 + (q - 1))
                    nc.vector.scalar_tensor_tensor(out=T[q % 2][:], in0=ps[b % 4][:], scalar=0.0, in1=R[c][:],
                                                   op0=ALU.max, op1=ALU.mult).then_inc(blk_taken, 1)
                for c in range(2):
                    q = q0 + 2 * u + c
                    dve.wait_ge(op_hi, i * 8 + (q + 1))
                    nc.vector.tensor_tensor(uL[:, 2 * u + c, :], T[q % 2][:], uH[:, 2 * u + c, :].bitcast(F32),
                                            ALU.subtract).then_inc(op_lo, 1)

            with dve.Fori(0, 3) as i:
                for u in range(8):
                    conditioning(0, i, u)
                    if u < 4:
                        hidden(u, i)
                    else:
                        for c in range(2):
                            b = b0 + 2 * u + c
                            residual(b, 2 * (u - 4) + c, None, i * 16 + b)
                modulations(0, i)
            plus_one(0)
            chain(nc.vector.tensor_tensor(gm, modp[:, 8:16], cols[:, V_FINAL:V_FINAL + 8], ALU.mult))
            for u in range(4):
                hidden(u, 3)
            residual_and_sums(b0 + 56, "ev", None, True)

            def mcol(t, layer, part):
                return lambda j: t[:, layer * 48 + part * 8 + j:layer * 48 + part * 8 + j + 1]

            inverse_root("ev")
            dve.wait_ge(inv_done, NORMS["ev"] + 1)
            chain(nc.vector.tensor_tensor(msq, rootinv, rootinv, ALU.mult))
            chain(nc.vector.scalar_tensor_tensor(out=nt1, in0=ps[6][:, 4:8], scalar=1.0 / D, in1=msq, op0=ALU.mult, op1=ALU.mult))
            nc.vector.tensor_scalar(nt1, nt1, EPS, None, ALU.add).then_inc(e_ms, 1)
            dve.wait_ge(e_root, 1)
            chain(nc.vector.reciprocal(msq, root))
            chain(newton(msq, nt1, nt2))
            nc.vector.tensor_tensor(msq, msq, rootinv, ALU.mult).then_inc(e_inv, 1)
            for _ in normed_steps("ev", lambda j: gm[:, j:j + 1], Q0["ev_norm"], mcol(mod, 0, 0), 5):
                pass
            for j in range(KC):
                nc.vector.scalar_tensor_tensor(out=xT[:, j, :], in0=xT[:, j, :], scalar=cols[:, V_FINAL + j:V_FINAL + j + 1],
                                               in1=ps[4][:], op0=ALU.mult, op1=ALU.mult).then_inc(dstep, 1)
                steps[0] += 1
            dve.wait_ge(dstep, steps[0])
            chain(nc.vector.memset(pu[:, :, 0:8], 0.0))
            chain(nc.vector.memset(pu[:, :, 8 + S:S + 24], 0.0))
            n, b = AT["ev_in"]
            for j in range(5):
                take(b + j, evq[:, j, :], ps[(b + j) % 4][:])
            take(b + 5, evv[:], ps[(b + 5) % 4][:].rearrange("p (a c) -> p a c", a=TB))
            dve.wait_ge(ev_in, 64)

            def head_gain(j):
                dve.wait_ge(g_rs, j + 1)
                gain = small[:, 148:149] if j < 4 else cols[:, V_KG:V_KG + 1]
                nc.vector.scalar_tensor_tensor(out=evq[:, j, :], in0=evq[:, j, :], scalar=gain, in1=gs[:, j, :],
                                               op0=ALU.mult, op1=ALU.mult).then_inc(g_n, 1)

            def rotate(i):
                j = ROPE_ORDER[i]
                dve.wait_ge(g_rot, i + 1)
                chain(nc.vector.tensor_tensor(T[i % 2][:], ps[ROPE_BANK[i]][:], sinb[:], ALU.mult))
                chain(nc.vector.tensor_tensor(evq[:, j, :], evq[:, j, :], cosb[:], ALU.mult))
                nc.vector.tensor_tensor(evq[:, j, :], evq[:, j, :], T[i % 2][:], ALU.add).then_inc(g_roped, 1)

            for j in range(4):
                head_gain(j)
            for j in range(2):
                take(b + 6 + j, pu[:, j, 8:8 + S], ps[(b + 6 + j) % 4][:])
            head_gain(4)
            rotate(0)
            take(b + 8, pu[:, 2, 8:8 + S], ps[(b + 8) % 4][:])
            rotate(1)
            rotate(2)
            take(b + 9, pu[:, 3, 8:8 + S], ps[(b + 9) % 4][:])
            rotate(3)
            rotate(4)
            attention("grid")
            for j in range(4):
                dve.wait_ge(p_mm, j + 1)
                nc.vector.tensor_scalar(T[j % 2][:], ps[2 + j % 2][:], cols[:, V_BPOOL + j:V_BPOOL + j + 1],
                                        cols[:, V_SPOOL + j:V_SPOOL + j + 1], ALU.add, ALU.mult).then_inc(op_t, 1)
                low_op(Q0["ev_mix"] + 4 + j, uL[:, j, :], T[j % 2][:], uH[:, j, :])
            n, b = AT["ev_out"]
            residual_and_sums(b, "ff2_0", mcol(mod, 0, 2))

            def gated_ffn(layer):
                name = f"ff2_{layer}"
                n0, b0 = AT[name]
                q0 = Q0[name + "_u"]

                def pair(p, i=None):
                    last = 0 if i is not None else 1
                    blocks, chunks = (None, None) if i is None else (i * 24, i * 8)
                    for c in range(2):
                        b, q = b0 + 48 * last + 4 * p + 2 + c, q0 + 16 * last + 2 * p + c
                        dve.wait_ge(silu_done, add(chunks, SILUS[b - 2] + 1))
                        dve.wait_ge(blk_done, add(blocks, b + 1))
                        dve.wait_ge(op_lo, add(chunks, q - 1))
                        nc.vector.tensor_tensor(T[(q0 + c) % 2][:], ps[b % 4][:], R[c][:], ALU.mult).then_inc(blk_taken, 1)
                    for c in range(2):
                        q = q0 + 16 * last + 2 * p + c
                        dve.wait_ge(op_hi, add(chunks, q + 1))
                        nc.vector.tensor_tensor(uL[:, 2 * p + c, :], T[(q0 + c) % 2][:], uH[:, 2 * p + c, :].bitcast(F32),
                                                ALU.subtract).then_inc(op_lo, 1)

                def cond(i, m):
                    if layer == 0:
                        conditioning(1, i, m)

                with dve.Fori(0, 2) as i:
                    for p in range(4):
                        cond(i, 2 * p)
                        cond(i, 2 * p + 1)
                        pair(p, i)
                    for j in range(KC):
                        if j % 2 == 0:
                            cond(i, 8 + j // 2)
                        residual(b0 + 16 + j, j, mcol(mod, layer, 5), i * 24 + (b0 + 16 + j))
                    if layer == 0:
                        modulations(1, i)
                if layer == 0:
                    plus_one(1)
                for p in range(3):
                    pair(p)
                if layer == 0:
                    residual_and_sums(b0 + 60, "od", mcol(mod, layer, 5))
                else:
                    for j in range(KC):
                        residual(b0 + 60 + j, j, mcol(mod, layer, 5))

            def gated_norm(name, part, layer):
                normed(name, mcol(modp, layer, part + 1), Q0[name + "_norm"], mcol(mod, layer, part))

            gated_norm("ff2_0", 3, 0)
            gated_ffn(0)
            gated_norm("od", 0, 1)
            chain(nc.vector.memset(cz[:, :, 0:2], 0.0))
            chain(nc.vector.memset(cz[:, :, 2 + S:4 + S], 0.0))
            chain(nc.vector.memset(vx[:, :, :, ML_V:ML_V + 1], 1.0))
            n, b = AT["od_in"]
            for j in range(KC):
                take(b + j, cz[:, j, 2:2 + S], ps[(b + j) % 4][:])
            gate_block = b + 8
            dve.wait_ge(blk_done, gate_block + 1)
            dve.wait_ge(op_lo, Q0["od_norm"] + 8)
            nc.vector.tensor_scalar(grow[96:128, :], ps[gate_block % 4][96:128, :], gbias[96:128, :], None, ALU.add).then_inc(blk_taken, 1)

            def take_values(bb, u, half):
                dve.wait_ge(blk_done, bb + 1)
                for tb in range(2):
                    src = ps[bb % 4][:, tb * UC:(tb + 1) * UC].rearrange("p (h v) -> p h v", h=2)
                    ins = nc.vector.tensor_copy(vx[:, 2 * half + tb, 2 * u:2 * u + 2, 0:ML_V], src)
                ins.then_inc(blk_taken, 1)

            def gate_rows():
                dve.wait_ge(r_sel, 1)
                chain(nc.vector.tensor_copy(irow[:], ps[4][0:64, :]))
                dve.wait_ge(r_ln, 1)
                chain(nc.vector.tensor_scalar(lrow[:], ps[5][0:64, :], 0.0, None, ALU.min))
                chain(nc.vector.tensor_tensor(lrow[:], lrow[:], Frow[:], ALU.subtract))
                chain(nc.vector.memset(Mrow[:], 0.0))
                one8 = [ones[32 * d:32 * d + 8, 0:1].to_broadcast([8, S]) for d in range(2)]
                chain(nc.vector.tensor_tensor_scan(Frow[0:8, :], one8[0], lrow[0:8, :], 0.0, ALU.mult, ALU.add))
                chain(nc.vector.tensor_tensor_scan(Frow[32:40, ::-1], one8[1], lrow[32:40, ::-1], 0.0, ALU.mult, ALU.add))
                chain(nc.vector.tensor_tensor(irow[:], irow[:], Frow[:], ALU.subtract))
                chain(nc.vector.tensor_tensor_scan(Mrow[0:8, :], irow[0:8, :], irow[0:8, :], 0.0, ALU.max, ALU.max))
                chain(nc.vector.tensor_tensor_scan(Mrow[32:40, ::-1], irow[32:40, ::-1], irow[32:40, ::-1], 0.0, ALU.max, ALU.max))
                nc.vector.tensor_tensor(erow[:], Frow[:], Mrow[:], ALU.add).then_inc(r_rows, 1)
                dve.wait_ge(r_rows, 1)
                nc.vector.tensor_scalar(Mrow[:], Mrow[:], -1.0, None, ALU.mult).then_inc(r_rows, 1)

            def convolution(j):
                for k in range(CONV_K):
                    tap = cols[:, V_CW + 8 * k + j:V_CW + 8 * k + j + 1]
                    src = cz[:, j, k:k + S]
                    if k == 0:
                        chain(nc.vector.tensor_scalar(cy[:, j, :], src, tap, cols[:, V_CB + j:V_CB + j + 1], ALU.mult, ALU.add))
                    else:
                        ins = nc.vector.scalar_tensor_tensor(out=cy[:, j, :], in0=src, scalar=tap, in1=cy[:, j, :],
                                                             op0=ALU.mult, op1=ALU.add)
                        if k < CONV_K - 1:
                            chain(ins)
                        else:
                            ins.then_inc(c_y, 1)

            for u in range(4):
                for half in range(2):
                    take_values(b + 9 + 2 * u + half, u, half)
                    if u:
                        convolution(2 * u - 2 + half)
                if u == 0:
                    gate_rows()
            for u in range(4):
                take_tokens(b + 17 + 2 * u, mo, u * UC)
                if u == 0:
                    convolution(6)
                    convolution(7)
            dve.wait_ge(c_y, KC)

            def decayed(r):
                h, d, j = r // 8, r // 4 % 2, r % 4
                lo, hi = (j * P, S) if d == 0 else (0, (j + 1) * P)
                dve.wait_ge(l_wm, r + 1)
                dve.wait_ge(l_qk, 4 * h + j + 1)
                if h >= 2:
                    dve.wait_ge(l_o, 2 * h - 4 + d + 1)
                nc.vector.scalar_tensor_tensor(out=ma[h % 2][d][:, j, lo:hi], in0=ps[j][:, lo:hi], scalar=FOX_D ** -0.5,
                                               in1=wt[r % WT_RING][:, lo:hi], op0=ALU.mult, op1=ALU.mult).then_inc(l_a, 1)

            def heads_out(h, d):
                dve.wait_ge(l_o, 2 * h + d + 1)
                row = h + 32 * d
                for p in range(2):
                    den = ps[6 + p][:, 0:258].rearrange("p (a c) -> p a c", a=2)[:, :, ML_V]
                    chain(nc.vector.scalar_tensor_tensor(out=mden[:, 2 * p:2 * p + 2], in0=den, scalar=-1.0,
                                                         in1=ecol[:, 2 * p:2 * p + 2, row], op0=ALU.mult, op1=ALU.max))
                    chain(nc.vector.tensor_tensor(mden[:, 2 * p:2 * p + 2], den, mden[:, 2 * p:2 * p + 2], ALU.max))
                chain(nc.vector.reciprocal(mden[:, 4:8], mden[:, 0:4]))
                for i in range(TB):
                    num = ps[6 + i // 2][:, (i % 2) * 129:(i % 2) * 129 + ML_V]
                    dst = hs[:, i, h * P:(h + 1) * P]
                    if d == 0:
                        ins = nc.vector.tensor_scalar(dst, num, mden[:, 4 + i:5 + i], None, ALU.mult)
                    else:
                        ins = nc.vector.scalar_tensor_tensor(out=dst, in0=num, scalar=mden[:, 4 + i:5 + i], in1=dst,
                                                             op0=ALU.mult, op1=ALU.add)
                ins.then_inc(l_h, 1)
                dve.wait_ge(l_h, 2 * h + d + 1)

            def head_sums(h):
                dve.wait_ge(n_sq, h + 1)
                nc.vector.tensor_reduce(hstat[:, h * TB:(h + 1) * TB], hsq[h % 2][:].rearrange("p (t v) -> p t v", v=ML_V), AX,
                                        ALU.add).then_inc(n_sum, 1)

            for h in range(ML_H):
                for x in range(2 * TB):
                    decayed(8 * h + x)
                    if x == 5 and h:
                        heads_out(h - 1, 1)
                heads_out(h, 0)
                if h >= 3:
                    head_sums(h - 3)
            head_sums(ML_H - 3)
            heads_out(ML_H - 1, 1)
            head_sums(ML_H - 2)
            head_sums(ML_H - 1)
            dve.wait_ge(n_sum, ML_H)
            chain(nc.vector.tensor_scalar(hnt[:, 0:32], hstat, 1.0 / ML_V, EPS, ALU.mult, ALU.add))
            dve.wait_ge(n_rs, 1)
            chain(nc.vector.reciprocal(hrs, hrs))
            chain(newton(hrs, hnt[:, 0:32], hnt[:, 32:64]))

            def mixed_low(j):
                low_op(Q0["od_mix"] + j, uL[:, j, :], ps[4 + j % 4][:], uH[:, j, :])

            for h in range(ML_H):
                dve.wait_ge(n_g, h + 1)
                x = hs[:, :, h * P:(h + 1) * P]
                nc.vector.tensor_tensor(x, x, hrs[:, h * TB:(h + 1) * TB].rearrange("p (t o) -> p t o", o=1)
                                        .to_broadcast([P, TB, P]), ALU.mult).then_inc(n_h, 1)
                if h >= 2:
                    mixed_low(h - 2)
            mixed_low(ML_H - 2)
            mixed_low(ML_H - 1)
            n, b = AT["od_out"]
            residual_and_sums(b, "ff2_1", mcol(mod, 1, 2))
            gated_norm("ff2_1", 3, 1)
            gated_ffn(1)
            for o in range(2 * TB):
                tb, half = o // 2, o % 2
                dve.wait_ge(o_tr, o + 1)
                nc.vector.tensor_copy(otok[:, tb, half * 512:(half + 1) * 512], ps[4 + o % 4][:]).then_inc(o_cp, 1)

        @block.tensor
        def _(pe):
            def bank_free(b, taken=None, silus=None):
                if b < 4:
                    return
                if BY_ACT[b - 4]:
                    pe.wait_ge(silu_done, add(silus, SILUS[b - 3]))
                else:
                    pe.wait_ge(blk_taken, add(taken, TAKEN[b - 3]))

            def parts(out_ap, wa, xa, first, last):
                (wh, wl), (xh, xl) = wa, xa
                nc.tensor.matmul(out_ap, wh, xh, start=first, stop=False)
                nc.tensor.matmul(out_ap, wh, xl, start=False, stop=False)
                return nc.tensor.matmul(out_ap, wl, xh, start=False, stop=last)

            def unit_ready(n, units=None):
                pe.wait_ge(w_hi, add(units, n + 1))
                pe.wait_ge(w_lo, add(units, n + 1))

            def feature_unit(n, xh, xl, tokens=S, need=None, i=None, du=0, dt=0, ds=0, beside=None):
                units, taken, silus = (None,) * 3 if i is None else (i * du, i * dt, i * ds)
                unit_ready(n, units)
                kc = UNITS[n][2]
                blocks = range(UNITS[n][5])

                def chunk(c, k):
                    cs = slice(c * P, (c + 1) * P)
                    ins = parts(ps[(BLOCK0[n] + c) % 4][:, 0:tokens], (wH[n % 2][:, k, cs], wL[n % 2][:, k, cs]),
                                (xh[:, k, :], xl[:, k, :]), k == 0, k == kc - 1)
                    if k == kc - 1:
                        ins.then_inc(blk_done, 1)

                if need is None:
                    for c in blocks:
                        bank_free(BLOCK0[n] + c, taken, silus)
                        for k in range(kc):
                            chunk(c, k)
                else:
                    for c in blocks:
                        bank_free(BLOCK0[n] + c, taken, silus)
                    for k in range(kc):
                        if beside is not None:
                            beside(k)
                        pe.wait_ge(op_lo, need(k))
                        for c in blocks:
                            chunk(c, k)

            def token_block(n, b, tbs, xh, xl, c0=0, width=UC):
                bank_free(b)
                for pos, tb in enumerate(tbs):
                    for k in range(KC):
                        ts = slice(tb * P, (tb + 1) * P)
                        ins = parts(ps[b % 4][:, pos * width:(pos + 1) * width], (xh[:, k, ts], xl[:, k, ts]),
                                    (wH[n % 2][:, k, c0:c0 + width], wL[n % 2][:, k, c0:c0 + width]), k == 0, k == KC - 1)
                ins.then_inc(blk_done, 1)

            def token_unit(n, xh, xl, blocks=((0, 1), (2, 3))):
                unit_ready(n)
                for c, tbs in enumerate(blocks):
                    token_block(n, BLOCK0[n] + c, tbs, xh, xl)

            def norm_sum(name, twice=False):
                pe.wait_ge(sq_added, SQ0[name] + (16 if twice else 8))
                for g in range(2 if twice else 1):
                    for tb in range(TB):
                        ins = nc.tensor.matmul(ps[6][:, 4 * g + tb:4 * g + tb + 1], (ssum, gsum)[g][:, tb * P:(tb + 1) * P],
                                               ones[:, 0:1], start=True, stop=True)
                ins.then_inc(sum_done, 1)

            def broadcast(src, bank):
                for tb in range(TB):
                    ins = nc.tensor.matmul(ps[bank][:, tb * P:(tb + 1) * P], src[:, tb:tb + 1].to_broadcast([P, P]), ident,
                                           start=True, stop=True)
                return ins

            def norm_broadcast(name):
                pe.wait_ge(inv_done, NORMS[name] + 1)
                broadcast(rootinv, 4).then_inc(bc_done, 1)

            def norm(name):
                norm_sum(name)
                norm_broadcast(name)

            def chunks_of(q0):
                return lambda k: q0 + k + 1

            def all_chunks_of(q0):
                return lambda k: q0 + KC

            def attention(kind):
                c = ATT[kind]
                ns = c["heads"] * TB
                pe.wait_ge(blk_taken, TAKEN[BLOCK0[AT[{"fox": "out", "cross": "xo", "grid": "ev_out"}[kind]][0]]])

                def gates_everywhere(h):
                    if h >= 2:
                        pe.wait_ge(f_bcs, h - 1)
                    nc.tensor.matmul(ps[2 + h % 2][:], ident[0:FOX_H, h:h + 1].to_broadcast([FOX_H, P]), frow[0][:],
                                     start=True, stop=True).then_inc(f_bc, 1)

                def scores(g, h, i):
                    hp, blk, ts = (h % 2) * 64, h // 2, slice(i * P, (i + 1) * P)
                    dst = ps[4 + g % 2]
                    if g >= 2:
                        pe.wait_ge(mx_done if kind == "fox" else ex_done, g - 1)
                    if kind == "fox":
                        nc.tensor.matmul(dst[:, 0:(i + 1) * P], fq[hp:hp + 64, blk, ts], fk[hp:hp + 64, blk, 0:(i + 1) * P],
                                         start=True, stop=False)
                        ins = nc.tensor.matmul(dst[:, ts], identb[:], causalb[:], start=False, stop=True)
                    elif kind == "cross":
                        nc.tensor.matmul(dst[:, 0:M_MEM], xq[:, 2 * h, ts], xk[:, 2 * h, :], start=True, stop=False)
                        ins = nc.tensor.matmul(dst[:, 0:M_MEM], xq[:, 2 * h + 1, ts], xk[:, 2 * h + 1, :], start=False, stop=True)
                    else:
                        ins = nc.tensor.matmul(dst[:], evq[hp:hp + 64, blk, ts], kdup[hp:hp + 64, h // 4, :], start=True, stop=True)
                    ins.then_inc(sc_done, 1)

                def values(h):
                    hp = (h % 2) * 64
                    pe.wait_ge(pt_done, c["step0"] + TB * h + TB)
                    if kind == "cross":
                        for cc in range(2):
                            if h:
                                pe.wait_ge(op_lo, c["q0"] + 2 * (h - 1) + cc + 1)
                            for m in range(2):
                                ins = nc.tensor.matmul(ps[cc][:], xv[:, m, h * UC + cc * P:h * UC + (cc + 1) * P],
                                                       pT[h % 2][:, m, :], start=(m == 0), stop=(m == 1))
                            ins.then_inc(pv_done, 1)
                        return
                    if h % 2 == 0 and h >= 4:
                        pe.wait_ge(op_lo, c["q0"] + h // 2 - 1)
                    for j in range(TB):
                        t0 = j * P if kind == "fox" else 0
                        v = fv[:, j, h * 64:(h + 1) * 64] if kind == "fox" else evv[:, j, (h // 4) * 64:(h // 4) * 64 + 64]
                        ins = nc.tensor.matmul(ps[h // 2 % 2][hp:hp + 64, t0:S], v, pT[h % 2][:, j, t0:S],
                                               start=(j == 0), stop=(j == TB - 1))
                    ins.then_inc(pv_done, 1)

                if kind == "fox":
                    pe.wait_ge(f_rows, 1)
                    gates_everywhere(0)
                if kind == "grid":
                    pe.wait_ge(g_kd, 2)
                for s in range(ns + 4):
                    if kind == "fox" and s % 4 == 1 and s // 4 + 1 < FOX_H:
                        gates_everywhere(s // 4 + 1)
                    if s < ns:
                        scores(c["step0"] + s, s // TB, s % TB)
                    t = s - 3
                    if 0 <= t < ns:
                        g, i = c["step0"] + t, t % TB
                        nj = {"fox": i + 1, "cross": 2, "grid": TB}[kind]
                        pe.wait_ge(pn_done, g + 1)
                        if g >= 2:
                            pe.wait_ge(pt_done, g - 1)
                        for j in range(nj):
                            ins = nc.tensor.transpose(ps[6 + g % 2][:, j * P:(j + 1) * P], pr[g % PR_RING][:, j * P:(j + 1) * P], ident)
                        ins.then_inc(tp_done, 1)
                    if s >= 4 and (s - 4) % TB == TB - 1:
                        values((s - 4) // TB)

            pe.wait_ge(cst_in, 16)
            for tb in range(TB):
                pe.wait_ge(x_in[tb], 16)
            for j in range(KC):
                if j >= 2:
                    pe.wait_ge(x_cols, j - 1)
                for tb in range(TB):
                    ins = nc.tensor.transpose(ps[6 + j % 2][:, tb * P:(tb + 1) * P], xtok[:, tb, j * P:(j + 1) * P], ident)
                ins.then_inc(x_tr, 1)
            pe.wait_ge(vec_in, 16 * 19)
            nc.tensor.transpose(ps[5][:, 0:V_ROWS], vrow[0:V_ROWS, :], ident[0:V_ROWS, 0:V_ROWS]).then_inc(vec_tr, 1)
            nc.tensor.transpose(ps[5][:, 128:224], brow[0:96, :], ident[0:96, 0:96]).then_inc(vec_tr, 1)
            pe.sem_inc(ada_mm, 2)
            norm_broadcast("mix")

            n = AT["in"][0]
            for u in range(4):
                feature_unit(n + u, hnH, hnL, need=chunks_of(Q0["mix_norm"]) if u == 0 else None)
            for u in range(4, 6):
                token_unit(n + u, hnH, hnL)
            for u in range(6, 11):
                feature_unit(n + u, hnH, hnL)
            for u in range(11, 13):
                token_unit(n + u, hnH, hnL)
            for u in range(13, 15):
                feature_unit(n + u, hnH, hnL)
            attention("fox")
            def head_out(h):
                pe.wait_ge(h_at, 8 * h + 8)
                pe.wait_ge(h_qb, h + 1)
                pe.wait_ge(h_st, 3 * h + 3)
                if h >= 2:
                    pe.wait_ge(h_os, h - 1)
                for c in range(TB):
                    cs = slice(c * P, (c + 1) * P)
                    hv = slice(h * P, (h + 1) * P)
                    ins = nc.tensor.matmul(ps[h % 2][:, cs], gi[:, c, hv], at_[h % 2][:, c, :], start=True, stop=(c == 0))
                    if c:
                        ins = nc.tensor.matmul(ps[h % 2][:, cs], st[:, c - 1, :], qb[:, cs], start=False, stop=True)
                ins.then_inc(h_o, 1)

            v = 0
            for h in range(HG_H):
                for l in range(8):
                    e = 8 * h + l
                    if l < 7:
                        pe.wait_ge(h_q, queries(v))
                        pe.wait_ge(h_k, v + 1)
                    if e >= 4:
                        pe.wait_ge(h_at, e - 3)
                    for c in range(TB):
                        cs = slice(c * P, (c + 1) * P)
                        k_, q_ = (kt[v % HG_RING][:, cs], qt[v % HG_RING][:, cs]) if l < 7 else (gk[:, h, cs], gq[:, h, cs])
                        ins = nc.tensor.matmul(ps[2 + e % 4][:, cs], k_, q_, start=True, stop=True)
                    ins.then_inc(h_pl, 1)
                    v += l < 7
                    if l == 1 and h:
                        head_out(h - 1)
                    if l == 4:
                        pe.wait_ge(h_kd, h + 1)
                        if h:
                            pe.wait_ge(h_kts, h)
                        for c in range(3):
                            ins = nc.tensor.transpose(ps[6][:, c * P:(c + 1) * P], kd[:, c * P:(c + 1) * P], ident)
                        ins.then_inc(h_kt, 1)
                    if l == 6:
                        pe.wait_ge(h_kts, h + 1)
                        if h:
                            pe.wait_ge(h_st, 3 * h)
                        hv = slice(h * P, (h + 1) * P)
                        for c in range(3):
                            ins = nc.tensor.matmul(ps[7][:, c * P:(c + 1) * P], kdT[:, c, :], gi[:, c, hv], start=True, stop=True)
                        ins.then_inc(h_sp, 1)
            head_out(HG_H - 1)
            hr = [dd[0], dd[1], kt[0], kt[1]]
            for h in range(HG_H):
                pe.wait_ge(h_sq, h + 1)
                for tb in range(TB):
                    ins = nc.tensor.matmul(ps[4][:, 4 * h + tb:4 * h + tb + 1], hr[h][:, tb * P:(tb + 1) * P], ones[:, 0:1],
                                           start=True, stop=True)
                ins.then_inc(h_sum, 1)
            pe.wait_ge(h_inv, 1)
            for h in range(HG_H):
                broadcast(hrs[:, 4 * h:4 * h + 4], (5, 6, 7, 2)[h]).then_inc(h_bc, 1)
            n = AT["out"][0]
            feature_unit(n, uH, uL, need=all_chunks_of(Q0["mix"]))
            for u in range(1, 4):
                feature_unit(n + u, uH, uL)
                if u == 3:
                    break
                pe.wait_ge(m_n, 2)
                for j in range(4 * u - 4, 4 * u):
                    if j >= 4:
                        pe.wait_ge(op_lo, Q0["mem"] + j - 3)
                    for mb in range(2):
                        ins = nc.tensor.transpose(ps[4 + j % 4][:, mb * P:(mb + 1) * P], mtok[:, mb, j * P:(j + 1) * P], ident)
                    ins.then_inc(m_tr, 1)
            n = AT["xkv"][0]
            for u in range(8):
                if u < 4:
                    feature_unit(n + u, memH, memL, M_MEM, need=chunks_of(Q0["mem"]) if u == 0 else None)
                else:
                    token_unit(n + u, memH, memL, ((0,), (1,)))
                if u == 1:
                    norm_sum("x")
                if u == 2:
                    norm_broadcast("x")
            for u, n in enumerate(range(*ranges("xq"))):
                feature_unit(n, hnH, hnL, need=chunks_of(Q0["x_norm"]) if u == 0 else None)
            attention("cross")
            for u, n in enumerate(range(*ranges("xo"))):
                feature_unit(n, uH, uL, need=all_chunks_of(Q0["x_att"]) if u == 0 else None)
            norm("ff1")
            n0, b0 = AT["ff1"]

            def conditioning_sums(layer, i, m):
                group = ADA_GROUP[layer]
                pe.wait_ge(ada_acc, i * group + (24 * layer + m + 1 + ADA_RING))
                if m == 0:
                    pe.wait_ge(mod_done, i + (1, 5)[layer])
                nc.tensor.matmul(ps[5][:, 2 * m:2 * m + 1], adacc[m % 2][:, 0:P], ones[:, 0:1], start=True, stop=True)
                nc.tensor.matmul(ps[5][:, 2 * m + 1:2 * m + 2], adacc[m % 2][:, P:UC], ones[:, 0:1],
                                 start=True, stop=True).then_inc(ada_mm, 1)

            def squared_relu(i, last=False):
                for u in range(8):
                    if u < 4:
                        feature_unit(n0 + u, hnH, hnL, need=chunks_of(Q0["ff1_norm"]) if u == 0 else None, i=i, du=8, dt=16)
                    else:
                        feature_unit(n0 + u, uH, uL, need=(lambda k: i * 8 + (Q0["ff1_u"] + k + 1)) if u == 4 else None,
                                     i=i, du=8, dt=16)
                    if not last:
                        conditioning_sums(0, i, u)

            with pe.Fori(0, 3) as i:
                squared_relu(i)
            squared_relu(3, True)
            norm_sum("ev", True)
            pe.wait_ge(e_inv, 1)
            broadcast(rootinv, 4)
            broadcast(msq, 5).then_inc(bc_done, 1)
            n = AT["ev_in"][0]

            def head_norm_sum(j):
                pe.wait_ge(g_sq, j + 1)
                nc.tensor.matmul(ps[4 + j % 4][:], cst[:, C_HALF, :], gs[:, j, :], start=True, stop=True).then_inc(g_sum, 1)

            def rotation(i):
                pe.wait_ge(g_n, ROPE_ORDER[i] + 1)
                if i >= 3:
                    pe.wait_ge(g_roped, i - 2)
                nc.tensor.matmul(ps[ROPE_BANK[i]][:], cst[:, C_ROT, :], evq[:, ROPE_ORDER[i], :], start=True,
                                 stop=True).then_inc(g_rot, 1)

            for u in range(2):
                feature_unit(n + u, hnH, hnL, need=chunks_of(Q0["ev_norm"]) if u == 0 else None)
            m = n + 2
            unit_ready(m)
            b = BLOCK0[m]
            bank_free(b)
            for k in range(KC):
                ins = parts(ps[b % 4][:], (wH[m % 2][:, k, 0:P], wL[m % 2][:, k, 0:P]), (hnH[:, k, :], hnL[:, k, :]),
                            k == 0, k == KC - 1)
            ins.then_inc(blk_done, 1)
            token_block(m, b + 1, range(TB), hnH, hnL, P, P)
            for j in range(4):
                head_norm_sum(j)
            feature_unit(n + 3, hnH, hnL)
            pe.wait_ge(g_rs, 4)
            head_norm_sum(4)
            for i in range(3):
                rotation(i)
            feature_unit(n + 4, hnH, hnL)
            rotation(3)
            rotation(4)
            pe.wait_ge(g_roped, 4)
            pe.wait_ge(g_rs, 5)
            for j in range(2):
                nc.tensor.matmul(ps[(7, 4)[j]][:], cst[:, C_DUP0 + j, :], evq[:, 4, :], start=True, stop=True).then_inc(g_dup, 1)
            pe.wait_ge(g_roped, 5)
            pe.wait_ge(blk_taken, TAKEN[BLOCK0[AT["ev_out"][0]]])
            attention("grid")
            for j in range(4):
                pe.wait_ge(p_done, j + 1)
                if j >= 2:
                    pe.wait_ge(op_lo, Q0["ev_mix"] + 4 + j - 1)
                nc.tensor.matmul(ps[2 + j % 2][:], wpool[:, j, :], pd[:, j, :], start=True, stop=True).then_inc(p_mm, 1)
            for u, n in enumerate(range(*ranges("ev_out"))):
                feature_unit(n, uH, uL, need=all_chunks_of(Q0["ev_mix"]) if u == 0 else None)

            def gated_ffn(layer):
                name = f"ff2_{layer}"
                n0, b0 = AT[name]
                q0 = Q0[name + "_u"]
                with pe.Fori(0, 2) as i:
                    for u in range(12):
                        if u < 8:
                            feature_unit(n0 + u, hnH, hnL, need=chunks_of(Q0[name + "_norm"]) if u == 0 else None,
                                         i=i, du=12, dt=16, ds=8)
                        else:
                            feature_unit(n0 + u, uH, uL, need=(lambda k: i * 8 + (q0 + k + 1)) if u == 8 else None,
                                         i=i, du=12, dt=16, ds=8)
                        if layer == 0:
                            conditioning_sums(1, i, u)
                for u in range(24, 30):
                    feature_unit(n0 + u, hnH, hnL)
                for u in range(30, 34):
                    feature_unit(n0 + u, uH, uL, need=chunks_of(q0 + 16) if u == 30 else None)

            norm("ff2_0")
            gated_ffn(0)
            norm("od")
            n = AT["od_in"][0]
            for u in range(4):
                feature_unit(n + u, hnH, hnL, need=chunks_of(Q0["od_norm"]) if u == 0 else None)
            feature_unit(n + 4, hnH, hnL)
            for u in range(5, 13):
                token_unit(n + u, hnH, hnL)
                if u == 5:
                    pe.wait_ge(blk_taken, TAKEN[BLOCK0[n + 4] + 1])
                    for half in range(2):
                        ins = nc.tensor.matmul(ps[4 + half][0:64, :], cst[96:128, C_GSEL, half * 64:(half + 1) * 64],
                                               grow[96:128, :], start=True, stop=True)
                    ins.then_inc(r_sel, 1)
                if u == 8:
                    pe.wait_ge(r_rows, 1)
                    for tb in range(TB):
                        ins = nc.tensor.transpose(ps[6][:, tb * 64:(tb + 1) * 64], irow[:, tb * P:(tb + 1) * P], ident[0:64, 0:64])
                    ins.then_inc(r_tr, 1)
                    pe.wait_ge(r_em, 1)
                    for tb in range(TB):
                        ins = nc.tensor.transpose(ps[7][:, tb * 64:(tb + 1) * 64], erow[:, tb * P:(tb + 1) * P], ident[0:64, 0:64])
                    ins.then_inc(r_tr, 1)
            pe.wait_ge(blk_taken, TAKEN[BLOCK0[AT["od_out"][0]]])
            pe.wait_ge(r_rows, 2)
            pe.wait_ge(r_cols, 2)

            def out_rows(h, d):
                pe.wait_ge(l_a, 8 * h + 4 * d + 4)
                if 2 * h + d:
                    pe.wait_ge(l_h, 2 * h + d)
                for i in range(TB):
                    dst = ps[6 + i // 2][:, (i % 2) * 129:(i % 2) * 129 + 129]
                    js = range(0, i + 1) if d == 0 else range(i, TB)
                    for j in js:
                        ins = nc.tensor.matmul(dst, ma[h % 2][d][:, j, i * P:(i + 1) * P], vx[:, j, h, :],
                                               start=(j == js[0]), stop=(j == js[-1]))
                ins.then_inc(l_o, 1)

            pe.wait_ge(c_silu, KC)

            def scores_half(h, d):
                if h >= ML_H:
                    return
                if h:
                    pe.wait_ge(l_w, 8 * (h - 1) + 4 * d + 4)
                row = h + 32 * d
                nc.tensor.matmul(ps[4 + d][:], ident[0:64, row:row + 1].to_broadcast([64, P]), Mrow[:],
                                 start=True, stop=True).then_inc(l_bc, 1)
                hp = (h % 2) * 64
                for j in range(2 * d, 2 * d + 2):
                    if h:
                        pe.wait_ge(l_a, 8 * (h - 1) + 4 + j + 1)
                    nc.tensor.matmul(ps[j][:], cy[hp:hp + 64, 4 + h // 2, j * P:(j + 1) * P], cy[hp:hp + 64, h // 2, :],
                                     start=True, stop=True).then_inc(l_qk, 1)

            scores_half(0, 0)
            scores_half(0, 1)
            for h in range(ML_H):
                scores_half(h + 1, 0)
                out_rows(h, 0)
                scores_half(h + 1, 1)
                out_rows(h, 1)

            def head_transposes(j):
                if j >= KC:
                    return
                pe.wait_ge(n_h, j + 1)
                if j >= 4:
                    pe.wait_ge(op_lo, Q0["od_mix"] + j - 3)
                for tb in range(TB):
                    ins = nc.tensor.transpose(ps[4 + j % 4][:, tb * P:(tb + 1) * P], hs[:, tb, j * P:(j + 1) * P], ident)
                ins.then_inc(n_tr, 1)

            for j in range(3):
                head_transposes(j)
            for u, n in enumerate(range(*ranges("od_out"))):
                feature_unit(n, uH, uL, need=chunks_of(Q0["od_mix"]) if u == 0 else None,
                             beside=(lambda k: head_transposes(k + 3)) if u == 0 else None)
            norm("ff2_1")
            gated_ffn(1)
            pe.wait_ge(blk_taken, TAKEN[-1])
            for o in range(2 * TB):
                tb, half = o // 2, o % 2
                if o >= 4:
                    pe.wait_ge(o_cp, o - 3)
                for j in range(4):
                    ins = nc.tensor.transpose(ps[4 + o % 4][:, j * P:(j + 1) * P], xT[:, 4 * half + j, tb * P:(tb + 1) * P], ident)
                ins.then_inc(o_tr, 1)


def constants():
    c = np.zeros((N_CONST, P, P), np.float32)
    c[C_IDENT] = np.eye(P)
    c[C_ONES] = 1.0
    half = np.arange(P) // 64
    c[C_HALF] = half[:, None] == half[None, :]
    for i in range(0, P, 2):
        c[C_ROT, i + 1, i] = -1.0
        c[C_ROT, i, i + 1] = 1.0
    for kv in range(2):
        for m in range(P):
            c[C_DUP0 + kv, kv * 64 + m % 64, m] = 1.0
    for d in range(2):
        for h in range(ML_H):
            c[C_GSEL, 96 + 16 * d + h, 32 * d + h] = 1.0
            c[C_GSEL, 96 + 16 * d + 8 + h, 64 + 32 * d + h] = 1.0
    t, s = np.arange(P)[:, None], np.arange(P)[None, :]
    c[C_CAUSAL] = np.where(t >= s, 0.0, NEG)
    levels = np.zeros((8, P, P), np.float32)
    s, t = np.arange(P)[:, None], np.arange(P)[None, :]
    for l, L in enumerate(HG_LEVELS):
        levels[l] = (s // (2 * L) == t // (2 * L)) & (s % (2 * L) < L) & (t % (2 * L) >= L)
    levels[7] = s == t
    row, colm = np.repeat(np.arange(S // 64), 64).astype(np.float32), np.tile(np.arange(64), S // 64).astype(np.float32)
    inv = (np.float32(10000.0) ** (-np.arange(16, dtype=np.float32) / np.float32(16))).astype(np.float32)
    ang = np.concatenate([row[:, None] * inv, colm[:, None] * inv], axis=-1)
    lane = (np.arange(P) % 64) // 2
    rope = np.stack([np.cos(ang)[:, lane].T, np.sin(ang)[:, lane].T]).astype(np.float32)
    t = np.arange(S)
    icount = np.stack([1.0 / (np.clip(t + w - w // 2, 0, S) - np.clip(t - w // 2, 0, S)) for w in WINDOWS]).astype(np.float32)
    return {"const": c, "levels": levels, "rope": np.ascontiguousarray(rope), "icount": icount}


_INS = ["x", "mem", "norm_mix_g", "w_in", "fox_f_bias", "hgrn_lb_logits", "hgrn_norm_g", "w_out", "norm_x_g", "norm_mem_g",
        "w_xq", "w_xkv", "w_xo", "norm_ff_g", "w1", "w2", "final_norm_g", "c_2", "ada_w_2", "ada_b_2", "ev_w_in_2",
        "ev_w_pool_2", "ev_b_pool_2", "ev_pool_scale_2", "ev_q_gain_2", "ev_k_gain_2", "ev_w_out_2", "od_w_in_2",
        "od_conv_w_2", "od_conv_b_2", "od_gate_b_2", "od_head_gain_2", "od_w_out_2", "ffn_w1_2", "ffn_w3_2", "ffn_w2_2"]


def kernel(**inputs):
    import numpy as _np
    import concourse.bacc as _bacc
    from concourse import mybir as _mybir
    from concourse.bass_utils import run_bass_kernel_spmd as _run

    nc = _bacc.Bacc("TRN2", target_bir_lowering=False, num_devices=1)
    arrays, aps = {}, {}
    given = {name: _np.ascontiguousarray(inputs[name]) for name in _INS}
    given.update(constants())
    for name, value in given.items():
        arrays[f"in_{name}_dram"] = value
        aps[name] = nc.dram_tensor(f"in_{name}_dram", value.shape, _mybir.dt.from_np(value.dtype), kind="ExternalInput").ap()
    out = nc.dram_tensor("out_0_dram", (1, S, D), _mybir.dt.float32, kind="ExternalOutput").ap()
    bass_block_pair(nc, aps, out)
    r = _run(nc, [arrays], core_ids=[0])
    return r.results[0]["out_0_dram"]
```
